# Optimizing a Trainium2 kernel written in Bass

```python
import math
import jax
import jax.numpy as jnp
from jax import lax
import numpy as np
import jax, jax.numpy as jnp

D_MODEL = 1024
BATCH = 1
SEQ = 512
DEPTH = 2

HEAD_DIM_ATTN = 64
N_HEADS_SB = 8
N_HEADS_DIL = 8
WIDTH_SB = N_HEADS_SB * HEAD_DIM_ATTN
WIDTH_DIL = N_HEADS_DIL * HEAD_DIM_ATTN
ATTN_WIDTH = WIDTH_SB + WIDTH_DIL
DIL_CONFIGS = ((128, 1), (512, 4), (2048, 16))
Q_BLOCK = 128
NUM_BUCKETS = 32
MAX_DISTANCE = 2048
N_HEADS_MLSTM = 8
HEAD_DIM_MLSTM = D_MODEL // N_HEADS_MLSTM
MLSTM_WIDTH = N_HEADS_MLSTM * HEAD_DIM_MLSTM
MLSTM_CHUNK = 128
CONV_WIDTH = 4
FORGET_BIAS_LO = 3.0
FORGET_BIAS_HI = 6.0
D_FF = 2816
N_EVEN = (DEPTH + 1) // 2
N_ODD = DEPTH // 2
EPS = 1e-6


def _rms_norm(x, g):
    xf = x.astype(jnp.float32)
    y = xf * lax.rsqrt(jnp.mean(xf * xf, axis=-1, keepdims=True) + EPS)
    return (y * g.astype(jnp.float32)).astype(x.dtype)

def _swiglu(x, w_gate, w_up, w_down):
    return (jax.nn.silu(x @ w_gate) * (x @ w_up)) @ w_down

def _t5_bucket(dist):
    max_exact = NUM_BUCKETS // 2
    d = jnp.maximum(dist, 1).astype(jnp.float32)
    log_b = max_exact + (jnp.log(d / max_exact) / math.log(MAX_DISTANCE / max_exact)
                         * (NUM_BUCKETS - max_exact)).astype(jnp.int32)
    log_b = jnp.minimum(log_b, NUM_BUCKETS - 1)
    return jnp.where(dist < max_exact, dist, log_b)

def _stick_breaking_attention(q, k, v):
    bsz, t, h, dh = q.shape
    nb = t // Q_BLOCK
    qb = q.reshape(bsz, nb, Q_BLOCK, h, dh).transpose(1, 0, 2, 3, 4)
    starts = jnp.arange(nb) * Q_BLOCK
    k_pos = jnp.arange(t)
    scale = 1.0 / math.sqrt(dh)

    def block(args):
        q_blk, start = args
        z = jnp.einsum('bqhd,bkhd->bhqk', q_blk, k) * scale
        causal = k_pos[None, :] < (start + jnp.arange(Q_BLOCK))[:, None]
        log_keep = jnp.where(causal, jax.nn.log_sigmoid(-z), 0.0)
        later = lax.cumsum(log_keep, axis=3, reverse=True) - log_keep
        log_w = jnp.where(causal, jax.nn.log_sigmoid(z) + later, -jnp.inf)
        return jnp.einsum('bhqk,bkhd->bqhd', jnp.exp(log_w), v)

    out = lax.map(block, (qb, starts))
    return out.transpose(1, 0, 2, 3, 4).reshape(bsz, t, h, dh)

def _dilated_branch(q, k, v, rel_bias, window, dil):
    bsz, t, h, dh = q.shape
    steps = window // dil
    seq_l = t // dil
    nb = -(-seq_l // Q_BLOCK)
    lp = nb * Q_BLOCK
    n = bsz * dil

    def to_res(a):
        return a.reshape(bsz, seq_l, dil, h, dh).transpose(0, 2, 1, 3, 4).reshape(n, seq_l, h, dh)

    qb = jnp.pad(to_res(q), ((0, 0), (0, lp - seq_l), (0, 0), (0, 0))).reshape(n, nb, Q_BLOCK, h, dh)

    def band(a):
        a = jnp.pad(to_res(a), ((0, 0), (Q_BLOCK, lp - seq_l), (0, 0), (0, 0)))
        a = a.reshape(n, nb + 1, Q_BLOCK, h, dh)
        return jnp.concatenate([a[:, :-1], a[:, 1:]], axis=2)

    kb, vb = band(k), band(v)
    qi = jnp.arange(Q_BLOCK)[:, None]
    ki = jnp.arange(2 * Q_BLOCK)[None, :]
    dist = qi + Q_BLOCK - ki
    bias = rel_bias[_t5_bucket(jnp.maximum(dist, 0) * dil)].transpose(2, 0, 1)
    key_pos = jnp.arange(nb)[:, None, None] * Q_BLOCK + ki[None] - Q_BLOCK
    valid = (dist >= 0) & (dist <= steps) & (key_pos >= 0)
    s = jnp.einsum('nbqhd,nbkhd->nbhqk', qb, kb) / math.sqrt(dh) + bias
    s = jnp.where(valid[None, :, None], s, -jnp.inf)
    m = jnp.max(s, axis=-1)
    p = jnp.exp(s - m[..., None])
    l = jnp.sum(p, axis=-1)
    num = jnp.einsum('nbhqk,nbkhd->nbqhd', p, vb)

    def back(a):
        a = a[:, :seq_l]
        rest = a.shape[2:]
        a = a.reshape((bsz, dil, seq_l) + rest)
        a = a.transpose((0, 2, 1) + tuple(range(3, a.ndim)))
        return a.reshape((bsz, t) + rest)

    num = back(num.reshape(n, lp, h, dh))
    m = back(m.transpose(0, 1, 3, 2).reshape(n, lp, h))
    l = back(l.transpose(0, 1, 3, 2).reshape(n, lp, h))
    return num, m, l

def _dilated_attention(q, k, v, rel_bias):
    outs = [_dilated_branch(q, k, v, rel_bias, w, d) for (w, d) in DIL_CONFIGS]
    m_all = jnp.stack([o[1] for o in outs])
    wts = jnp.exp(m_all - jnp.max(m_all, axis=0))
    num = sum(wts[i][..., None] * outs[i][0] for i in range(len(outs)))
    den = sum(wts[i] * outs[i][2] for i in range(len(outs)))
    return num / den[..., None]

def _attn_mixer(xn, w_in, w_out, rel_bias):
    bsz, t, _ = xn.shape
    proj = (xn @ w_in).astype(jnp.float32)
    idx = [WIDTH_SB, 2 * WIDTH_SB, 3 * WIDTH_SB, 3 * WIDTH_SB + WIDTH_DIL, 3 * WIDTH_SB + 2 * WIDTH_DIL]
    qa, ka, va, qd, kd, vd = jnp.split(proj, idx, axis=-1)
    sb = lambda a: a.reshape(bsz, t, N_HEADS_SB, HEAD_DIM_ATTN)
    dl = lambda a: a.reshape(bsz, t, N_HEADS_DIL, HEAD_DIM_ATTN)
    out_sb = _stick_breaking_attention(sb(qa), sb(ka), sb(va))
    out_dil = _dilated_attention(dl(qd), dl(kd), dl(vd), rel_bias.astype(jnp.float32))
    mixed = jnp.concatenate([out_sb.reshape(bsz, t, WIDTH_SB), out_dil.reshape(bsz, t, WIDTH_DIL)], axis=-1)
    return mixed.astype(xn.dtype) @ w_out

def _causal_depthwise_conv(x, w):
    return lax.conv_general_dilated(
        x, w[:, None, :], window_strides=(1,), padding=((CONV_WIDTH - 1, 0),),
        dimension_numbers=('NWC', 'WIO', 'NWC'), feature_group_count=x.shape[-1])

def _mlstm(q, k, v, i_pre, f_pre):
    bsz, t, h, dh = q.shape
    nc = t // MLSTM_CHUNK
    cl = MLSTM_CHUNK

    def chunks(a):
        a = a.reshape((bsz, nc, cl, h) + a.shape[3:])
        return a.transpose((0, 3, 1, 2) + tuple(range(4, a.ndim)))

    qc = chunks(q) / math.sqrt(dh)
    kc, vc = chunks(k), chunks(v)
    ic = chunks(i_pre)
    bc = jnp.cumsum(jax.nn.log_sigmoid(chunks(f_pre)), axis=-1)

    def step(carry, xs):
        c_st, n_st, m_st = carry
        k_, v_, i_, b_ = xs
        g = b_[..., -1]
        w = g[..., None] - b_ + i_
        m_new = jnp.maximum(g + m_st, jnp.max(w, axis=-1))
        decay = jnp.exp(g + m_st - m_new)
        ws = jnp.exp(w - m_new[..., None])
        c_new = decay[..., None, None] * c_st + jnp.einsum('bhs,bhsk,bhsv->bhkv', ws, k_, v_)
        n_new = decay[..., None] * n_st + jnp.einsum('bhs,bhsk->bhk', ws, k_)
        return (c_new, n_new, m_new), (c_st, n_st, m_st)

    init = (jnp.zeros((bsz, h, dh, dh), jnp.float32),
            jnp.zeros((bsz, h, dh), jnp.float32),
            jnp.zeros((bsz, h), jnp.float32))
    xs = tuple(jnp.moveaxis(a, 2, 0) for a in (kc, vc, ic, bc))
    _, (c_prev, n_prev, m_prev) = lax.scan(step, init, xs)
    c_prev = jnp.moveaxis(c_prev, 0, 2)
    n_prev = jnp.moveaxis(n_prev, 0, 2)
    m_prev = jnp.moveaxis(m_prev, 0, 2)

    a = bc + m_prev[..., None]
    tri = jnp.arange(cl)[:, None] >= jnp.arange(cl)[None, :]
    dmat = jnp.where(tri, bc[..., :, None] - bc[..., None, :] + ic[..., None, :], -jnp.inf)
    m_t = jnp.maximum(a, jnp.max(dmat, axis=-1))
    p = jnp.einsum('bhcld,bhcsd->bhcls', qc, kc) * jnp.exp(dmat - m_t[..., None])
    w_inter = jnp.exp(a - m_t)
    h_num = (jnp.einsum('bhcls,bhcsd->bhcld', p, vc)
             + w_inter[..., None] * jnp.einsum('bhcld,bhcde->bhcle', qc, c_prev))
    n_num = jnp.sum(p, axis=-1) + w_inter * jnp.einsum('bhcld,bhcd->bhcl', qc, n_prev)
    hid = h_num / jnp.maximum(jnp.abs(n_num), jnp.exp(-m_t))[..., None]
    return hid.transpose(0, 2, 3, 1, 4).reshape(bsz, t, h, dh)

def _mlstm_mixer(xn, w_in, b_gates, conv_w, head_g, w_out):
    bsz, t, _ = xn.shape
    proj = (xn @ w_in).astype(jnp.float32)
    qk, v, o, gates = jnp.split(proj, [2 * MLSTM_WIDTH, 3 * MLSTM_WIDTH, 4 * MLSTM_WIDTH], axis=-1)
    qk = jax.nn.silu(_causal_depthwise_conv(qk, conv_w.astype(jnp.float32)))
    q, k = jnp.split(qk, 2, axis=-1)
    gates = gates + b_gates.astype(jnp.float32)
    i_pre, f_pre = gates[..., :N_HEADS_MLSTM], gates[..., N_HEADS_MLSTM:]
    hd = lambda a: a.reshape(bsz, t, N_HEADS_MLSTM, HEAD_DIM_MLSTM)
    hid = _mlstm(hd(q), hd(k), hd(v), i_pre, f_pre)
    hid = hid * lax.rsqrt(jnp.mean(hid * hid, axis=-1, keepdims=True) + EPS)
    hid = hid * head_g.astype(jnp.float32).reshape(N_HEADS_MLSTM, HEAD_DIM_MLSTM)
    hid = hid.reshape(bsz, t, MLSTM_WIDTH) * jax.nn.sigmoid(o)
    return hid.astype(xn.dtype) @ w_out

def first_inputs(seed: int = 0) -> dict:
    key = jax.random.key(seed)
    ks = jax.random.split(key, 16)
    nrm = jax.random.normal
    x = nrm(ks[0], (BATCH, SEQ, D_MODEL), jnp.float32)
    norm_g = 1.0 + 0.02 * nrm(ks[1], (DEPTH, 6, D_MODEL), jnp.float32)
    ffn_w_gate = nrm(ks[2], (DEPTH, 2, D_MODEL, D_FF), jnp.float32) * D_MODEL ** -0.5
    ffn_w_up = nrm(ks[3], (DEPTH, 2, D_MODEL, D_FF), jnp.float32) * D_MODEL ** -0.5
    ffn_w_down = nrm(ks[4], (DEPTH, 2, D_FF, D_MODEL), jnp.float32) * D_FF ** -0.5
    attn_w_in = nrm(ks[5], (N_EVEN, D_MODEL, 3 * ATTN_WIDTH), jnp.float32) * D_MODEL ** -0.5
    attn_w_out = nrm(ks[6], (N_EVEN, ATTN_WIDTH, D_MODEL), jnp.float32) * ATTN_WIDTH ** -0.5
    rel_bias = 0.5 * nrm(ks[7], (NUM_BUCKETS, N_HEADS_DIL), jnp.float32)
    mlstm_w_in = nrm(ks[8], (N_ODD, D_MODEL, 4 * MLSTM_WIDTH + 2 * N_HEADS_MLSTM), jnp.float32) * D_MODEL ** -0.5
    b_i = 0.1 * nrm(ks[9], (N_ODD, N_HEADS_MLSTM), jnp.float32)
    b_f = (jnp.linspace(FORGET_BIAS_LO, FORGET_BIAS_HI, N_HEADS_MLSTM, dtype=jnp.float32)[None]
           + 0.1 * nrm(ks[10], (N_ODD, N_HEADS_MLSTM), jnp.float32))
    mlstm_b_gates = jnp.concatenate([b_i, b_f], axis=-1)
    mlstm_conv_w = nrm(ks[11], (N_ODD, CONV_WIDTH, 2 * MLSTM_WIDTH), jnp.float32) * CONV_WIDTH ** -0.5
    mlstm_head_g = 1.0 + 0.02 * nrm(ks[12], (N_ODD, MLSTM_WIDTH), jnp.float32)
    mlstm_w_out = nrm(ks[13], (N_ODD, MLSTM_WIDTH, D_MODEL), jnp.float32) * MLSTM_WIDTH ** -0.5
    return {'x': x, 'norm_g': norm_g, 'ffn_w_gate': ffn_w_gate, 'ffn_w_up': ffn_w_up,
            'ffn_w_down': ffn_w_down, 'attn_w_in': attn_w_in, 'attn_w_out': attn_w_out,
            'rel_bias': rel_bias, 'mlstm_w_in': mlstm_w_in, 'mlstm_b_gates': mlstm_b_gates,
            'mlstm_conv_w': mlstm_conv_w, 'mlstm_head_g': mlstm_head_g, 'mlstm_w_out': mlstm_w_out}

def first_block(x, norm_g, ffn_w_gate, ffn_w_up, ffn_w_down, attn_w_in, attn_w_out, rel_bias,
              mlstm_w_in, mlstm_b_gates, mlstm_conv_w, mlstm_head_g, mlstm_w_out):
    for layer in range(DEPTH):
        g = norm_g[layer]
        j = layer // 2
        hf = _swiglu(_rms_norm(x, g[0]), ffn_w_gate[layer, 0], ffn_w_up[layer, 0], ffn_w_down[layer, 0])
        x = x + 0.5 * _rms_norm(hf, g[1])
        xn = _rms_norm(x, g[2])
        if layer % 2 == 0:
            mix = _attn_mixer(xn, attn_w_in[j], attn_w_out[j], rel_bias)
        else:
            mix = _mlstm_mixer(xn, mlstm_w_in[j], mlstm_b_gates[j], mlstm_conv_w[j],
                               mlstm_head_g[j], mlstm_w_out[j])
        x = x + _rms_norm(mix, g[3])
        hf = _swiglu(_rms_norm(x, g[4]), ffn_w_gate[layer, 1], ffn_w_up[layer, 1], ffn_w_down[layer, 1])
        x = x + 0.5 * _rms_norm(hf, g[5])
    return x


RMS_EPS = 1e-6
LN_EPS = 1e-5
MIX_WIDTH = D_MODEL
POOL_WIDTH = MIX_WIDTH // 2
POOL_WINDOWS = (2, 4, 8, 16)
POOL_GROUPS = len(POOL_WINDOWS)
POOL_GROUP_DIM = POOL_WIDTH // POOL_GROUPS
SSM_WIDTH = MIX_WIDTH - POOL_WIDTH
SSM_GROUP_DIM = 16
SSM_GROUPS = SSM_WIDTH // SSM_GROUP_DIM
SSM_STATE = 64
DT_MIN = 0.001
DT_MAX = 0.1
CONV_CHANNELS = D_MODEL
CONV_KERNEL = 31
N_EVEN_2 = (DEPTH + 1) // 2
N_ODD_2 = DEPTH // 2


def _rmsnorm(x, g):
    x32 = x.astype(jnp.float32)
    y = x32 * lax.rsqrt(jnp.mean(x32 * x32, axis=-1, keepdims=True) + RMS_EPS)
    return (y * g.astype(jnp.float32)).astype(x.dtype)

def _multiscale_pool(u, pool_w, pool_scale):
    b, s, _ = u.shape
    u32 = u.astype(jnp.float32).reshape(b, s, POOL_GROUPS, POOL_GROUP_DIM)
    csum = jnp.cumsum(u32, axis=1)
    pos = jnp.arange(1, s + 1, dtype=jnp.float32)[None, :, None]
    outs = []
    for g, w in enumerate(POOL_WINDOWS):
        c = csum[:, :, g, :]
        lag = jnp.pad(c, ((0, 0), (w, 0), (0, 0)))[:, :s, :]
        outs.append((c - lag) / jnp.minimum(pos, float(w)) - u32[:, :, g, :])
    pooled = jnp.stack(outs, axis=2)
    mixed = jnp.einsum('bsgc,gcd->bsgd', pooled, pool_w.astype(jnp.float32))
    return (mixed.reshape(b, s, POOL_WIDTH) * pool_scale.astype(jnp.float32)).astype(u.dtype)

def _scan_combine(left, right):
    a1r, a1i, b1r, b1i = left
    a2r, a2i, b2r, b2i = right
    ar = a2r * a1r - a2i * a1i
    ai = a2r * a1i + a2i * a1r
    br = a2r * b1r - a2i * b1i + b2r
    bi = a2r * b1i + a2i * b1r + b2i
    return (ar, ai, br, bi)

def _s5(u, log_dt, a_re, a_im, b_re, b_im, c_re, c_im, d_skip, w_glu):
    bsz, s, _ = u.shape
    f32 = jnp.float32
    u32 = u.astype(f32).reshape(bsz, s, SSM_GROUPS, SSM_GROUP_DIM)
    dt = jnp.exp(log_dt.astype(f32))[:, None]
    ar = a_re.astype(f32)
    ai = a_im.astype(f32)
    mag = jnp.exp(ar * dt)
    ang = ai * dt
    abar_re = mag * jnp.cos(ang)
    abar_im = mag * jnp.sin(ang)
    den = ar * ar + ai * ai
    nr = abar_re - 1.0
    ni = abar_im
    k_re = (nr * ar + ni * ai) / den
    k_im = (ni * ar - nr * ai) / den
    br = b_re.astype(f32)
    bi = b_im.astype(f32)
    bb_re = k_re[..., None] * br - k_im[..., None] * bi
    bb_im = k_re[..., None] * bi + k_im[..., None] * br
    bu_re = jnp.einsum('bsgh,gph->bsgp', u32, bb_re)
    bu_im = jnp.einsum('bsgh,gph->bsgp', u32, bb_im)
    shape = bu_re.shape
    _, _, x_re, x_im = lax.associative_scan(
        _scan_combine,
        (jnp.broadcast_to(abar_re, shape), jnp.broadcast_to(abar_im, shape), bu_re, bu_im),
        axis=1)
    y = (jnp.einsum('bsgp,ghp->bsgh', x_re, c_re.astype(f32))
         - jnp.einsum('bsgp,ghp->bsgh', x_im, c_im.astype(f32)))
    y = y.reshape(bsz, s, SSM_WIDTH) + d_skip.astype(f32) * u32.reshape(bsz, s, SSM_WIDTH)
    gv = jnp.einsum('bsc,ce->bse', y, w_glu.astype(f32))
    val, gate = jnp.split(gv, 2, axis=-1)
    return (val * jax.nn.sigmoid(gate)).astype(u.dtype)

def _even_mixer(h, w_in, pool_w, pool_scale, log_dt, a_re, a_im, b_re, b_im,
                c_re, c_im, d_skip, w_glu, w_out):
    proj = jnp.einsum('bsd,de->bse', h, w_in)
    u_pool = proj[..., :POOL_WIDTH]
    u_ssm = proj[..., POOL_WIDTH:MIX_WIDTH]
    z = proj[..., MIX_WIDTH:]
    y_pool = _multiscale_pool(u_pool, pool_w, pool_scale)
    y_ssm = _s5(u_ssm, log_dt, a_re, a_im, b_re, b_im, c_re, c_im, d_skip, w_glu)
    y = jnp.concatenate([y_pool, y_ssm], axis=-1) * jax.nn.silu(z)
    return jnp.einsum('bse,ed->bsd', y, w_out)

def _odd_mixer(h, w_in, conv_w, conv_b, ln_g, ln_b, w_out):
    proj = jnp.einsum('bsd,de->bse', h, w_in)
    val = proj[..., :CONV_CHANNELS]
    gt = proj[..., CONV_CHANNELS:2 * CONV_CHANNELS]
    z = proj[..., 2 * CONV_CHANNELS:]
    g = (val * jax.nn.sigmoid(gt)).astype(jnp.float32)
    kern = conv_w.astype(jnp.float32)[:, None, :]
    c = lax.conv_general_dilated(
        g, kern, window_strides=(1,), padding=[(CONV_KERNEL - 1, 0)],
        dimension_numbers=('NWC', 'WIO', 'NWC'), feature_group_count=CONV_CHANNELS)
    c = c + conv_b.astype(jnp.float32)
    mu = jnp.mean(c, axis=-1, keepdims=True)
    cc = c - mu
    var = jnp.mean(cc * cc, axis=-1, keepdims=True)
    c = cc * lax.rsqrt(var + LN_EPS) * ln_g.astype(jnp.float32) + ln_b.astype(jnp.float32)
    y = (jax.nn.silu(c) * jax.nn.silu(z.astype(jnp.float32))).astype(h.dtype)
    return jnp.einsum('bse,ed->bsd', y, w_out)

def second_inputs(seed: int = 0) -> dict:
    key = jax.random.key(seed)
    ks = jax.random.split(key, 24)
    f32 = jnp.float32

    def nrm(k, shape, scale):
        return jax.random.normal(k, shape, f32) * scale

    n_idx = jnp.arange(SSM_STATE, dtype=f32)
    a_im0 = jnp.broadcast_to(math.pi * n_idx, (N_EVEN_2, SSM_GROUPS, SSM_STATE))
    return {
        "x": jax.random.normal(ks[0], (BATCH, SEQ, D_MODEL), f32),
        "even_norm": 1.0 + nrm(ks[1], (N_EVEN_2, D_MODEL), 0.05),
        "even_w_in": nrm(ks[2], (N_EVEN_2, D_MODEL, 2 * MIX_WIDTH), D_MODEL ** -0.5),
        "pool_w": nrm(ks[3], (N_EVEN_2, POOL_GROUPS, POOL_GROUP_DIM, POOL_GROUP_DIM), POOL_GROUP_DIM ** -0.5),
        "pool_scale": 1.0 + nrm(ks[4], (N_EVEN_2, POOL_WIDTH), 0.05),
        "ssm_log_dt": jax.random.uniform(ks[5], (N_EVEN_2, SSM_GROUPS), f32,
                                         math.log(DT_MIN), math.log(DT_MAX)),
        "ssm_a_re": -0.5 * jnp.exp(nrm(ks[6], (N_EVEN_2, SSM_GROUPS, SSM_STATE), 0.05)),
        "ssm_a_im": a_im0 + nrm(ks[7], (N_EVEN_2, SSM_GROUPS, SSM_STATE), 0.01),
        "ssm_b_re": nrm(ks[8], (N_EVEN_2, SSM_GROUPS, SSM_STATE, SSM_GROUP_DIM), (2 * SSM_GROUP_DIM) ** -0.5),
        "ssm_b_im": nrm(ks[9], (N_EVEN_2, SSM_GROUPS, SSM_STATE, SSM_GROUP_DIM), (2 * SSM_GROUP_DIM) ** -0.5),
        "ssm_c_re": nrm(ks[10], (N_EVEN_2, SSM_GROUPS, SSM_GROUP_DIM, SSM_STATE), SSM_STATE ** -0.5),
        "ssm_c_im": nrm(ks[11], (N_EVEN_2, SSM_GROUPS, SSM_GROUP_DIM, SSM_STATE), SSM_STATE ** -0.5),
        "ssm_d": nrm(ks[12], (N_EVEN_2, SSM_WIDTH), 1.0),
        "ssm_w_glu": nrm(ks[13], (N_EVEN_2, SSM_WIDTH, 2 * SSM_WIDTH), SSM_WIDTH ** -0.5),
        "even_w_out": nrm(ks[14], (N_EVEN_2, MIX_WIDTH, D_MODEL), MIX_WIDTH ** -0.5),
        "odd_norm": 1.0 + nrm(ks[15], (N_ODD_2, D_MODEL), 0.05),
        "odd_w_in": nrm(ks[16], (N_ODD_2, D_MODEL, 3 * CONV_CHANNELS), D_MODEL ** -0.5),
        "conv_w": nrm(ks[17], (N_ODD_2, CONV_KERNEL, CONV_CHANNELS), CONV_KERNEL ** -0.5),
        "conv_b": nrm(ks[18], (N_ODD_2, CONV_CHANNELS), 0.02),
        "conv_ln_g": 1.0 + nrm(ks[19], (N_ODD_2, CONV_CHANNELS), 0.05),
        "conv_ln_b": nrm(ks[20], (N_ODD_2, CONV_CHANNELS), 0.02),
        "odd_w_out": nrm(ks[21], (N_ODD_2, CONV_CHANNELS, D_MODEL), CONV_CHANNELS ** -0.5),
        "final_norm": 1.0 + nrm(ks[22], (D_MODEL,), 0.05),
    }

def second_block(x, even_norm, even_w_in, pool_w, pool_scale, ssm_log_dt, ssm_a_re, ssm_a_im,
              ssm_b_re, ssm_b_im, ssm_c_re, ssm_c_im, ssm_d, ssm_w_glu, even_w_out,
              odd_norm, odd_w_in, conv_w, conv_b, conv_ln_g, conv_ln_b, odd_w_out, final_norm):
    for i in range(DEPTH):
        j = i // 2
        if i % 2 == 0:
            h = _rmsnorm(x, even_norm[j])
            x = x + _even_mixer(h, even_w_in[j], pool_w[j], pool_scale[j], ssm_log_dt[j],
                                ssm_a_re[j], ssm_a_im[j], ssm_b_re[j], ssm_b_im[j],
                                ssm_c_re[j], ssm_c_im[j], ssm_d[j], ssm_w_glu[j], even_w_out[j])
        else:
            h = _rmsnorm(x, odd_norm[j])
            x = x + _odd_mixer(h, odd_w_in[j], conv_w[j], conv_b[j], conv_ln_g[j],
                               conv_ln_b[j], odd_w_out[j])
    return _rmsnorm(x, final_norm)


def setup_inputs(seed=0):
    out = dict(first_inputs(seed))
    for name, value in second_inputs(seed + 1).items():
        if name != "x":
            out[name + "_2"] = value
    return out


def reference(
    x, norm_g, ffn_w_gate, ffn_w_up, ffn_w_down, attn_w_in, attn_w_out, rel_bias, mlstm_w_in,
    mlstm_b_gates, mlstm_conv_w, mlstm_head_g, mlstm_w_out, even_norm_2, even_w_in_2, pool_w_2,
    pool_scale_2, ssm_log_dt_2, ssm_a_re_2, ssm_a_im_2, ssm_b_re_2, ssm_b_im_2, ssm_c_re_2,
    ssm_c_im_2, ssm_d_2, ssm_w_glu_2, even_w_out_2, odd_norm_2, odd_w_in_2, conv_w_2, conv_b_2,
    conv_ln_g_2, conv_ln_b_2, odd_w_out_2, final_norm_2,
):
    x = first_block(
        x, norm_g, ffn_w_gate, ffn_w_up, ffn_w_down, attn_w_in, attn_w_out, rel_bias,
        mlstm_w_in, mlstm_b_gates, mlstm_conv_w, mlstm_head_g, mlstm_w_out,
    )
    return second_block(
        x, even_norm_2, even_w_in_2, pool_w_2, pool_scale_2, ssm_log_dt_2, ssm_a_re_2,
        ssm_a_im_2, ssm_b_re_2, ssm_b_im_2, ssm_c_re_2, ssm_c_im_2, ssm_d_2, ssm_w_glu_2,
        even_w_out_2, odd_norm_2, odd_w_in_2, conv_w_2, conv_b_2, conv_ln_g_2, conv_ln_b_2,
        odd_w_out_2, final_norm_2,
    )


_drawn_inputs = setup_inputs


def setup_inputs(seed=0):
    import zlib

    import numpy as np

    out = dict(_drawn_inputs(seed))
    spreads = {}
    factors = {'mlstm_head_g': 21.919,
     'even_norm_2': 3.741,
     'pool_scale_2': 7.115,
     'ssm_log_dt_2': 41.688,
     'ssm_a_re_2': 64.0,
     'ssm_a_im_2': 37.752,
     'ssm_b_re_2': 55.376,
     'ssm_b_im_2': 50.432,
     'ssm_c_re_2': 54.648,
     'ssm_c_im_2': 51.72,
     'odd_norm_2': 4.361,
     'conv_b_2': 22.722,
     'conv_ln_g_2': 18.569,
     'conv_ln_b_2': 51.012}
    for name, (base, spread) in spreads.items():
        noise = np.random.default_rng([zlib.crc32(name.encode()), seed]).standard_normal(out[name].shape)
        drawn = base * np.exp(spread * noise) if base else spread * noise
        out[name] = jnp.asarray(drawn.astype(out[name].dtype))
    for name, factor in factors.items():
        out[name] = (out[name] * factor).astype(out[name].dtype)
    return out
```

```python
from contextlib import ExitStack

import numpy as np
import concourse.bass as bass
from concourse import mybir

F32 = mybir.dt.float32
ALU = mybir.AluOpType
ACT = mybir.ActivationFunctionType
AX = mybir.AxisListType

P = 128
T = 512
D = 1024
KD = D // P
FF = 2816
KF = FF // P
HALF_KF = KF // 2
NB_BUCKETS = 32
RING = 4
SLOT = HALF_KF * P
HEADS = 8
EPS_RMS = 1e-6
EPS_LN = 1e-5
CONV_K = 31
PAD = CONV_K - 1
MCONV_K = 4
NSTATE_T = 16
TWO_PI = 6.2831845
ROUND = 12582912.0
NEG = -1e30
STRIP_W = 5 * P
OFF = (0, 512, 896, 1152)
PACKED = 1280

SECTIONS = []
for _name, _kinds in (("ffn0", "f"), ("attn", "a"), ("ffn1", "f"), ("ffn2", "f"), ("mlstm", "m"),
                      ("ffn3", "f"), ("even", "e"), ("odd", "o")):
    SECTIONS += {
        "f": [(_name + ".gu", 2 * KF, "w8"), (_name + ".dn", 2 * KD, "wd")],
        "a": [("attn.qk", 16, "w8"), ("attn.v", 8, "w8"), ("attn.out", 8, "w8")],
        "m": [("mlstm.qk", 16, "w8"), ("mlstm.v", 8, "w8"), ("mlstm.o", 8, "w8"), ("mlstm.out", 8, "w8")],
        "e": [("even.in", 16, "w8"), ("even.glu", 4, "w8"), ("even.out", 8, "w8")],
        "o": [("odd.in", 24, "w8"), ("odd.out", 8, "w8")],
    }[_kinds]

BLK, TILE, SRC = {}, {}, {}
_b = _t = 0
_rows = {"w8": 0, "wd": 0}
for _name, _n, _s in SECTIONS:
    BLK[_name], TILE[_name], SRC[_name] = _b, _t, _rows[_s]
    _b += _n
    _t += _n // 2 if _s == "wd" else (8 if _name == "even.glu" else _n)
    _rows[_s] += _n
NBLK = dict((n, c) for n, c, _ in SECTIONS)

NORMS = ["ffn0.pre", "ffn0.post", "attn.pre", "attn.post", "ffn1.pre", "ffn1.post", "ffn2.pre", "ffn2.post",
         "mlstm.pre", "mlstm.post", "ffn3.pre", "ffn3.post", "even.pre", "odd.pre", "odd.ln", "final"]
PRE = [n for n in NORMS if not n.endswith(("post", "ln"))]
UPD = ["ffn0", "attn", "ffn1", "ffn2", "mlstm", "ffn3", "even", "odd"]

VEC = {}
_c = 0
for _name, _n in (("norm_g", 96), ("even_norm", 8), ("odd_norm", 8), ("final_norm", 8), ("pool_scale", 4),
                  ("ssm_d", 4), ("conv_b", 8), ("ln_g", 8), ("ln_b", 8), ("head_g", 8), ("conv_w", 31 * 8),
                  ("mconv_w", 4 * 16), ("log_dt", 16), ("a_re", 16), ("a_im", 16), ("b_i", 1), ("b_f", 1)):
    VEC[_name] = _c
    _c += _n
NVEC = _c
GCOL = {"ffn0.pre": 0, "ffn0.post": 8, "attn.pre": 16, "attn.post": 24, "ffn1.pre": 32, "ffn1.post": 40,
        "ffn2.pre": 48, "ffn2.post": 56, "mlstm.pre": 64, "mlstm.post": 72, "ffn3.pre": 80, "ffn3.post": 88,
        "even.pre": VEC["even_norm"], "odd.pre": VEC["odd_norm"], "final": VEC["final_norm"]}

C_ID, C_TRI, C_ONE, C_INV = 0, P, 2 * P, 3 * P
NCONST = C_INV + 64


def skewed(scratch):
    w = HEADS * STRIP_W
    return bass.AP(tensor=scratch.tensor, offset=scratch.offset + P - 1,
                   ap=[[w - 1, P], [STRIP_W, HEADS], [1, T]])


def build(nc, x_in, w8, wd, vecs, consts, rel_bias, buckets, w_gates, pool_w, bst, cst, scratch, out):
    ctx = ExitStack()
    with ctx:
        def sb(name, cols):
            return ctx.enter_context(nc.sbuf_tensor(name + "_sb", [P, cols], F32))

        def sem(name):
            return ctx.enter_context(nc.semaphore(name))

        def chunks(ap, n=None):
            return ap.rearrange("p (a n) -> p a n", n=n or T)

        def at(buf, i):
            return buf[:, bass.ds(i, 1), :].rearrange("p a n -> p (a n)")

        x = chunks(sb("x", KD * T)[:, :])
        xn_f = sb("xn", KD * T)
        xn = chunks(xn_f[:, :])
        sq_f = sb("sq", KD * T)
        sq = chunks(sq_f[:, :])
        hf_f = sb("hf", KD * T)
        hf = chunks(hf_f[:, :])
        ring_f = sb("ring", RING * SLOT)
        ring = chunks(ring_f[:, :], SLOT)
        mix = sb("mix", 27 * 1024)
        cst_sb = sb("consts", NCONST)
        vec = sb("vecs", NVEC)
        rstd = sb("rstd", T)
        std = sb("std", T)
        small = sb("small", 320)
        wg = sb("wg", KD * 2 * HEADS)
        sg = hf[:, 0:2, :]
        ident = cst_sb[:, C_ID:C_ID + P]
        negtri = cst_sb[:, C_TRI:C_TRI + P]
        ones = cst_sb[:, C_ONE:C_ONE + P]
        negones = sb("negones", P)

        def region(start, n):
            return mix[:, start:start + n]

        h = chunks(region(0, KF * T))
        qkT = chunks(region(0, 16 * T))
        va = chunks(region(8192, 4 * T))
        vd = chunks(region(10240, 4 * T))
        strip = chunks(region(12288, HEADS * T))
        mixed = chunks(region(16384, KD * T))
        work = region(20480, 7168)
        mqk = chunks(region(0, 16 * T))
        mv = region(8192, 4 * D).rearrange("p (a n) -> p a n", n=D)
        sigo = chunks(region(12288, KD * T))
        hid = chunks(region(16384, KD * T))
        cosT = chunks(region(11264, 16 * T))
        sinT = chunks(region(19456, 16 * T))
        uin = chunks(region(0, 8 * T))
        zin = chunks(region(4096, 8 * T))
        gpad = region(0, KD * (T + PAD)).rearrange("p (a n) -> p a n", n=T + PAD)
        cc = chunks(region(8192, KD * T))
        zz = chunks(region(12288, KD * T))
        yo = chunks(region(16384, KD * T))

        banks = ctx.enter_context(nc.psum_tensor("banks", [P, 8, T], F32))
        lin = [banks[:, i, :] for i in range(4)]
        ps_n = banks[:, 7, :]

        w_loaded = [sem(f"w_loaded{i}") for i in range(RING)]
        blocks_done = sem("blocks_done")
        tiles_freed = sem("tiles_freed")
        gate_act = sem("gate_act")
        in_loaded = sem("in_loaded")
        squares = sem("squares")
        sumsq_ready = sem("sumsq_ready")
        var_ready = sem("var_ready")
        std_ready = sem("std_ready")
        rstd_ready = sem("rstd_ready")
        xn_ready = sem("xn_ready")
        scaled = sem("scaled")
        x_ready = sem("x_ready")
        prep = sem("prep")
        prep_act = sem("prep_act")
        prep_pe = sem("prep_pe")
        prep_pool = sem("prep_pool")
        strip_line = sem("strip_line")
        strip_out = sem("strip_out")
        strip_in = sem("strip_in")
        out_done = sem("out_done")
        pool_turn = sem("pool_turn")
        tab = sem("tab")
        tab_act = sem("tab_act")
        a_abs = sem("a_abs")
        a_ex = sem("a_ex")
        a_exp = sem("a_exp")
        a_ln = sem("a_ln")
        a_mx = sem("a_mx")
        a_odl = sem("a_odl")
        a_oev = sem("a_oev")
        a_oev2 = sem("a_oev2")
        a_osb = sem("a_osb")
        a_p = sem("a_p")
        a_rc = sem("a_rc")
        a_rl = sem("a_rl")
        a_s = sem("a_s")
        a_sadd = sem("a_sadd")
        a_sp = sem("a_sp")
        a_spr = sem("a_spr")
        a_staged = sem("a_staged")
        a_t = sem("a_t")
        a_tc = sem("a_tc")
        a_w = sem("a_w")
        a_wm = sem("a_wm")
        a_z = sem("a_z")
        conv_act = sem("conv_act")
        conv_v = sem("conv_v")
        e_bb = sem("e_bb")
        e_btc = sem("e_btc")
        e_loaded = sem("e_loaded")
        e_pm = sem("e_pm")
        e_pool = sem("e_pool")
        e_sig = sem("e_sig")
        e_t = sem("e_t")
        e_val = sem("e_val")
        e_w2 = sem("e_w2")
        e_win = sem("e_win")
        e_y = sem("e_y")
        g_act = sem("g_act")
        g_chain = sem("g_chain")
        g_cols = sem("g_cols")
        g_pe = sem("g_pe")
        g_rows = sem("g_rows")
        g_vec = sem("g_vec")
        halved = sem("halved")
        iota_ready = sem("iota_ready")
        m_d = sem("m_d")
        m_d2 = sem("m_d2")
        m_dm = sem("m_dm")
        m_dn = sem("m_dn")
        m_eb = sem("m_eb")
        m_ebc = sem("m_ebc")
        m_fin = sem("m_fin")
        m_hid = sem("m_hid")
        m_mb = sem("m_mb")
        m_nd = sem("m_nd")
        m_p = sem("m_p")
        m_pm = sem("m_pm")
        m_rec = sem("m_rec")
        m_s = sem("m_s")
        m_sqr = sem("m_sqr")
        m_ss = sem("m_ss")
        m_staged = sem("m_staged")
        m_std = sem("m_std")
        m_var = sem("m_var")
        o_cen = sem("o_cen")
        o_conv = sem("o_conv")
        o_n = sem("o_n")
        o_s = sem("o_s")
        o_sig = sem("o_sig")
        o_sum = sem("o_sum")
        o_v = sem("o_v")
        o_y = sem("o_y")
        prep_exp = sem("prep_exp")
        prep_x = sem("prep_x")
        s_bu = sem("s_bu")
        s_buc = sem("s_buc")
        s_pr = sem("s_pr")
        s_rot = sem("s_rot")
        s_staged = sem("s_staged")
        s_v = sem("s_v")
        s_y = sem("s_y")
        s_ych = sem("s_ych")
        s_ym = sem("s_ym")
        tab_v = sem("tab_v")

        norm_no = {n: i for i, n in enumerate(NORMS)}
        pre_no = {n: i for i, n in enumerate(PRE)}
        FREE0 = 4

        def g_of(name, c):
            col = GCOL[name] + c
            return vec[:, col:col + 1]

        def wait_w(pe, name, n_blk, rounds):
            pe.wait_ge(w_loaded[n_blk % RING], 16 * (BLK[name] // RING + n_blk // RING + 1) + 16 * rounds)


        DT, XR, PHI, R_, EM, SER, MASK, E1, SI, S2, CO, NR, NI, KRE, KIM, DEN, TA, TB = range(0, 288, 16)
        NMX, LSUM, RL = 288, 296, 304

        def col(c, n=16):
            return small[:, c:c + n]

        lines = work[:, 0:HEADS * STRIP_W].rearrange("p (h n) -> p h n", n=STRIP_W)
        bk = work[:, 5120:5760]
        rb = work[:, 5760:5768]
        rb8 = work[:, 5768:6792].rearrange("p (h n) -> p h n", n=P)
        LB = NB_BUCKETS + 1

        def prep_tensor(pe):
            pe.wait_ge(prep, 2)
            for hh in range(HEADS):
                if hh >= 2:
                    pe.wait_ge(prep_act, hh - 1)
                for half in range(2):
                    last = pe.matmul(banks[:, 2 * (hh % 2) + half, 0:320], rb8[0:LB, hh, :],
                                     bk[0:LB, 320 * half:320 * half + 320], start=True, stop=True)
                last.then_inc(prep_pe, 1)

        def prep_scalar(act):
            act.dma_start(bk[0:LB, :], buckets).then_inc(strip_line, 16)
            act.dma_start(rb[0:NB_BUCKETS, :], rel_bias).then_inc(strip_line, 16)
            act.dma_start(wg[:, :], w_gates).then_inc(strip_line, 16)
            act.wait_ge(in_loaded, 48)
            act.activation(std[:, 0:1], vec[:, 0:1], ACT.Copy).then_inc(a_w, 1)
            act.activation(std[:, 1:2], vec[:, 0:1], ACT.Copy).then_inc(a_oev, 1)
            act.activation(std[:, 2:3], vec[:, 0:1], ACT.Copy).then_inc(a_oev2, 1)
            act.activation(std[:, 3:4], vec[:, 0:1], ACT.Copy).then_inc(a_tc, 1)
            act.activation(std[:, 4:5], vec[:, 0:1], ACT.Copy).then_inc(m_ebc, 1)
            act.activation(std[:, 5:6], vec[:, 0:1], ACT.Copy).then_inc(m_sqr, 1)
            act.activation(std[:, 6:7], vec[:, 0:1], ACT.Copy).then_inc(s_buc, 1)
            for hh in range(HEADS):
                act.wait_ge(prep_pe, hh + 1)
                act.activation(lines[:, hh, :].rearrange("p (a n) -> p a n", a=2),
                               banks[:, 2 * (hh % 2):2 * (hh % 2) + 2, 0:320], ACT.Copy).then_inc(prep_act, 1)
            act.wait_ge(prep_act, HEADS)
            act.dma_start(scratch, work[:, 0:HEADS * STRIP_W]).then_inc(strip_out, 16)
            act.activation(col(DT), vec[:, VEC["log_dt"]:VEC["log_dt"] + 16], ACT.Exp).then_inc(prep_exp, 1)
            act.wait_ge(strip_out, 16)
            act.dma_start(strip, skewed(scratch)).then_inc(strip_in, 16)
            act.wait_ge(prep_x, 1)
            act.activation(col(E1), col(XR), ACT.Exp).then_inc(prep_exp, 1)
            act.activation(col(SI), col(PHI), ACT.Sin, scale=TWO_PI).then_inc(prep_exp, 1)
            act.activation(col(S2), col(PHI), ACT.Sin, scale=TWO_PI / 2).then_inc(prep_exp, 1)

        def prep_vector(dve):
            chain = [0]

            def link(ins):
                chain[0] += 1
                ins.then_inc(prep, 1)
                dve.wait_ge(prep, chain[0])

            link(dve.memset(rb[NB_BUCKETS:LB, :], 1.0))
            dve.wait_ge(strip_line, 48)
            link(dve.tensor_copy(rb8[0:LB, :, :], rb[0:LB, :].unsqueeze(2).to_broadcast([LB, HEADS, P])))
            dve.memset(negones[:, :], -1.0).then_inc(tiles_freed, FREE0)
            dve.memset(rstd[:, 0:1], 0.0).then_inc(a_sadd, 2)
            dve.memset(rstd[:, 1:2], 0.0).then_inc(m_dm, 1)
            dve.memset(rstd[:, 2:3], 0.0).then_inc(m_p, 1)
            dve.memset(rstd[:, 3:4], 0.0).then_inc(m_dn, 1)
            dve.memset(rstd[:, 4:5], 0.0).then_inc(m_hid, 2)
            dve.memset(rstd[:, 5:6], 0.0).then_inc(s_rot, 2)
            dve.memset(rstd[:, 7:8], 0.0).then_inc(a_t, 2)
            dve.memset(rstd[:, 8:9], 0.0).then_inc(conv_act, 2)
            dve.memset(rstd[:, 9:10], 0.0).then_inc(s_pr, 1)
            dve.memset(rstd[:, 10:11], 0.0).then_inc(s_ym, 1)
            dve.memset(rstd[:, 6:7], 0.0).then_inc(s_ych, 1)
            dve.wait_ge(in_loaded, 48)
            for c in (8, 40, 56, 88):
                dve.tensor_scalar(vec[:, c:c + 8], vec[:, c:c + 8], 0.5, None, ALU.mult).then_inc(halved, 1)
            dve.wait_ge(halved, 4)
            are, aim = (vec[:, VEC[n]:VEC[n] + 16] for n in ("a_re", "a_im"))
            tt = dve.tensor_tensor
            ts = dve.tensor_scalar
            dve.wait_ge(prep_exp, 1)
            link(tt(col(XR), are, col(DT), ALU.mult))
            link(tt(col(TA), aim, col(DT), ALU.mult))
            link(ts(col(TA), col(TA), float(1 / (2 * np.pi)), None, ALU.mult))
            link(ts(col(TB), col(TA), ROUND, ROUND, ALU.add, ALU.subtract))
            tt(col(PHI), col(TA), col(TB), ALU.subtract).then_inc(prep_x, 1)
            dve.wait_ge(prep_x, 1)
            link(ts(col(TA), col(XR), 0.5, -0.5, ALU.min, ALU.max))
            link(dve.memset(col(SER), 1.0))
            for k in range(9, 1, -1):
                link(dve.scalar_tensor_tensor(col(SER), col(SER), 1.0 / k, col(TA), ALU.mult, ALU.mult))
                link(ts(col(SER), col(SER), 1.0, None, ALU.add))
            link(tt(col(SER), col(SER), col(TA), ALU.mult))
            link(tt(col(MASK), col(TA), col(XR), ALU.is_equal))
            link(tt(col(SER), col(SER), col(MASK), ALU.mult))
            link(ts(col(MASK), col(MASK), -1.0, 1.0, ALU.mult, ALU.add))
            dve.wait_ge(prep_exp, 4)
            link(ts(col(E1), col(E1), -1.0, None, ALU.add))
            link(tt(col(E1), col(E1), col(MASK), ALU.mult))
            link(tt(col(EM), col(E1), col(SER), ALU.add))
            link(ts(col(R_), col(EM), 1.0, None, ALU.add))
            link(tt(col(S2), col(S2), col(S2), ALU.mult))
            link(ts(col(CO), col(S2), -2.0, 1.0, ALU.mult, ALU.add))
            link(tt(col(NR), col(EM), col(CO), ALU.mult))
            link(dve.scalar_tensor_tensor(col(NR), col(S2), -2.0, col(NR), ALU.mult, ALU.add))
            link(tt(col(NI), col(R_), col(SI), ALU.mult))
            link(tt(col(DEN), are, are, ALU.mult))
            link(tt(col(TA), aim, aim, ALU.mult))
            link(tt(col(DEN), col(DEN), col(TA), ALU.add))
            link(dve.reciprocal(col(DEN), col(DEN)))
            link(tt(col(TA), col(NR), are, ALU.mult))
            link(tt(col(TB), col(NI), aim, ALU.mult))
            link(tt(col(TA), col(TA), col(TB), ALU.add))
            link(tt(col(KRE), col(TA), col(DEN), ALU.mult))
            link(tt(col(TA), col(NI), are, ALU.mult))
            link(tt(col(TB), col(NR), aim, ALU.mult))
            link(tt(col(TA), col(TA), col(TB), ALU.subtract))
            link(tt(col(KIM), col(TA), col(DEN), ALU.mult))

        def evac(eng, name, n, fn):
            with eng.Fori(0, n // 4) as i:
                for m in range(4):
                    eng.wait_ge(blocks_done, BLK[name] + 4 * i + m + 1)
                    fn(i, m).then_inc(tiles_freed, 1)

        qp, kp, vp, qdp, kdp, vdp = (xn[:, j, :] for j in range(6))
        ab = [sq_f[:, PACKED * e:PACKED * (e + 1)] for e in range(2)]
        sp_ = [hf_f[:, PACKED * e:PACKED * (e + 1)] for e in range(2)]
        wk = [work[:, PACKED * e:PACKED * (e + 1)] for e in range(2)]
        ssb = [work[:, 2560 + T * j:3072 + T * j] for j in range(2)]
        pT = [work[:, 3584 + PACKED * e:3584 + PACKED * (e + 1)] for e in range(2)]
        Z01 = banks[:, 0, :]
        Z23 = banks[:, 1:3, 0:384]

        def zcols(kb):
            return (banks[:, 0, :], banks[:, 1, 0:384], banks[:, 2, 0:256], banks[:, 2, 256:384])[kb]

        def packed(buf, kb):
            return buf[:, OFF[kb]:OFF[kb] + T - P * kb]

        def two(buf):
            return buf[:, 0:T], buf[:, T:PACKED].rearrange("p (a n) -> p a n", a=2)

        def attention_in_scalar(act):
            for c in range(16):
                act.wait_ge(blocks_done, BLK["attn.qk"] + c + 1)
                act.activation(qkT[:, c, :], lin[c % 4], ACT.Copy,
                               scale=0.125 if c // 4 % 2 == 0 else 1.0).then_inc(tiles_freed, 1)
            for half, dst in enumerate((va, vd)):
                act.wait_ge(blocks_done, BLK["attn.v"] + 4 * half + 4)
                for t in range(4):
                    act.activation(dst[:, t, :], lin[t], ACT.Copy).then_inc(tiles_freed, 1)

        def attention_in_vector(dve):
            pass

        def attention_pool(pool):
            pool.wait_ge(tiles_freed, FREE0 + TILE["attn.v"] + 8)
            with pool.Fori(0, 4) as i:
                pool.tensor_copy(qp, at(qkT, i))
                pool.tensor_copy(kp, at(qkT, i + 4))
                pool.tensor_copy(vp.rearrange("p (a n) -> p a n", a=4), va[:, :, bass.ds(P * i, P)])
                pool.tensor_copy(qdp, at(qkT, i + 8))
                pool.tensor_copy(kdp, at(qkT, i + 12))
                pool.tensor_copy(vdp.rearrange("p (a n) -> p a n", a=4),
                                 vd[:, :, bass.ds(P * i, P)]).then_inc(a_staged, 1)
                for e in range(2):
                    for buf, signal, done, base in ((sp_[e], a_spr, a_sp, 1), (wk[e], a_w, a_wm, 2)):
                        pool.wait_ge(signal, 2 * i + e + base)
                        pool.sem_inc(pool_turn, 1)
                        for kb in range(4):
                            d = buf[:, OFF[kb]:OFF[kb] + P]
                            last = pool.affine_select(out=d, in_=d, pattern=[[1, P]], compare_op=ALU.is_gt,
                                                      fill=0.0, base=0, channel_multiplier=-1)
                        last.then_inc(done, 1)
                pool.wait_ge(a_odl, 2 * i + 2)

        def attention_tensor(pe):
            with pe.Fori(0, 4) as i:
                for e in range(2):
                    rows = slice(64 * e, 64 * e + 64)
                    u = 2 * i + e

                    def scores(qb):
                        pe.wait_ge(a_sadd, 4 * u + qb + 1)
                        pe.matmul(banks[:, 3 + qb % 2, 0:P * (qb + 1)], qdp[rows, P * qb:P * (qb + 1)],
                                  kdp[rows, 0:P * (qb + 1)], start=True, stop=True).then_inc(a_s, 1)

                    def turn(qb):
                        pe.wait_ge(a_p, 4 * u + qb + 1)
                        pe.wait_ge(a_tc, 4 * u + qb + 1)
                        for kb in range(qb + 1):
                            last = pe.transpose(banks[:, 5, P * kb:P * (kb + 1)],
                                                ssb[qb % 2][:, P * kb:P * (kb + 1)], ident)
                        last.then_inc(a_t, 1)

                    if e == 0:
                        pe.wait_ge(a_staged, i + 1)
                    pe.wait_ge(a_w, u + 1)
                    for kb in range(4):
                        last = pe.matmul(zcols(kb), kp[rows, P * kb:P * (kb + 1)], qp[rows, P * kb:T],
                                         start=(kb != 3), stop=False, skip_group_check=True)
                    last.then_inc(a_z, 1)
                    scores(0)
                    scores(1)
                    pe.wait_ge(a_sp, u + 1)
                    for kb in range(4):
                        dst = zcols(kb)
                        last = pe.matmul(dst, negtri, packed(sp_[e], kb), start=False, stop=(kb == 3),
                                         skip_group_check=True)
                        for later in range(kb + 1, 4):
                            last = pe.matmul(dst[:, P * (later - kb):T - P * kb], negones[:, :],
                                             packed(sp_[e], later), start=False, stop=True,
                                             skip_group_check=True)
                    last.then_inc(a_rc, 1)
                    turn(0)
                    scores(2)
                    turn(1)
                    scores(3)
                    turn(2)
                    pe.wait_ge(a_wm, u + 1)
                    if e == 0:
                        pe.wait_ge(a_oev, i + 1)
                    for kb in range(4):
                        last = pe.matmul(banks[rows, 6, P * kb:T], vp[:, P * kb + 64 * e:P * kb + 64 * e + 64],
                                         packed(wk[e], kb), start=(kb == 0), stop=(kb == 3),
                                         skip_group_check=True)
                    last.then_inc(a_osb, 1)
                    turn(3)
                    pe.wait_ge(a_tc, 4 * u + 5)
                    if e == 0:
                        pe.wait_ge(a_oev2, i + 1)
                    for kb in range(4):
                        last = pe.matmul(banks[rows, 7, P * kb:T], vdp[:, P * kb + 64 * e:P * kb + 64 * e + 64],
                                         packed(pT[e], kb), start=(kb == 0), stop=(kb == 3),
                                         skip_group_check=True)
                    last.then_inc(a_odl, 1)
            pe.wait_ge(a_oev, 5)
            pe.wait_ge(a_oev2, 5)

        def attention_scalar(act):
            with act.Fori(0, 4) as i:
                for e in range(2):
                    u = 2 * i + e

                    def exps(qb):
                        act.wait_ge(a_mx, 4 * u + qb + 1)
                        n = P * (qb + 1)
                        act.activation(ssb[qb % 2][:, 0:n], ssb[qb % 2][:, 0:n], ACT.Exp,
                                       bias=small[:, NMX + qb:NMX + qb + 1],
                                       accum_out=small[:, LSUM + qb:LSUM + qb + 1]).then_inc(a_exp, 1)

                    def copy_turned(qb):
                        act.wait_ge(a_t, 4 * u + qb + 3)
                        for kb in range(qb + 1):
                            o = OFF[kb] + P * (qb - kb)
                            last = act.activation(pT[e][:, o:o + P], banks[:, 5, P * kb:P * (kb + 1)], ACT.Copy)
                        last.then_inc(a_tc, 1)

                    act.wait_ge(a_z, u + 1)
                    act.activation(two(ab[e])[0], Z01, ACT.Abs)
                    act.activation(two(ab[e])[1], Z23, ACT.Abs).then_inc(a_abs, 1)
                    act.wait_ge(a_abs, u + 1)
                    act.activation(ab[e], ab[e], ACT.Exp, scale=-1.0).then_inc(a_ex, 1)
                    act.wait_ge(a_ex, u + 1)
                    act.activation(ab[e], ab[e], ACT.Ln, bias=1.0).then_inc(a_ln, 1)
                    exps(0)
                    exps(1)
                    act.wait_ge(a_rc, u + 1)
                    act.activation(two(wk[e])[0], Z01, ACT.Exp)
                    act.activation(two(wk[e])[1], Z23, ACT.Exp).then_inc(a_w, 1)
                    copy_turned(0)
                    exps(2)
                    copy_turned(1)
                    exps(3)
                    copy_turned(2)
                    copy_turned(3)
                act.wait_ge(a_osb, 2 * i + 2)
                act.activation(at(mixed, i), banks[:, 6, :], ACT.Copy).then_inc(a_oev, 1)
                act.wait_ge(a_odl, 2 * i + 2)
                act.activation(at(mixed, i + 4), banks[:, 7, :], ACT.Copy).then_inc(a_oev2, 1)

        def attention_vector(dve):
            dve.wait_ge(strip_in, 16)
            with dve.Fori(0, 4) as i:
                for e in range(2):
                    u = 2 * i + e

                    def add_bias(qb):
                        n = P * (qb + 1)
                        dve.wait_ge(a_s, 4 * u + qb + 1)
                        dve.wait_ge(a_t, 4 * u + qb + 1)
                        dve.tensor_tensor(ssb[qb % 2][:, 0:n], banks[:, 3 + qb % 2, 0:n],
                                          strip[:, bass.ds(u, 1), T - n:T].rearrange("p a n -> p (a n)"),
                                          ALU.add).then_inc(a_sadd, 1)
                        dve.wait_ge(a_sadd, 4 * u + qb + 3)
                        dve.tensor_reduce(small[:, NMX + qb:NMX + qb + 1], ssb[qb % 2][:, 0:n], AX.X, ALU.max,
                                          negate=True).then_inc(a_mx, 1)

                    def normalise(qb):
                        n = P * (qb + 1)
                        dve.wait_ge(a_exp, 4 * u + qb + 1)
                        dve.reciprocal(small[:, RL + qb:RL + qb + 1],
                                       small[:, LSUM + qb:LSUM + qb + 1]).then_inc(a_rl, 1)
                        dve.wait_ge(a_rl, 4 * u + qb + 1)
                        dve.tensor_scalar(ssb[qb % 2][:, 0:n], ssb[qb % 2][:, 0:n],
                                          small[:, RL + qb:RL + qb + 1], None, ALU.mult).then_inc(a_p, 1)

                    add_bias(0)
                    dve.wait_ge(a_ln, u + 1)
                    dve.scalar_tensor_tensor(two(sp_[e])[0], Z01, 0.0, two(ab[e])[0], ALU.max, ALU.add)
                    dve.scalar_tensor_tensor(two(sp_[e])[1], Z23, 0.0, two(ab[e])[1], ALU.max,
                                             ALU.add).then_inc(a_spr, 1)
                    add_bias(1)
                    normalise(0)
                    normalise(1)
                    add_bias(2)
                    normalise(2)
                    add_bias(3)
                    normalise(3)

        i_row, f_row, cum, c_row, m_row, e_row = (work[0:HEADS, T * j:T * (j + 1)] for j in range(6))
        one_row = work[0:HEADS, 6 * T:7 * T]
        ccols = work[:, 5888:5920].rearrange("p (s h) -> p s h", h=HEADS)
        cbuf = [hf[:, j, :] for j in range(2)]
        ms_k = [xn[:, e, :] for e in range(2)]
        ms_v = [xn[:, 2 + e, :] for e in range(2)]
        num_sb = [xn[:, 4 + e, :] for e in range(2)]
        num_sq = [xn[:, 6 + e, :] for e in range(2)]
        pm = [sq_f[:, PACKED * e:PACKED * (e + 1)] for e in range(2)]
        dm = [hf_f[:, PACKED * e:PACKED * (e + 1)] for e in range(2)]
        dn = [work[:, 3584 + T * e:3584 + T * (e + 1)] for e in range(2)]
        fac = [work[:, 4608 + T * e:4608 + T * (e + 1)] for e in range(2)]
        ms_sel = [work[0:HEADS, 5632 + P * e:5632 + P * (e + 1)] for e in range(2)]
        ms_c = [work[:, 5920 + 4 * e:5924 + 4 * e] for e in range(2)]
        ms_g = [work[:, 5928 + e:5929 + e] for e in range(2)]

        def gates_tensor(pe):
            pe.wait_ge(strip_line, 48)
            for g in range(2):
                for k in range(KD):
                    last = pe.matmul(banks[0:HEADS, 4 + g, :], wg[:, 2 * HEADS * k + HEADS * g:
                                                                 2 * HEADS * k + HEADS * (g + 1)],
                                     xn[:, k, :], start=(k == 0), stop=(k == KD - 1))
            last.then_inc(g_pe, 1)

        def mlstm_tensor(pe):
            pe.wait_ge(g_rows, 1)
            for s in range(4):
                last = pe.transpose(banks[:, 6, HEADS * s:HEADS * (s + 1)], c_row[:, P * s:P * (s + 1)],
                                    ident[0:HEADS, 0:HEADS])
            last.then_inc(g_pe, 1)
            pe.wait_ge(g_cols, 1)
            pe.wait_ge(tiles_freed, FREE0 + TILE["mlstm.o"] + 8)
            with pe.Fori(0, 4) as i:
                def first(e):
                    u = 2 * i + e
                    pe.wait_ge(m_staged, u + 1)
                    pe.wait_ge(m_dm, u + 1)
                    pe.matmul(banks[:, 3, :], ms_sel[e], m_row, start=True, stop=True).then_inc(m_mb, 1)
                    pe.wait_ge(m_p, u + 1)
                    for kb in range(4):
                        last = pe.matmul(zcols(kb), ms_k[e][:, P * kb:P * (kb + 1)],
                                         mqk[:, bass.ds(u, 1), P * kb:T].rearrange("p a n -> p (a n)"),
                                         start=(kb != 3), stop=True, skip_group_check=True)
                    last.then_inc(m_s, 1)
                    pe.wait_ge(m_ebc, u + 1)
                    pe.matmul(banks[:, 4, :], ms_sel[e], e_row, start=True, stop=True).then_inc(m_eb, 1)

                def second(e):
                    u = 2 * i + e
                    pe.wait_ge(m_pm, u + 1)
                    pe.wait_ge(m_sqr, u + 1)
                    pe.wait_ge(m_dn, u + 1)
                    for kb in range(4):
                        pe.matmul(banks[:, 5, P * kb:T], ms_v[e][:, P * kb:P * (kb + 1)], packed(pm[e], kb),
                                  start=(kb == 0), stop=(kb == 3), skip_group_check=True)
                    for kb in range(4):
                        last = pe.matmul(banks[:, 6, P * kb:T], ones, packed(pm[e], kb),
                                         start=(kb == 0), stop=(kb == 3), skip_group_check=True)
                    last.then_inc(m_nd, 1)
                    pe.wait_ge(m_sqr, u + 2)
                    pe.matmul(ps_n, ones, num_sq[e], start=True, stop=True).then_inc(m_ss, 1)

                first(0)
                first(1)
                second(0)
                pe.wait_ge(m_var, 2 * i + 1)
                second(1)
                pe.wait_ge(m_var, 2 * i + 2)
            pe.wait_ge(m_hid, 10)

        def mlstm_scalar(act):
            act.wait_ge(g_vec, 1)
            act.activation(e_row, f_row, ACT.Abs).then_inc(g_act, 1)
            act.wait_ge(g_act, 1)
            act.activation(e_row, e_row, ACT.Exp, scale=-1.0).then_inc(g_act, 1)
            act.wait_ge(g_act, 2)
            act.activation(e_row, e_row, ACT.Ln, bias=1.0).then_inc(g_act, 1)
            act.wait_ge(g_vec, 2)
            act.activation(e_row, e_row, ACT.Exp, scale=-1.0).then_inc(g_act, 1)
            with act.Fori(0, 4) as i:
                for m in range(4):
                    act.wait_ge(tiles_freed, FREE0 + TILE["mlstm.qk"] + 4 * i + m + 1)
                    act.activation(at(mqk, 4 * i + m), cbuf[m % 2], ACT.Silu).then_inc(conv_act, 1)
            for half in range(2):
                act.wait_ge(blocks_done, BLK["mlstm.v"] + 4 * half + 4)
                for t in range(4):
                    act.activation(mv[:, t, T * half:T * (half + 1)], lin[t], ACT.Copy).then_inc(tiles_freed, 1)
            evac(act, "mlstm.o", 8, lambda i, m: act.activation(at(sigo, 4 * i + m), lin[m], ACT.Sigmoid))
            with act.Fori(0, 4) as i:
                for e in range(2):
                    u = 2 * i + e
                    act.wait_ge(m_dm, u + 2)
                    act.activation(dm[e], dm[e], ACT.Exp, scale=-1.0).then_inc(m_d, 1)
                    act.wait_ge(m_eb, u + 1)
                    act.activation(dn[e], banks[:, 4, :], ACT.Copy).then_inc(m_ebc, 1)
                for e in range(2):
                    u = 2 * i + e
                    act.wait_ge(m_nd, u + 1)
                    act.activation(fac[e], banks[:, 6, :], ACT.Abs)
                    act.activation(num_sb[e], banks[:, 5, :], ACT.Copy)
                    act.activation(num_sq[e], banks[:, 5, :], ACT.Square).then_inc(m_sqr, 1)
                for e in range(2):
                    act.wait_ge(m_var, 2 * i + e + 1)
                    act.activation(fac[e], fac[e], ACT.Sqrt).then_inc(m_std, 1)

        def mlstm_vector(dve):
            tt, ts, stt = dve.tensor_tensor, dve.tensor_scalar, dve.scalar_tensor_tensor
            chain = [0]

            def link(ins):
                chain[0] += 1
                ins.then_inc(g_chain, 1)
                dve.wait_ge(g_chain, chain[0])

            dve.wait_ge(g_pe, 1)
            dve.memset(one_row, 1.0)
            link(ts(i_row, banks[0:HEADS, 4, :], vec[0:HEADS, VEC["b_i"]:VEC["b_i"] + 1], None, ALU.add))
            ts(f_row, banks[0:HEADS, 5, :], vec[0:HEADS, VEC["b_f"]:VEC["b_f"] + 1], None,
               ALU.add).then_inc(g_vec, 1)
            dve.wait_ge(g_act, 3)
            link(stt(f_row, f_row, 0.0, e_row, ALU.min, ALU.subtract))
            link(dve.tensor_tensor_scan(cum, one_row, f_row, 0.0, ALU.mult, ALU.add))
            tt(c_row, i_row, cum, ALU.subtract).then_inc(g_rows, 1)
            dve.wait_ge(g_rows, 1)
            link(dve.tensor_tensor_scan(m_row, c_row, c_row, 0.0, ALU.max, ALU.max))
            tt(e_row, cum, m_row, ALU.add).then_inc(g_vec, 1)
            dve.wait_ge(g_act, 4)
            ts(e_row, e_row, 3e38, None, ALU.min).then_inc(g_cols, 1)
            mc = VEC["mconv_w"]
            with dve.Fori(0, 4) as i:
                for m in range(4):
                    dve.wait_ge(blocks_done, BLK["mlstm.qk"] + 4 * i + m + 1)
                    dve.wait_ge(conv_act, 4 * i + m + 1)
                    c = cbuf[m % 2]
                    w = lambda tap: vec[:, bass.ds(16 * i + (mc + 4 * m + tap), 1)]
                    ts(c, lin[m], w(3), None, ALU.mult).then_inc(conv_v, 1)
                    for tap in (2, 1, 0):
                        d = 3 - tap
                        dve.wait_ge(conv_v, 12 * i + 3 * m + d)
                        last = stt(c[:, d:T], lin[m][:, 0:T - d], w(tap), c[:, d:T], ALU.mult, ALU.add)
                        last.then_inc(conv_v if tap > 0 else tiles_freed, 1)
            dve.wait_ge(g_pe, 2)
            dve.tensor_copy(work[:, 5888:5920], banks[:, 6, 0:32]).then_inc(g_cols, 1)
            dve.wait_ge(tiles_freed, FREE0 + TILE["mlstm.o"] + 8)
            with dve.Fori(0, 4) as i:
                for e in range(2):
                    u = 2 * i + e
                    dve.wait_ge(m_mb, u + 1)
                    dve.wait_ge(m_staged, u + 1)
                    for s in range(4):
                        last = ts(packed(dm[e], s), banks[:, 3, P * s:T], ms_c[e][:, s:s + 1], 0.0,
                                  ALU.subtract, ALU.max)
                    last.then_inc(m_dm, 1)
                    dve.wait_ge(m_d, u + 1)
                    dve.wait_ge(m_s, u + 1)
                    stt(two(pm[e])[0], Z01, P ** -0.5, two(dm[e])[0], ALU.mult, ALU.mult)
                    stt(two(pm[e])[1], Z23, P ** -0.5, two(dm[e])[1], ALU.mult, ALU.mult).then_inc(m_p, 1)
                for e in range(2):
                    u = 2 * i + e
                    dve.wait_ge(m_sqr, u + 2)
                    dve.wait_ge(m_ebc, u + 2)
                    tt(dn[e], fac[e], dn[e], ALU.max).then_inc(m_dn, 1)
                    dve.wait_ge(m_dn, u + 2)
                    stt(fac[e], dn[e], EPS_RMS, dn[e], ALU.mult, ALU.mult).then_inc(m_d2, 1)
                    dve.wait_ge(m_d2, u + 1)
                    dve.wait_ge(m_ss, u + 1)
                    stt(fac[e], ps_n, 1.0 / P, fac[e], ALU.mult, ALU.add).then_inc(m_var, 1)
                for e in range(2):
                    u = 2 * i + e
                    dve.wait_ge(m_std, u + 1)
                    dve.reciprocal(fac[e], fac[e]).then_inc(m_rec, 1)
                    dve.wait_ge(m_rec, u + 1)
                    stt(fac[e], num_sb[e], ms_g[e], fac[e], ALU.mult, ALU.mult).then_inc(m_fin, 1)
                    dve.wait_ge(m_fin, u + 1)
                    tt(at(hid, u), fac[e], at(sigo, u), ALU.mult).then_inc(m_hid, 1)

        def mlstm_pool(pool):
            pool.wait_ge(tiles_freed, FREE0 + TILE["mlstm.o"] + 8)
            pool.wait_ge(g_cols, 2)
            with pool.Fori(0, 4) as i:
                for e in range(2):
                    u = 2 * i + e
                    pool.wait_ge(m_hid, u + 1)
                    pool.tensor_copy(ms_k[e], at(mqk, u + 8))
                    pool.tensor_copy(ms_v[e].rearrange("p (a n) -> p a n", a=4), mv[:, :, bass.ds(P * u, P)])
                    pool.tensor_copy(ms_sel[e], ident[0:HEADS, bass.ds(u, 1)].to_broadcast([HEADS, P]))
                    pool.tensor_copy(ms_c[e].unsqueeze(2), ccols[:, :, bass.ds(u, 1)])
                    pool.tensor_copy(ms_g[e], vec[:, bass.ds(u + VEC["head_g"], 1)]).then_inc(m_staged, 1)
                for e in range(2):
                    pool.wait_ge(m_p, 2 * i + e + 2)
                    pool.sem_inc(pool_turn, 1)
                    for kb in range(4):
                        d = pm[e][:, OFF[kb]:OFF[kb] + P]
                        last = pool.affine_select(out=d, in_=d, pattern=[[1, P]], compare_op=ALU.is_ge,
                                                  fill=0.0, base=0, channel_multiplier=-1)
                    last.then_inc(m_pm, 1)

        iota_t = xn[:, 0, :]
        tmp_t = rstd[:, :]

        def tables_pool(pool):
            pool.wait_ge(blocks_done, BLK["ffn3.dn"])
            pool.iota(iota_t, [[1, T]], base=0, channel_multiplier=0,
                      allow_small_or_imprecise_dtypes=True).then_inc(iota_ready, 1)

        def tables_vector(dve):
            ts, tt = dve.tensor_scalar, dve.tensor_tensor
            dve.wait_ge(iota_ready, 1)
            with dve.Fori(0, NSTATE_T) as i:
                si = at(sinT, i)
                ts(si, iota_t, small[:, bass.ds(i + PHI, 1)], None, ALU.mult).then_inc(tab_v, 1)
                dve.wait_ge(tab_v, 4 * i + 1)
                ts(tmp_t, si, ROUND, ROUND, ALU.add, ALU.subtract).then_inc(tab_v, 1)
                dve.wait_ge(tab_v, 4 * i + 2)
                tt(si, si, tmp_t, ALU.subtract).then_inc(tab_v, 1)
                dve.wait_ge(tab_v, 4 * i + 3)
                ts(tmp_t, si, 0.25, None, ALU.is_gt).then_inc(tab_v, 1)
                dve.wait_ge(tab_v, 4 * i + 4)
                dve.scalar_tensor_tensor(at(cosT, i), si, 0.25, tmp_t, ALU.add, ALU.subtract).then_inc(tab, 1)

        def tables_scalar(act, i, m):
            for j in range(2):
                n = 8 * i + 2 * m + j
                act.wait_ge(tab, n + 1)
                act.activation(at(sinT, n), at(sinT, n), ACT.Sin, scale=TWO_PI)
                act.activation(at(cosT, n), at(cosT, n), ACT.Sin, scale=TWO_PI).then_inc(tab_act, 1)

        b_raw = [hf_f[:, 0:512], hf_f[:, 512:1024]]
        c_raw = [hf_f[:, 1024:1536], hf_f[:, 1536:2048]]
        pw = hf_f[:, 2048:2560]
        c_neg = [hf_f[:, 2560:3072], hf_f[:, 3072:3584]]
        bt = [region(8192, 512), region(8704, 512)]
        ucs = region(9216, 512)
        bts = [region(9728, 128), region(9856, 128)]
        cs = [region(9984 + 128 * j, 128) for j in range(3)]
        br = [sq[:, e, :] for e in range(2)]
        bi = [sq[:, 2 + e, :] for e in range(2)]
        r1, r2, r3 = (sq[:, 4 + j, :] for j in range(3))
        pr = [sq[:, 7, :], hf_f[:, 3584:4096], hf_f[:, 0:512], hf_f[:, 512:1024]]
        yr, yi = rstd[:, :], std[:, :]
        bb = [sq_f[:, 0:512], sq_f[:, 512:1024]]
        bb_t = [sq_f[:, 1024:1536], sq_f[:, 1536:2048]]

        def even_tensor(pe):
            pe.wait_ge(e_bb, 8)
            for q in range(2):
                for c in range(4):
                    last = pe.transpose(banks[:, 4 + q, P * c:P * (c + 1)], bb[q][:, P * c:P * (c + 1)], ident)
            last.then_inc(e_t, 1)

            def drive(c, j):
                n = 4 * c + j
                rows = slice(32 * j, 32 * j + 32)
                if j == 0:
                    pe.wait_ge(s_staged, c + 1)
                pe.wait_ge(s_buc, n + 1)
                for q in range(2):
                    last = pe.matmul(banks[:, 4 + q, :], bts[q][rows, :], ucs[rows, :], start=True, stop=True)
                last.then_inc(s_bu, 1)

            def read_out(c, j):
                n = 4 * c + j
                rows = slice(32 * j, 32 * j + 32)
                if j == 0:
                    pe.wait_ge(s_ych, c + 1)
                pe.wait_ge(s_pr, n + 2)
                for q, k in enumerate((0, 1, 2, 2)):
                    last = pe.matmul(banks[rows, 6, :], cs[k][:, rows], pr[q], start=(q == 0), stop=(q == 3),
                                     skip_group_check=True)
                last.then_inc(s_ym, 1)

            def gate_chunk(c, j):
                pe.wait_ge(w_loaded[j], 16 * (BLK["even.in"] // 4 + 3) + 16 * c)
                pe.wait_ge(tiles_freed, FREE0 + TILE["even.in"] + 8 + 4 * c + j - 3)
                block_mm_of(pe, lin[j], j, xn)

            for lo, gates in ((0, True), (2, False)):
                with pe.Fori(lo, lo + 2) as c:
                    drive(c, 0)
                    for j in range(4):
                        if j < 3:
                            drive(c, j + 1)
                        if gates:
                            gate_chunk(c, j)
                        read_out(c, j)
            pe.wait_ge(s_ych, 5)
            pe.wait_ge(tiles_freed, FREE0 + TILE["even.glu"])
            for b in range(4):
                wait_w(pe, "even.glu", b, 0)
                if b >= 2:
                    pe.wait_ge(tiles_freed, FREE0 + TILE["even.glu"] + 2 * b - 2)
                for vg in range(2):
                    for k in range(4):
                        last = pe.matmul(lin[2 * (b % 2) + vg], ring[:, b, (4 * vg + k) * P:(4 * vg + k + 1) * P],
                                         uin[:, k, :], start=(k == 0), stop=(k == 3))
                last.then_inc(blocks_done, 1)
            for g in range(4):
                pe.wait_ge(e_pool, g + 1)
                if g >= 2:
                    pe.wait_ge(e_y, g - 1)
                pe.matmul(banks[:, 4 + g % 2, :], pw[:, P * g:P * (g + 1)], r_pool[g], start=True,
                          stop=True).then_inc(e_pm, 1)
            pe.wait_ge(e_y, 8)
            pe.wait_ge(tiles_freed, FREE0 + TILE["even.out"])

        r_pool = [sq[:, 4 + g, :] for g in range(4)]
        sig_e = [sq[:, 2 + g, :] for g in range(2)]

        def even_scalar(act):
            with act.Fori(0, 2) as i:
                for m in range(4):
                    act.wait_ge(blocks_done, BLK["even.in"] + 4 * i + m + 1)
                    act.activation(at(uin, 4 * i + m), lin[m], ACT.Copy).then_inc(tiles_freed, 1)
            act.wait_ge(e_t, 1)
            for q in range(2):
                act.activation(bt[q], banks[:, 4 + q, :], ACT.Copy).then_inc(e_btc, 1)

            def take(c, j):
                n = 4 * c + j
                act.wait_ge(s_bu, n + 1)
                act.wait_ge(s_rot, n + 1)
                act.activation(br[j % 2], banks[:, 4, :], ACT.Copy)
                act.activation(bi[j % 2], banks[:, 5, :], ACT.Copy).then_inc(s_buc, 1)

            for lo, gates in ((0, True), (2, False)):
                with act.Fori(lo, lo + 2) as c:
                    take(c, 0)
                    for j in range(4):
                        if j < 3:
                            take(c, j + 1)
                        if gates:
                            act.wait_ge(blocks_done, BLK["even.in"] + 8 + 4 * c + j + 1)
                            act.activation(at(zin, 4 * c + j), lin[j], ACT.Silu).then_inc(tiles_freed, 1)
            for b in range(4):
                act.wait_ge(blocks_done, BLK["even.glu"] + b + 1)
                if b >= 2:
                    act.wait_ge(tiles_freed, FREE0 + TILE["even.glu"] + 2 * b - 2)
                act.activation(sig_e[b % 2], lin[2 * (b % 2) + 1], ACT.Sigmoid).then_inc(e_sig, 1)

        def residual(dve, name):
            with dve.Fori(0, 2) as i:
                for m in range(4):
                    dve.wait_ge(blocks_done, BLK[name] + 4 * i + m + 1)
                    dve.tensor_tensor(at(x, 4 * i + m), at(x, 4 * i + m), lin[m], ALU.add).then_inc(tiles_freed, 1)

        def even_vector(dve):
            ts, tt, stt = dve.tensor_scalar, dve.tensor_tensor, dve.scalar_tensor_tensor
            dve.wait_ge(e_loaded, 80)

            def v3(ap):
                return ap.rearrange("p (a n) -> p a n", a=NSTATE_T)

            def gain(c):
                return col(c).unsqueeze(2).to_broadcast([P, NSTATE_T, 32])

            tt(v3(bb[0]), v3(b_raw[0]), gain(KRE), ALU.mult).then_inc(e_bb, 1)
            tt(v3(bb_t[0]), v3(b_raw[1]), gain(KIM), ALU.mult).then_inc(e_bb, 1)
            tt(v3(bb[1]), v3(b_raw[1]), gain(KRE), ALU.mult).then_inc(e_bb, 1)
            tt(v3(bb_t[1]), v3(b_raw[0]), gain(KIM), ALU.mult).then_inc(e_bb, 1)
            dve.wait_ge(e_bb, 4)
            tt(bb[0], bb[0], bb_t[0], ALU.subtract).then_inc(e_bb, 1)
            tt(bb[1], bb[1], bb_t[1], ALU.add).then_inc(e_bb, 1)
            for q in range(2):
                ts(c_neg[q], c_raw[q], -1.0, None, ALU.mult).then_inc(e_bb, 1)
            dve.wait_ge(tab_act, NSTATE_T)
            with dve.Fori(0, 4) as c:
                for j in range(4):
                    n = 4 * c + j
                    co, si = at(cosT, n), at(sinT, n)
                    dve.wait_ge(s_buc, n + 2)
                    tt(r1, co, br[j % 2], ALU.mult)
                    tt(r2, si, bi[j % 2], ALU.mult).then_inc(s_v, 1)
                    tt(r3, co, bi[j % 2], ALU.mult)
                    dve.wait_ge(s_v, 3 * n + 1)
                    tt(r1, r1, r2, ALU.add).then_inc(s_v, 1)
                    dve.wait_ge(s_v, 3 * n + 2)
                    tt(r2, si, br[j % 2], ALU.mult).then_inc(s_rot, 1)
                    dve.wait_ge(s_pr, n + 1)
                    decay = small[:, bass.ds(n + R_, 1)].to_broadcast([P, T])
                    dve.tensor_tensor_scan(yr, decay, r1, 0.0, ALU.mult, ALU.add)
                    dve.wait_ge(s_rot, n + 3)
                    tt(r3, r3, r2, ALU.subtract).then_inc(s_v, 1)
                    dve.wait_ge(s_v, 3 * n + 3)
                    dve.tensor_tensor_scan(yi, decay, r3, 0.0, ALU.mult, ALU.add).then_inc(s_y, 1)
                    dve.wait_ge(s_y, n + 1)
                dve.wait_ge(s_ym, 4 * c + 5)
                stt(at(uin, c), at(uin, c), vec[:, bass.ds(c + VEC["ssm_d"], 1)], banks[:, 6, :],
                    ALU.mult, ALU.add).then_inc(s_ych, 1)
            dve.wait_ge(s_ych, 5)
            steps = 0
            for g, w in enumerate((2, 4, 8, 16)):
                u_g = uin[:, 4 + g, :]
                src, k = u_g, 1
                while k < w:
                    dst = sq[:, steps % 2, :]
                    dve.tensor_copy(dst[:, 0:k], src[:, 0:k])
                    tt(dst[:, k:T], src[:, k:T], src[:, 0:T - k], ALU.add).then_inc(e_win, 1)
                    steps += 1
                    dve.wait_ge(e_win, steps)
                    src, k = dst, 2 * k
                o = C_INV + 16 * g
                stt(r_pool[g][:, 16:T], src[:, 16:T], 1.0 / w, u_g[:, 16:T], ALU.mult, ALU.subtract)
                tt(r_pool[g][:, 0:16], src[:, 0:16], cst_sb[:, o:o + 16], ALU.mult).then_inc(e_w2, 1)
                dve.wait_ge(e_w2, g + 1)
                tt(r_pool[g][:, 0:16], r_pool[g][:, 0:16], u_g[:, 0:16], ALU.subtract).then_inc(e_pool, 1)
            for b in range(4):
                dve.wait_ge(e_sig, b + 1)
                tt(sig_e[b % 2], lin[2 * (b % 2)], sig_e[b % 2], ALU.mult).then_inc(e_val, 1)
                dve.wait_ge(e_val, b + 1)
                tt(xn[:, 4 + b, :], sig_e[b % 2], zin[:, 4 + b, :], ALU.mult).then_inc(tiles_freed, 2)
            for g in range(4):
                dve.wait_ge(e_pm, g + 1)
                c0 = VEC["pool_scale"] + g
                stt(xn[:, g, :], banks[:, 4 + g % 2, :], vec[:, c0:c0 + 1], zin[:, g, :],
                    ALU.mult, ALU.mult).then_inc(e_y, 1)
            dve.wait_ge(tiles_freed, FREE0 + TILE["even.glu"] + 8)
            dve.memset(small[:, 0:1], 0.0).then_inc(e_y, 4)
            residual(dve, "even.out")

        def even_pool(pool):
            pool.wait_ge(x_ready, 48)
            for dst, src in ((b_raw[0], bst[0]), (b_raw[1], bst[1]), (c_raw[0], cst[0]), (c_raw[1], cst[1]),
                             (pw, pool_w)):
                pool.dma_start(dst, src).then_inc(e_loaded, 16)
            pool.wait_ge(e_btc, 2)
            pool.wait_ge(e_bb, 8)
            pool.wait_ge(tiles_freed, FREE0 + TILE["even.in"] + 8)
            tt = pool.tensor_tensor
            with pool.Fori(0, 4) as c:
                pool.tensor_copy(ucs, at(uin, c))
                for dst, src in ((bts[0], bt[0]), (bts[1], bt[1]), (cs[0], c_raw[0]), (cs[1], c_neg[0]),
                                 (cs[2], c_neg[1])):
                    last = pool.tensor_copy(dst, src[:, bass.ds(P * c, P)])
                last.then_inc(s_staged, 1)
                for j in range(4):
                    n = 4 * c + j
                    co, si = at(cosT, n), at(sinT, n)
                    pool.wait_ge(s_y, n + 1)
                    pool.wait_ge(s_ym, n + 1)
                    tt(pr[0], co, yr, ALU.mult)
                    tt(pr[1], si, yi, ALU.mult)
                    tt(pr[2], si, yr, ALU.mult)
                    tt(pr[3], co, yi, ALU.mult).then_inc(s_pr, 1)
                pool.wait_ge(s_ym, 4 * c + 5)

        sig_o = [hf[:, s, :] for s in range(2)]
        mean = hf[:, 2, :]

        def odd_tensor(pe):
            for c in range(KD):
                pe.wait_ge(o_conv, c + 1)
                last = pe.matmul(banks[:, 6, :], ones, cc[:, c, :], start=(c == 0), stop=(c == KD - 1))
            last.then_inc(o_sum, 1)
            sumsq_of(pe, squares, 64)
            pe.wait_ge(o_y, KD)
            pe.wait_ge(tiles_freed, FREE0 + TILE["odd.out"])

        def odd_scalar(act):
            with act.Fori(0, 4) as i:
                for s in range(2):
                    act.wait_ge(blocks_done, BLK["odd.in"] + 4 * i + 2 * s + 2)
                    act.wait_ge(tiles_freed, FREE0 + TILE["odd.in"] + 4 * i + 2 * s - 2)
                    act.activation(sig_o[s], lin[2 * s + 1], ACT.Sigmoid).then_inc(o_sig, 1)
            with act.Fori(0, 2) as i:
                for m in range(4):
                    act.wait_ge(blocks_done, BLK["odd.in"] + 16 + 4 * i + m + 1)
                    act.activation(at(zz, 4 * i + m), lin[m], ACT.Silu).then_inc(tiles_freed, 1)
            act.wait_ge(sumsq_ready, norm_no["odd.ln"])
            for c in range(KD):
                act.wait_ge(o_cen, c + 2)
                act.activation(sq[:, c, :], cc[:, c, :], ACT.Square).then_inc(squares, 1)
            n = norm_no["odd.ln"]
            act.wait_ge(var_ready, n + 1)
            act.activation(std[:, :], std[:, :], ACT.Sqrt).then_inc(std_ready, 1)
            for c in range(KD):
                act.wait_ge(o_n, c + 1)
                b = VEC["ln_b"] + c
                act.activation(cc[:, c, :], cc[:, c, :], ACT.Silu, bias=vec[:, b:b + 1]).then_inc(o_s, 1)

        def odd_vector(dve):
            ts, tt, stt = dve.tensor_scalar, dve.tensor_tensor, dve.scalar_tensor_tensor
            dve.memset(gpad[:, :, 0:PAD], 0.0).then_inc(o_v, 1)
            dve.wait_ge(o_v, 1)
            cw = VEC["conv_w"]
            with dve.Fori(0, 4) as i:
                for s in range(2):
                    dve.wait_ge(o_sig, 2 * i + s + 1)
                    g = gpad[:, bass.ds(2 * i + s, 1), :].rearrange("p a n -> p (a n)")
                    c = at(cc, 2 * i + s)
                    tt(g[:, PAD:PAD + T], lin[2 * s], sig_o[s], ALU.mult).then_inc(tiles_freed, 2)
                    dve.wait_ge(tiles_freed, FREE0 + TILE["odd.in"] + 4 * i + 2 * s + 2)

                    def w(tap):
                        return vec[:, bass.ds(2 * CONV_K * i + (cw + CONV_K * s + tap), 1)]

                    ts(c, g[:, 0:T], w(0), vec[:, bass.ds(2 * i + (VEC["conv_b"] + s), 1)], ALU.mult,
                       ALU.add).then_inc(o_v, 1)
                    for tap in range(1, CONV_K):
                        dve.wait_ge(o_v, (CONV_K - 1) * (2 * i + s) + tap + 1)
                        last = stt(c, g[:, tap:tap + T], w(tap), c, ALU.mult, ALU.add)
                        last.then_inc(o_v if tap < CONV_K - 1 else o_conv, 1)
            dve.wait_ge(o_sum, 1)
            ts(mean, banks[:, 6, :], 1.0 / D, None, ALU.mult).then_inc(o_cen, 1)
            dve.wait_ge(o_cen, 1)
            for c in range(KD):
                tt(cc[:, c, :], cc[:, c, :], mean, ALU.subtract).then_inc(o_cen, 1)
            norm_stats(dve, "odd.ln", eps=EPS_LN)
            for c in range(KD):
                b = VEC["ln_g"] + c
                stt(cc[:, c, :], cc[:, c, :], vec[:, b:b + 1], rstd[:, :], ALU.mult, ALU.mult).then_inc(o_n, 1)
            for c in range(KD):
                dve.wait_ge(o_s, c + 1)
                tt(yo[:, c, :], cc[:, c, :], zz[:, c, :], ALU.mult).then_inc(o_y, 1)
            residual(dve, "odd.out")

        def norm_stats(dve, name, scale=1.0 / D, eps=EPS_RMS):
            n = norm_no[name]
            dve.wait_ge(sumsq_ready, n + 1)
            dve.tensor_scalar(std[:, :], ps_n, scale, eps, ALU.mult, ALU.add).then_inc(var_ready, 1)
            dve.wait_ge(std_ready, n + 1)
            dve.reciprocal(rstd[:, :], std[:, :]).then_inc(rstd_ready, 1)
            dve.wait_ge(rstd_ready, n + 1)

        def sumsq_of(pe, signal, base):
            for c in range(KD):
                pe.wait_ge(signal, base + c + 1)
                last = pe.matmul(ps_n, ones, sq[:, c, :], start=(c == 0), stop=(c == KD - 1))
            last.then_inc(sumsq_ready, 1)

        def block_mm_of(pe, dst, slot, rhs, n=KD, k0=0, total=KD):
            for k in range(n):
                last = pe.matmul(dst, ring[:, slot, k * P:(k + 1) * P], rhs[:, k0 + k, :],
                                 start=(k0 + k == 0), stop=(k0 + k == total - 1))
            last.then_inc(blocks_done, 1)

        block = ctx.enter_context(nc.Block())

        @block.sync
        def _(sp):
            for dst, src in ((cst_sb[:, :], consts), (vec[:, :], vecs), (x, x_in)):
                sp.dma_start(dst, src).then_inc(in_loaded, 16)
            for name, n, stream in SECTIONS:
                src = {"w8": w8, "wd": wd}[stream]
                cols = KD * P if stream == "w8" else SLOT
                b0, r0 = BLK[name], SRC[name]

                def load(i, s):
                    sp.dma_start(ring[:, s, 0:cols],
                                 src[bass.ds(r0 + 4 * i + s, 1)].rearrange("b p n -> (b p) n")
                                 ).then_inc(w_loaded[s], 16)

                first = 0
                if b0 == 0:
                    for s in range(RING):
                        load(0, s)
                    first = 1
                with sp.Fori(first, n // RING) as i:
                    for s in range(RING):
                        sp.wait_ge(blocks_done, b0 + 4 * i + s - 3)
                        load(i, s)
            sp.wait_ge(xn_ready, 8 * len(PRE))
            sp.dma_start(out, xn).then_inc(out_done, 16)
            sp.wait_ge(out_done, 16)

        @block.tensor
        def _(pe):
            def sumsq(name, signal, base):
                sumsq_of(pe, signal, base)

            def block_mm(dst, slot, rhs, **span):
                block_mm_of(pe, dst, slot, rhs, **span)

            def linear(name, rhs, lo=0, hi=None, per=4):
                hi = NBLK[name] if hi is None else hi
                with pe.Fori(lo // 4, hi // 4) as i:
                    for s in range(4):
                        pe.wait_ge(w_loaded[s], 16 * (BLK[name] // 4 + 1) + 16 * i)
                        pe.wait_ge(tiles_freed, FREE0 + TILE[name] + 4 * i + s - 3)
                        block_mm(lin[s], s, rhs)

            def token_major(name, n_half):
                for half in range(n_half):
                    pe.wait_ge(tiles_freed, FREE0 + TILE[name] + 4 * half)
                    for b in range(4):
                        wait_w(pe, name, 4 * half + b, 0)
                        for kk in range(2):
                            k = 2 * b + kk
                            for t in range(4):
                                last = pe.matmul(lin[t], xn[:, k, t * P:(t + 1) * P],
                                                 ring[:, b, kk * T:(kk + 1) * T], start=(k == 0), stop=(k == 7))
                        last.then_inc(blocks_done, 1)

            def ffn(name):
                pe.wait_ge(xn_ready, 8 * (pre_no[name + ".pre"] + 1))
                gu, dn = name + ".gu", name + ".dn"
                pe.wait_ge(tiles_freed, FREE0 + TILE[gu])
                with pe.Fori(0, KF // 2) as i:
                    for s in range(4):
                        pe.wait_ge(w_loaded[s], 16 * (BLK[gu] // 4 + 1) + 16 * i)
                        if s % 2 == 0:
                            pe.wait_ge(tiles_freed, FREE0 + TILE[gu] + 4 * i + s - 2)
                        block_mm(lin[s], s, xn)
                pe.wait_ge(tiles_freed, FREE0 + TILE[dn])
                with pe.Fori(0, 2) as i:
                    for m in range(4):
                        pe.wait_ge(tiles_freed, FREE0 + TILE[dn] + 4 * i + m - 3)
                        for half in range(2):
                            b = 2 * m + half
                            wait = 16 * (BLK[dn] // 4 + b // 4 + 1)
                            pe.wait_ge(w_loaded[b % 4], wait + 32 * i)
                            block_mm(lin[m], b % 4, h, n=HALF_KF, k0=HALF_KF * half, total=KF)
                sumsq(name + ".post", tiles_freed, FREE0 + TILE[dn])

            pe.wait_ge(in_loaded, 48)
            prep_tensor(pe)
            sumsq("ffn0.pre", squares, 0)
            ffn("ffn0")
            sumsq("attn.pre", squares, 8)
            pe.wait_ge(xn_ready, 8 * (pre_no["attn.pre"] + 1))
            pe.wait_ge(tiles_freed, FREE0 + TILE["attn.qk"])
            linear("attn.qk", xn)
            token_major("attn.v", 2)
            attention_tensor(pe)
            pe.wait_ge(tiles_freed, FREE0 + TILE["attn.out"])
            linear("attn.out", mixed)
            sumsq("attn.post", tiles_freed, FREE0 + TILE["attn.out"])
            sumsq("ffn1.pre", squares, 16)
            ffn("ffn1")
            sumsq("ffn2.pre", squares, 24)
            ffn("ffn2")
            sumsq("mlstm.pre", squares, 32)
            pe.wait_ge(xn_ready, 8 * (pre_no["mlstm.pre"] + 1))
            pe.wait_ge(tiles_freed, FREE0 + TILE["mlstm.qk"])
            gates_tensor(pe)
            linear("mlstm.qk", xn)
            token_major("mlstm.v", 2)
            pe.wait_ge(tiles_freed, FREE0 + TILE["mlstm.o"])
            linear("mlstm.o", xn)
            mlstm_tensor(pe)
            linear("mlstm.out", hid)
            sumsq("mlstm.post", tiles_freed, FREE0 + TILE["mlstm.out"])
            sumsq("ffn3.pre", squares, 40)
            ffn("ffn3")
            sumsq("even.pre", squares, 48)
            pe.wait_ge(xn_ready, 8 * (pre_no["even.pre"] + 1))
            pe.wait_ge(tiles_freed, FREE0 + TILE["even.in"])
            linear("even.in", xn, 0, 8)
            even_tensor(pe)
            linear("even.out", xn)
            sumsq("odd.pre", squares, 56)
            pe.wait_ge(xn_ready, 8 * (pre_no["odd.pre"] + 1))
            pe.wait_ge(tiles_freed, FREE0 + TILE["odd.in"])
            linear("odd.in", xn, 0, 16)
            pe.wait_ge(tiles_freed, FREE0 + TILE["odd.in"] + 16)
            linear("odd.in", xn, 16, 24)
            odd_tensor(pe)
            linear("odd.out", yo)
            sumsq("final", squares, 72)

        @block.scalar
        def _(act):
            def square_x(u):
                if u > 0:
                    act.wait_ge(sumsq_ready, norm_no[PRE[u]])
                for c in range(KD):
                    if u == 0:
                        act.wait_ge(in_loaded, 48)
                    elif u <= 6:
                        act.wait_ge(x_ready, 8 * (u - 1) + c + 1)
                    else:
                        act.wait_ge(tiles_freed, FREE0 + TILE[("even.out", "odd.out")[u - 7]] + c + 1)
                    act.activation(sq[:, c, :], x[:, c, :], ACT.Square).then_inc(squares, 1)

            def take_std(name):
                n = norm_no[name]
                act.wait_ge(var_ready, n + 1)
                act.activation(std[:, :], std[:, :], ACT.Sqrt).then_inc(std_ready, 1)

            def branch_out(name, blocks_per, idx):
                n = norm_no[name.split(".")[0] + ".post"]
                act.wait_ge(sumsq_ready, n)
                rounds = 2
                with act.Fori(0, rounds) as i:
                    for m in range(4):
                        act.wait_ge(blocks_done, BLK[name] + blocks_per * (4 * i + m + 1))
                        act.activation(at(hf, 4 * i + m), lin[m], ACT.Copy)
                        act.activation(at(sq, 4 * i + m), lin[m], ACT.Square).then_inc(tiles_freed, 1)
                        if name == "ffn3.dn":
                            tables_scalar(act, i, m)

            def ffn(name, idx):
                take_std(name + ".pre")
                gu = name + ".gu"
                with act.Fori(0, KF // 2) as i:
                    for s in range(2):
                        act.wait_ge(blocks_done, BLK[gu] + 4 * i + 2 * s + 1)
                        act.wait_ge(tiles_freed, FREE0 + TILE[gu] + 4 * i + 2 * s - 2)
                        act.activation(sg[:, s, :], lin[2 * s], ACT.Silu).then_inc(gate_act, 1)
                branch_out(name + ".dn", 2, idx)
                take_std(name + ".post")

            prep_scalar(act)
            square_x(0)
            ffn("ffn0", 0)
            square_x(1)
            take_std("attn.pre")
            attention_in_scalar(act)
            attention_scalar(act)
            branch_out("attn.out", 1, 0)
            take_std("attn.post")
            square_x(2)
            ffn("ffn1", 1)
            square_x(3)
            ffn("ffn2", 2)
            square_x(4)
            take_std("mlstm.pre")
            mlstm_scalar(act)
            branch_out("mlstm.out", 1, 0)
            take_std("mlstm.post")
            square_x(5)
            ffn("ffn3", 3)
            square_x(6)
            take_std("even.pre")
            even_scalar(act)
            square_x(7)
            take_std("odd.pre")
            odd_scalar(act)
            square_x(8)
            take_std("final")

        @block.vector
        def _(dve):
            def pre(name):
                norm_stats(dve, name)
                for c in range(KD):
                    dve.scalar_tensor_tensor(xn[:, c, :], x[:, c, :], g_of(name, c), rstd[:, :],
                                             ALU.mult, ALU.mult).then_inc(xn_ready, 1)

            def post(name):
                norm_stats(dve, name + ".post")
                for c in range(KD):
                    dve.scalar_tensor_tensor(hf[:, c, :], hf[:, c, :], g_of(name + ".post", c), rstd[:, :],
                                             ALU.mult, ALU.mult).then_inc(scaled, 1)

            def ffn(name, idx):
                pre(name + ".pre")
                gu, dn = name + ".gu", name + ".dn"
                with dve.Fori(0, KF // 2) as i:
                    for s in range(2):
                        dve.wait_ge(blocks_done, BLK[gu] + 4 * i + 2 * s + 2)
                        dve.wait_ge(gate_act, KF * idx + 2 * i + s + 1)
                        dve.tensor_tensor(at(h, 2 * i + s), sg[:, s, :], lin[2 * s + 1],
                                          ALU.mult).then_inc(tiles_freed, 2)
                if name == "ffn3":
                    tables_vector(dve)
                post(name)

            prep_vector(dve)
            ffn("ffn0", 0)
            pre("attn.pre")
            attention_in_vector(dve)
            attention_vector(dve)
            post("attn")
            ffn("ffn1", 1)
            ffn("ffn2", 2)
            pre("mlstm.pre")
            mlstm_vector(dve)
            post("mlstm")
            ffn("ffn3", 3)
            pre("even.pre")
            even_vector(dve)
            pre("odd.pre")
            odd_vector(dve)
            pre("final")

        @block.gpsimd
        def _(pool):
            def update(u, n_before):
                for c in range(KD):
                    pool.wait_ge(scaled, 8 * n_before + c + 1)
                    pool.tensor_tensor(x[:, c, :], x[:, c, :], hf[:, c, :], ALU.add).then_inc(x_ready, 1)

            update(0, 0)
            attention_pool(pool)
            update(1, 1)
            update(2, 2)
            update(3, 3)
            mlstm_pool(pool)
            update(4, 4)
            tables_pool(pool)
            update(5, 5)
            even_pool(pool)



def bucket(d):
    if d < 16:
        return d
    return min(16 + int(np.log(d / 16) / np.log(2048 / 16) * 16), NB_BUCKETS - 1)


def bias_columns():
    table = np.zeros((NB_BUCKETS + 1, STRIP_W), np.float32)
    for c in range(STRIP_W):
        d = T - 1 - c
        count = 0 if d < 0 else (d <= 128) + (d % 4 == 0) + (d % 16 == 0)
        if d >= 0:
            table[bucket(d), c] = 1.0
        table[NB_BUCKETS, c] = np.log(count) if count else NEG
    return table


def constants():
    c = np.zeros((P, NCONST), np.float32)
    c[:, C_ID:C_ID + P] = np.eye(P)
    c[:, C_TRI:C_TRI + P] = -np.tril(np.ones((P, P)))
    c[:, C_ONE:C_ONE + P] = 1.0
    for g, w in enumerate((2, 4, 8, 16)):
        c[:, C_INV + 16 * g:C_INV + 16 * (g + 1)] = 1.0 / np.minimum(np.arange(1, 17), w)
    return c


def kernel(**inputs):
    import concourse.bacc as _bacc
    from concourse.bass_utils import run_bass_kernel_spmd as _run

    a = {k: np.asarray(v) for k, v in inputs.items()}

    def blocks(w):
        k, n = w.shape
        return w.reshape(k // P, P, n // P, P).transpose(2, 1, 0, 3).reshape(n // P, P, k)

    def row_blocks(w):
        return w.reshape(4, 2, P, T).transpose(0, 2, 1, 3).reshape(4, P, 2 * T)

    def pairs(u, v):
        return np.stack([u, v], 1).reshape(-1, *u.shape[1:])

    def ffn(layer, j):
        w8.append(pairs(blocks(a["ffn_w_gate"][layer, j]), blocks(a["ffn_w_up"][layer, j])))
        wd.append(blocks(a["ffn_w_down"][layer, j]).reshape(KD, P, 2, SLOT).transpose(0, 2, 1, 3)
                  .reshape(2 * KD, P, SLOT))

    w8, wd = [], []
    ffn(0, 0)
    w = a["attn_w_in"][0]
    for lo in (0, 512, 1536, 2048):
        w8.append(blocks(w[:, lo:lo + 512]))
    w8.append(row_blocks(w[:, 1024:1536]))
    w8.append(row_blocks(w[:, 2560:3072]))
    w8.append(blocks(a["attn_w_out"][0]))
    ffn(0, 1)
    ffn(1, 0)
    w = a["mlstm_w_in"][0]
    w8.append(blocks(w[:, 0:2048]))
    w8.append(row_blocks(w[:, 2048:2560]))
    w8.append(row_blocks(w[:, 2560:3072]))
    w8.append(blocks(w[:, 3072:4096]))
    w_gates = w[:, 4096:].reshape(KD, P, 16).transpose(1, 0, 2).reshape(P, 128)
    w8.append(blocks(a["mlstm_w_out"][0]))
    ffn(1, 1)
    w = a["even_w_in_2"][0]
    w8.append(blocks(w[:, 512:1024]))
    w8.append(blocks(w[:, 0:512]))
    w8.append(blocks(w[:, 1024:2048]))
    w = blocks(a["ssm_w_glu_2"][0])
    w8.append(np.concatenate([w[0:4], w[4:8]], 2))
    w8.append(blocks(a["even_w_out_2"][0]))
    w = blocks(a["odd_w_in_2"][0])
    w8.append(pairs(w[0:8], w[8:16]))
    w8.append(w[16:24])
    w8.append(blocks(a["odd_w_out_2"][0]))
    w8 = np.concatenate(w8)
    wd = np.concatenate(wd)

    def per_channel(v):
        return v.reshape(-1, P).T

    def per_state(v):
        return np.broadcast_to(v.reshape(32, -1), (32, 64)).reshape(NSTATE_T, P).T

    vecs = np.zeros((P, NVEC), np.float32)
    for name, v in (("norm_g", per_channel(a["norm_g"])), ("even_norm", per_channel(a["even_norm_2"])),
                    ("odd_norm", per_channel(a["odd_norm_2"])), ("final_norm", per_channel(a["final_norm_2"])),
                    ("pool_scale", per_channel(a["pool_scale_2"])), ("ssm_d", per_channel(a["ssm_d_2"])),
                    ("conv_b", per_channel(a["conv_b_2"])), ("ln_g", per_channel(a["conv_ln_g_2"])),
                    ("ln_b", per_channel(a["conv_ln_b_2"])), ("head_g", per_channel(a["mlstm_head_g"])),
                    ("conv_w", a["conv_w_2"][0].reshape(CONV_K, KD, P).transpose(2, 1, 0).reshape(P, -1)),
                    ("mconv_w", a["mlstm_conv_w"][0].reshape(MCONV_K, 16, P).transpose(2, 1, 0).reshape(P, -1)),
                    ("log_dt", per_state(a["ssm_log_dt_2"][0][:, None])), ("a_re", per_state(a["ssm_a_re_2"][0])),
                    ("a_im", per_state(a["ssm_a_im_2"][0]))):
        vecs[:, VEC[name]:VEC[name] + v.shape[1]] = v
    vecs[0:HEADS, VEC["b_i"]] = a["mlstm_b_gates"][0, 0:HEADS]
    vecs[0:HEADS, VEC["b_f"]] = a["mlstm_b_gates"][0, HEADS:]

    def diagonal(v):
        out = np.zeros((NSTATE_T, 2, 64, 2, 16), np.float32)
        v = v.reshape(NSTATE_T, 2, 64, 16)
        out[:, 0, :, 0] = v[:, 0]
        out[:, 1, :, 1] = v[:, 1]
        return out.reshape(NSTATE_T, P, 32).transpose(1, 0, 2).reshape(P, 512)

    bst = np.stack([diagonal(a["ssm_b_re_2"][0]), diagonal(a["ssm_b_im_2"][0])])
    cst = np.stack([diagonal(a["ssm_c_re_2"][0].transpose(0, 2, 1)),
                    diagonal(a["ssm_c_im_2"][0].transpose(0, 2, 1))])
    arrays = {
        "x_in": a["x"].reshape(T, KD, P).transpose(2, 1, 0), "w8": w8, "wd": wd, "vecs": vecs,
        "consts": constants(), "rel_bias": a["rel_bias"], "buckets": bias_columns(), "w_gates": w_gates,
        "pool_w": a["pool_w_2"][0].transpose(1, 0, 2).reshape(P, 512), "bst": bst, "cst": cst,
    }
    arrays = {k: np.ascontiguousarray(v) for k, v in arrays.items()}
    nc = _bacc.Bacc("TRN2", target_bir_lowering=False, num_devices=1)
    args = [nc.dram_tensor(k, v.shape, F32, kind="ExternalInput").ap() for k, v in arrays.items()]
    scratch = nc.dram_tensor("scratch", (P, HEADS * STRIP_W), F32, kind="Internal").ap()
    out = nc.dram_tensor("out", (P, KD, T), F32, kind="ExternalOutput").ap()
    build(nc, *args, scratch, out)
    r = _run(nc, [arrays], core_ids=[0])
    return r.results[0]["out"].transpose(2, 1, 0).reshape(1, T, D)
```

```python
from contextlib import ExitStack

import numpy as np
import concourse.bass as bass
from concourse import mybir

F32 = mybir.dt.float32
F32R = mybir.dt.float32r
ALU = mybir.AluOpType
ACT = mybir.ActivationFunctionType
AX = mybir.AxisListType

P = 128
T = 512
D = 1024
KD = D // P
FF = 2816
KF = FF // P
DN = (8, 8, 6)
NB_BUCKETS = 32
RING = 4
SLOT = KD * P
HEADS = 8
EPS_RMS = 1e-6
EPS_LN = 1e-5
CONV_K = 31
PAD = CONV_K - 1
MCONV_K = 4
NSTATE_T = 16
TWO_PI = 6.2831845
ROUND = 12582912.0
NEG = -1e30
STRIP_W = 5 * P
OFF = (0, 512, 896, 1152)
PACKED = 1280

SECTIONS = []
for _name, _kinds in (("ffn0", "f"), ("attn", "a"), ("ffn1", "f"), ("ffn2", "f"), ("mlstm", "m"),
                      ("ffn3", "f"), ("even", "e"), ("odd", "o")):
    SECTIONS += {
        "f": [(_name + ".gu", 2 * KF), (_name + ".dn", len(DN) * KD)],
        "a": [("attn.qk", 16), ("attn.v", 8), ("attn.out", 8)],
        "m": [("mlstm.qk", 16), ("mlstm.v", 8), ("mlstm.o", 8), ("mlstm.out", 8)],
        "e": [("even.in", 16), ("even.glu", 4), ("even.out", 8)],
        "o": [("odd.in", 24), ("odd.out", 8)],
    }[_kinds]

BLK, TILE = {}, {}
_b = _t = 0
for _name, _n in SECTIONS:
    BLK[_name], TILE[_name] = _b, _t
    _b += _n
    _t += KD if _name.endswith(("dn", "glu")) else _n
NBLK = dict(SECTIONS)
BLOCKS = _b

SPLIT = {}
_c = 0
for _name, _n in (("ffn0", 8), ("attn", 8), ("ffn1", 8), ("ffn2", 8), ("mlstm", 8), ("ffn3", 8), ("even", 8),
                  ("glu", 4), ("even.y", 8), ("odd", 8), ("odd.y", 8), ("final", 8)):
    SPLIT[_name] = _c
    _c += _n

NORMS = ["ffn0.pre", "ffn0.post", "attn.pre", "attn.post", "ffn1.pre", "ffn1.post", "ffn2.pre", "ffn2.post",
         "mlstm.pre", "mlstm.post", "ffn3.pre", "ffn3.post", "even.pre", "odd.pre", "odd.ln", "final"]
PRE = [n for n in NORMS if not n.endswith(("post", "ln"))]
UPD = ["ffn0", "attn", "ffn1", "ffn2", "mlstm", "ffn3", "even", "odd"]

VEC = {}
_c = 0
for _name, _n in (("norm_g", 96), ("even_norm", 8), ("odd_norm", 8), ("final_norm", 8), ("pool_scale", 4),
                  ("ssm_d", 4), ("conv_b", 8), ("ln_g", 8), ("ln_b", 8), ("head_g", 8), ("conv_w", 31 * 8),
                  ("mconv_w", 4 * 16), ("log_dt", 16), ("a_re", 16), ("a_im", 16), ("b_i", 1), ("b_f", 1)):
    VEC[_name] = _c
    _c += _n
NVEC = _c
GCOL = {"ffn0.pre": 0, "ffn0.post": 8, "attn.pre": 16, "attn.post": 24, "ffn1.pre": 32, "ffn1.post": 40,
        "ffn2.pre": 48, "ffn2.post": 56, "mlstm.pre": 64, "mlstm.post": 72, "ffn3.pre": 80, "ffn3.post": 88,
        "even.pre": VEC["even_norm"], "odd.pre": VEC["odd_norm"], "final": VEC["final_norm"]}

C_ID, C_TRI, C_ONE, C_INV = 0, P, 2 * P, 3 * P
NCONST = C_INV + 64


def skewed(scratch):
    w = HEADS * STRIP_W
    return bass.AP(tensor=scratch.tensor, offset=scratch.offset + P - 1,
                   ap=[[w - 1, P], [STRIP_W, HEADS], [1, T]])


def build(nc, x_in, weights, vecs, consts, rel_bias, buckets, w_gates, pool_w, bst, cst, scratch, out):
    ctx = ExitStack()
    with ctx:
        def sem(name):
            return ctx.enter_context(nc.semaphore(name))

        def chunks(ap, n=None):
            return ap.rearrange("p (a n) -> p a n", n=n or T)

        def at(buf, i):
            return buf[:, bass.ds(i, 1), :].rearrange("p a n -> p (a n)")

        base = (nc.sbuf_base + 31) // 32 * 32
        X, XH, XL, HF, MIX = 0, 4096, 8192, 12288, 16384
        RAW = MIX + 24576
        WH, WL = RAW + RING * SLOT, RAW + RING * SLOT + 2 * SLOT
        REST = WL + 2 * SLOT

        def place(name, col, cols, dtype=F32):
            return nc.alloc_sbuf_tensor_at(name + "_sb", [P, cols], dtype, offset=base + 4 * col)

        x = chunks(place("x", X, 4096)[:, :])
        xh = chunks(place("xh", XH, 4096, F32R)[:, :])
        xl = chunks(place("xl", XL, 4096, F32R)[:, :])
        xs = place("xs", XH, 8192)
        xh_f = xh.bitcast(F32)
        sq = chunks(xs[:, 0:4096])
        hf_f = place("hf", HF, 4096)
        hf = chunks(hf_f[:, :])
        mix = place("mix", MIX, 24576)
        hh = chunks(place("hh", MIX, KF * T, F32R)[:, :])
        hl = chunks(place("hl", MIX + KF * T, KF * T, F32R)[:, :])
        raw = chunks(place("raw", RAW, RING * SLOT)[:, :], SLOT)
        wh = chunks(place("wh", WH, 2 * SLOT, F32R)[:, :], SLOT)
        wl = chunks(place("wl", WL, 2 * SLOT, F32R)[:, :], SLOT)
        wh_f, hh_f = wh.bitcast(F32), hh.bitcast(F32)
        rest = [REST]

        def sb(name, cols):
            rest[0] += cols
            return place(name, rest[0] - cols, cols)

        cst_sb = sb("consts", NCONST)
        vec = sb("vecs", (NVEC + 7) // 8 * 8)[:, 0:NVEC]
        rstd = sb("rstd", T)
        std = sb("std", T)
        small = sb("small", 320)
        wg = sb("wg", KD * 2 * HEADS)
        pw = sb("pw", T)
        sg = hf[:, 0:2, :]
        ht = hf[:, 2:4, :]
        ident = cst_sb[:, C_ID:C_ID + P]
        negtri = cst_sb[:, C_TRI:C_TRI + P]
        ones = cst_sb[:, C_ONE:C_ONE + P]
        negones = sb("negones", P)

        def region(start, n):
            return mix[:, start:start + n]

        mix_sq = chunks(region(0, KD * T))
        qkT = chunks(region(0, 16 * T))
        va = chunks(region(8192, 4 * T))
        vd = chunks(region(10240, 4 * T))
        strip = chunks(region(12288, HEADS * T))
        mqk = chunks(region(0, 16 * T))
        mv = region(8192, 4 * D).rearrange("p (a n) -> p a n", n=D)
        sigo = chunks(region(12288, KD * T))
        uin = chunks(region(0, 8 * T))
        zin = chunks(region(4096, 8 * T))
        cosT = chunks(region(8192, 16 * T))
        sinT = chunks(region(16384, 16 * T))
        gpad = region(0, KD * (T + PAD)).rearrange("p (a n) -> p a n", n=T + PAD)
        cc = chunks(region(4608, KD * T))
        zz = chunks(region(8704, KD * T))

        banks = ctx.enter_context(nc.psum_tensor("banks", [P, 8, T], F32))
        lin = [banks[:, i, :] for i in range(4)]
        ps_n = banks[:, 7, :]

        w_loaded = [sem(f"w_loaded{i}") for i in range(RING)]
        blocks_done = sem("blocks_done")
        tiles_freed = sem("tiles_freed")
        gate_act = sem("gate_act")
        in_loaded = sem("in_loaded")
        squares = sem("squares")
        sumsq_ready = sem("sumsq_ready")
        var_ready = sem("var_ready")
        std_ready = sem("std_ready")
        rstd_ready = sem("rstd_ready")
        xn_ready = sem("xn_ready")
        scaled = sem("scaled")
        x_ready = sem("x_ready")
        prep = sem("prep")
        prep_act = sem("prep_act")
        prep_pe = sem("prep_pe")
        prep_pool = sem("prep_pool")
        strip_line = sem("strip_line")
        strip_out = sem("strip_out")
        strip_in = sem("strip_in")
        out_done = sem("out_done")
        pool_turn = sem("pool_turn")
        tab = sem("tab")
        w_hi = sem("w_hi")
        w_split = sem("w_split")
        t_ready = sem("t_ready")
        hi_ready = sem("hi_ready")
        h_hi = sem("h_hi")
        h_lo = sem("h_lo")
        a_oh = sem("a_oh")
        m_hh = sem("m_hh")
        m_out = sem("m_out")
        tab_act = sem("tab_act")
        a_abs = sem("a_abs")
        a_ex = sem("a_ex")
        a_exp = sem("a_exp")
        a_ln = sem("a_ln")
        a_mx = sem("a_mx")
        a_odl = sem("a_odl")
        a_oev = sem("a_oev")
        a_oev2 = sem("a_oev2")
        a_osb = sem("a_osb")
        a_p = sem("a_p")
        a_rc = sem("a_rc")
        a_rl = sem("a_rl")
        a_s = sem("a_s")
        a_sadd = sem("a_sadd")
        a_sp = sem("a_sp")
        a_spr = sem("a_spr")
        a_staged = sem("a_staged")
        a_t = sem("a_t")
        a_tc = sem("a_tc")
        a_w = sem("a_w")
        a_wm = sem("a_wm")
        a_z = sem("a_z")
        conv_act = sem("conv_act")
        conv_v = sem("conv_v")
        e_bb = sem("e_bb")
        e_btc = sem("e_btc")
        e_loaded = sem("e_loaded")
        e_pm = sem("e_pm")
        e_pool = sem("e_pool")
        e_sig = sem("e_sig")
        e_t = sem("e_t")
        e_val = sem("e_val")
        e_w2 = sem("e_w2")
        e_win = sem("e_win")
        e_y = sem("e_y")
        g_act = sem("g_act")
        g_chain = sem("g_chain")
        g_cols = sem("g_cols")
        g_pe = sem("g_pe")
        g_rows = sem("g_rows")
        g_vec = sem("g_vec")
        halved = sem("halved")
        iota_ready = sem("iota_ready")
        m_d = sem("m_d")
        m_d2 = sem("m_d2")
        m_dm = sem("m_dm")
        m_dn = sem("m_dn")
        m_eb = sem("m_eb")
        m_ebc = sem("m_ebc")
        m_fin = sem("m_fin")
        m_hid = sem("m_hid")
        m_mb = sem("m_mb")
        m_nd = sem("m_nd")
        m_p = sem("m_p")
        m_pm = sem("m_pm")
        m_rec = sem("m_rec")
        m_s = sem("m_s")
        m_sqr = sem("m_sqr")
        m_ss = sem("m_ss")
        m_staged = sem("m_staged")
        m_std = sem("m_std")
        m_var = sem("m_var")
        o_cen = sem("o_cen")
        o_conv = sem("o_conv")
        o_n = sem("o_n")
        o_s = sem("o_s")
        o_sig = sem("o_sig")
        o_sum = sem("o_sum")
        o_v = sem("o_v")
        o_y = sem("o_y")
        prep_exp = sem("prep_exp")
        prep_x = sem("prep_x")
        s_bu = sem("s_bu")
        s_buc = sem("s_buc")
        s_pr = sem("s_pr")
        s_rot = sem("s_rot")
        s_staged = sem("s_staged")
        s_v = sem("s_v")
        s_y = sem("s_y")
        s_ych = sem("s_ych")
        s_ym = sem("s_ym")
        tab_v = sem("tab_v")

        norm_no = {n: i for i, n in enumerate(NORMS)}
        pre_no = {n: i for i, n in enumerate(PRE)}
        FREE0 = 4

        def g_of(name, c):
            col = GCOL[name] + c
            return vec[:, col:col + 1]

        def high_part(act, name, s, k=0):
            if isinstance(k, int) and BLK[name] + k + s + 2 >= BLOCKS:
                return
            act.wait_ge(w_loaded[(s + 2) % RING], 16 * (BLK[name] // RING + (s + 2) // RING + 1) + 4 * k)
            act.wait_ge(blocks_done, BLK[name] + s + 1 + k)
            act.activation(wh[:, s % 2, :], raw[:, (s + 2) % RING, :], ACT.Copy).then_inc(w_hi, 1)

        def low_part(pool, name, s, k=0):
            if isinstance(k, int) and BLK[name] + k + s + 2 >= BLOCKS:
                return
            pool.wait_ge(w_hi, BLK[name] + s + 3 + k)
            pool.tensor_tensor(wl[:, s % 2, :], raw[:, (s + 2) % RING, :], wh_f[:, s % 2, :],
                               ALU.subtract).then_inc(w_split, 1)

        def first_parts(eng, low):
            for s in range(2):
                if low:
                    eng.wait_ge(w_hi, s + 1)
                    eng.tensor_tensor(wl[:, s, :], raw[:, s, :], wh_f[:, s, :], ALU.subtract).then_inc(w_split, 1)
                else:
                    eng.wait_ge(w_loaded[s], 16)
                    eng.activation(wh[:, s, :], raw[:, s, :], ACT.Copy).then_inc(w_hi, 1)

        def low_parts(pool, name):
            with pool.Fori(0, NBLK[name] // 4) as i:
                for s in range(4):
                    low_part(pool, name, s, 4 * i)

        def split_high(act, key, n=KD, src=None, order=None):
            for j in range(n):
                c = order[j] if order else j
                act.wait_ge(t_ready, SPLIT[key] + j + 1)
                act.activation(xh[:, c, :], (hf if src is None else src)[:, c, :], ACT.Copy).then_inc(hi_ready, 1)

        def split_low(pool, key, n=KD, src=None, order=None):
            for j in range(n):
                c = order[j] if order else j
                pool.wait_ge(hi_ready, SPLIT[key] + j + 1)
                pool.tensor_tensor(xl[:, c, :], (hf if src is None else src)[:, c, :], xh_f[:, c, :],
                                   ALU.subtract).then_inc(xn_ready, 1)

        DT, XR, PHI, R_, EM, SER, MASK, E1, SI, S2, CO, NR, NI, KRE, KIM, DEN, TA, TB = range(0, 288, 16)
        NMX, LSUM, RL = 288, 296, 304

        def col(c, n=16):
            return small[:, c:c + n]

        lines = region(0, HEADS * STRIP_W).rearrange("p (h n) -> p h n", n=STRIP_W)
        bk = region(5120, 640)
        rb = region(5760, 8)
        rb8 = region(5768, 1024).rearrange("p (h n) -> p h n", n=P)
        LB = NB_BUCKETS + 1

        def prep_tensor(pe):
            pe.wait_ge(prep, 2)
            for hh in range(HEADS):
                if hh >= 2:
                    pe.wait_ge(prep_act, hh - 1)
                for half in range(2):
                    last = pe.matmul(banks[:, 2 * (hh % 2) + half, 0:320], rb8[0:LB, hh, :],
                                     bk[0:LB, 320 * half:320 * half + 320], start=True, stop=True)
                last.then_inc(prep_pe, 1)

        def prep_scalar(act):
            act.dma_start(bk[0:LB, :], buckets).then_inc(strip_line, 16)
            act.dma_start(rb[0:NB_BUCKETS, :], rel_bias).then_inc(strip_line, 16)
            act.dma_start(wg[:, :], w_gates).then_inc(strip_line, 16)
            act.dma_start(pw[:, :], pool_w).then_inc(strip_line, 16)
            first_parts(act, False)
            act.wait_ge(in_loaded, 48)
            act.activation(std[:, 0:1], vec[:, 0:1], ACT.Copy).then_inc(a_w, 1)
            act.activation(std[:, 1:2], vec[:, 0:1], ACT.Copy).then_inc(a_oev, 1)
            act.activation(std[:, 2:3], vec[:, 0:1], ACT.Copy).then_inc(a_oev2, 1)
            act.activation(std[:, 3:4], vec[:, 0:1], ACT.Copy).then_inc(a_tc, 1)
            act.activation(std[:, 4:5], vec[:, 0:1], ACT.Copy).then_inc(m_ebc, 1)
            act.activation(std[:, 5:6], vec[:, 0:1], ACT.Copy).then_inc(m_sqr, 1)
            act.activation(std[:, 6:7], vec[:, 0:1], ACT.Copy).then_inc(s_buc, 1)
            for hh in range(HEADS):
                act.wait_ge(prep_pe, hh + 1)
                act.activation(lines[:, hh, :].rearrange("p (a n) -> p a n", a=2),
                               banks[:, 2 * (hh % 2):2 * (hh % 2) + 2, 0:320], ACT.Copy).then_inc(prep_act, 1)
            act.wait_ge(prep_act, HEADS)
            act.dma_start(scratch, region(0, HEADS * STRIP_W)).then_inc(strip_out, 16)
            act.activation(col(DT), vec[:, VEC["log_dt"]:VEC["log_dt"] + 16], ACT.Exp).then_inc(prep_exp, 1)
            act.wait_ge(strip_out, 16)
            act.wait_ge(prep_x, 1)
            act.activation(col(E1), col(XR), ACT.Exp).then_inc(prep_exp, 1)
            act.activation(col(SI), col(PHI), ACT.Sin, scale=TWO_PI).then_inc(prep_exp, 1)
            act.activation(col(S2), col(PHI), ACT.Sin, scale=TWO_PI / 2).then_inc(prep_exp, 1)

        def prep_vector(dve):
            chain = [0]

            def link(ins):
                chain[0] += 1
                ins.then_inc(prep, 1)
                dve.wait_ge(prep, chain[0])

            link(dve.memset(rb[NB_BUCKETS:LB, :], 1.0))
            dve.wait_ge(strip_line, 64)
            link(dve.tensor_copy(rb8[0:LB, :, :], rb[0:LB, :].unsqueeze(2).to_broadcast([LB, HEADS, P])))
            dve.memset(negones[:, :], -1.0).then_inc(tiles_freed, FREE0)
            dve.memset(rstd[:, 0:1], 0.0).then_inc(a_sadd, 2)
            dve.memset(rstd[:, 1:2], 0.0).then_inc(m_dm, 1)
            dve.memset(rstd[:, 2:3], 0.0).then_inc(m_p, 1)
            dve.memset(rstd[:, 3:4], 0.0).then_inc(m_dn, 1)
            dve.memset(rstd[:, 4:5], 0.0).then_inc(m_hid, 2)
            dve.memset(rstd[:, 5:6], 0.0).then_inc(s_rot, 2)
            dve.memset(rstd[:, 7:8], 0.0).then_inc(a_t, 2)
            dve.memset(rstd[:, 8:9], 0.0).then_inc(conv_act, 2)
            dve.memset(rstd[:, 11:12], 0.0).then_inc(h_lo, 2)
            dve.memset(rstd[:, 9:10], 0.0).then_inc(s_pr, 1)
            dve.memset(rstd[:, 10:11], 0.0).then_inc(s_ym, 1)
            dve.memset(rstd[:, 6:7], 0.0).then_inc(s_ych, 1)
            dve.wait_ge(in_loaded, 48)
            for c in (8, 40, 56, 88):
                dve.tensor_scalar(vec[:, c:c + 8], vec[:, c:c + 8], 0.5, None, ALU.mult).then_inc(halved, 1)
            dve.wait_ge(halved, 4)
            are, aim = (vec[:, VEC[n]:VEC[n] + 16] for n in ("a_re", "a_im"))
            tt = dve.tensor_tensor
            ts = dve.tensor_scalar
            dve.wait_ge(prep_exp, 1)
            link(tt(col(XR), are, col(DT), ALU.mult))
            link(tt(col(TA), aim, col(DT), ALU.mult))
            link(ts(col(TA), col(TA), float(1 / (2 * np.pi)), None, ALU.mult))
            link(ts(col(TB), col(TA), ROUND, ROUND, ALU.add, ALU.subtract))
            tt(col(PHI), col(TA), col(TB), ALU.subtract).then_inc(prep_x, 1)
            dve.wait_ge(prep_x, 1)
            link(ts(col(TA), col(XR), 0.5, -0.5, ALU.min, ALU.max))
            link(dve.memset(col(SER), 1.0))
            for k in range(9, 1, -1):
                link(dve.scalar_tensor_tensor(col(SER), col(SER), 1.0 / k, col(TA), ALU.mult, ALU.mult))
                link(ts(col(SER), col(SER), 1.0, None, ALU.add))
            link(tt(col(SER), col(SER), col(TA), ALU.mult))
            link(tt(col(MASK), col(TA), col(XR), ALU.is_equal))
            link(tt(col(SER), col(SER), col(MASK), ALU.mult))
            link(ts(col(MASK), col(MASK), -1.0, 1.0, ALU.mult, ALU.add))
            dve.wait_ge(prep_exp, 4)
            link(ts(col(E1), col(E1), -1.0, None, ALU.add))
            link(tt(col(E1), col(E1), col(MASK), ALU.mult))
            link(tt(col(EM), col(E1), col(SER), ALU.add))
            link(ts(col(R_), col(EM), 1.0, None, ALU.add))
            link(tt(col(S2), col(S2), col(S2), ALU.mult))
            link(ts(col(CO), col(S2), -2.0, 1.0, ALU.mult, ALU.add))
            link(tt(col(NR), col(EM), col(CO), ALU.mult))
            link(dve.scalar_tensor_tensor(col(NR), col(S2), -2.0, col(NR), ALU.mult, ALU.add))
            link(tt(col(NI), col(R_), col(SI), ALU.mult))
            link(tt(col(DEN), are, are, ALU.mult))
            link(tt(col(TA), aim, aim, ALU.mult))
            link(tt(col(DEN), col(DEN), col(TA), ALU.add))
            link(dve.reciprocal(col(DEN), col(DEN)))
            link(tt(col(TA), col(NR), are, ALU.mult))
            link(tt(col(TB), col(NI), aim, ALU.mult))
            link(tt(col(TA), col(TA), col(TB), ALU.add))
            link(tt(col(KRE), col(TA), col(DEN), ALU.mult))
            link(tt(col(TA), col(NI), are, ALU.mult))
            link(tt(col(TB), col(NR), aim, ALU.mult))
            link(tt(col(TA), col(TA), col(TB), ALU.subtract))
            link(tt(col(KIM), col(TA), col(DEN), ALU.mult))

        def evac(eng, name, n, fn):
            with eng.Fori(0, n // 4) as i:
                for m in range(4):
                    high_part(eng, name, m, 4 * i)
                    fn(i, m).then_inc(tiles_freed, 1)

        qp, kp, vp, qdp, kdp, vdp = (region(16384 + T * j, T) for j in range(6))
        wk = [region(19456 + PACKED * e, PACKED) for e in range(2)]
        ab = [region(22016 + PACKED * e, PACKED) for e in range(2)]
        sp_ = ab
        pT = [hf_f[:, PACKED * e:PACKED * (e + 1)] for e in range(2)]
        ssb = [hf_f[:, 2560 + T * j:3072 + T * j] for j in range(2)]
        Z01 = banks[:, 0, :]
        Z23 = banks[:, 1:3, 0:384]

        def zcols(kb):
            return (banks[:, 0, :], banks[:, 1, 0:384], banks[:, 2, 0:256], banks[:, 2, 256:384])[kb]

        def packed(buf, kb):
            return buf[:, OFF[kb]:OFF[kb] + T - P * kb]

        def two(buf):
            return buf[:, 0:T], buf[:, T:PACKED].rearrange("p (a n) -> p a n", a=2)

        def attention_in_scalar(act):
            for c in range(16):
                high_part(act, "attn.qk", c % 4, c - c % 4)
                act.activation(qkT[:, c, :], lin[c % 4], ACT.Copy,
                               scale=0.125 if c // 4 % 2 == 0 else 1.0).then_inc(tiles_freed, 1)
            for half, dst in enumerate((va, vd)):
                for s in range(4):
                    high_part(act, "attn.v", s, 4 * half)
                for t in range(4):
                    act.activation(dst[:, t, :], lin[t], ACT.Copy).then_inc(tiles_freed, 1)

        def attention_in_vector(dve):
            pass

        def attention_pool(pool):
            low_parts(pool, "attn.qk")
            low_parts(pool, "attn.v")
            pool.wait_ge(tiles_freed, FREE0 + TILE["attn.v"] + 8)
            with pool.Fori(0, 4) as i:
                pool.tensor_copy(qp, at(qkT, i))
                pool.tensor_copy(kp, at(qkT, i + 4))
                pool.tensor_copy(vp.rearrange("p (a n) -> p a n", a=4), va[:, :, bass.ds(P * i, P)])
                pool.tensor_copy(qdp, at(qkT, i + 8))
                pool.tensor_copy(kdp, at(qkT, i + 12))
                pool.tensor_copy(vdp.rearrange("p (a n) -> p a n", a=4),
                                 vd[:, :, bass.ds(P * i, P)]).then_inc(a_staged, 1)
                for e in range(2):
                    for buf, signal, done, base in ((sp_[e], a_spr, a_sp, 1), (wk[e], a_w, a_wm, 2)):
                        pool.wait_ge(signal, 2 * i + e + base)
                        pool.sem_inc(pool_turn, 1)
                        for kb in range(4):
                            d = buf[:, OFF[kb]:OFF[kb] + P]
                            last = pool.affine_select(out=d, in_=d, pattern=[[1, P]], compare_op=ALU.is_gt,
                                                      fill=0.0, base=0, channel_multiplier=-1)
                        last.then_inc(done, 1)
                pool.wait_ge(a_odl, 2 * i + 2)

        def attention_tensor(pe):
            with pe.Fori(0, 4) as i:
                for e in range(2):
                    rows = slice(64 * e, 64 * e + 64)
                    u = 2 * i + e

                    def scores(qb):
                        pe.wait_ge(a_sadd, 4 * u + qb + 1)
                        pe.matmul(banks[:, 3 + qb % 2, 0:P * (qb + 1)], qdp[rows, P * qb:P * (qb + 1)],
                                  kdp[rows, 0:P * (qb + 1)], start=True, stop=True).then_inc(a_s, 1)

                    def turn(qb):
                        pe.wait_ge(a_p, 4 * u + qb + 1)
                        pe.wait_ge(a_tc, 4 * u + qb + 1)
                        for kb in range(qb + 1):
                            last = pe.transpose(banks[:, 5, P * kb:P * (kb + 1)],
                                                ssb[qb % 2][:, P * kb:P * (kb + 1)], ident)
                        last.then_inc(a_t, 1)

                    if e == 0:
                        pe.wait_ge(a_staged, i + 1)
                    pe.wait_ge(a_w, u + 1)
                    for kb in range(4):
                        last = pe.matmul(zcols(kb), kp[rows, P * kb:P * (kb + 1)], qp[rows, P * kb:T],
                                         start=(kb != 3), stop=False, skip_group_check=True)
                    last.then_inc(a_z, 1)
                    scores(0)
                    scores(1)
                    pe.wait_ge(a_sp, u + 1)
                    for kb in range(4):
                        dst = zcols(kb)
                        last = pe.matmul(dst, negtri, packed(sp_[e], kb), start=False, stop=(kb == 3),
                                         skip_group_check=True)
                        for later in range(kb + 1, 4):
                            last = pe.matmul(dst[:, P * (later - kb):T - P * kb], negones[:, :],
                                             packed(sp_[e], later), start=False, stop=True,
                                             skip_group_check=True)
                    last.then_inc(a_rc, 1)
                    turn(0)
                    scores(2)
                    turn(1)
                    scores(3)
                    turn(2)
                    pe.wait_ge(a_wm, u + 1)
                    if e == 0:
                        pe.wait_ge(a_oev, i + 1)
                    for kb in range(4):
                        last = pe.matmul(banks[rows, 6, P * kb:T], vp[:, P * kb + 64 * e:P * kb + 64 * e + 64],
                                         packed(wk[e], kb), start=(kb == 0), stop=(kb == 3),
                                         skip_group_check=True)
                    last.then_inc(a_osb, 1)
                    turn(3)
                    pe.wait_ge(a_tc, 4 * u + 5)
                    if e == 0:
                        pe.wait_ge(a_oev2, i + 1)
                    for kb in range(4):
                        last = pe.matmul(banks[rows, 7, P * kb:T], vdp[:, P * kb + 64 * e:P * kb + 64 * e + 64],
                                         packed(pT[e], kb), start=(kb == 0), stop=(kb == 3),
                                         skip_group_check=True)
                    last.then_inc(a_odl, 1)
            pe.wait_ge(a_oev, 5)
            pe.wait_ge(a_oev2, 5)

        def attention_scalar(act):
            with act.Fori(0, 4) as i:
                for e in range(2):
                    u = 2 * i + e

                    def exps(qb):
                        act.wait_ge(a_mx, 4 * u + qb + 1)
                        n = P * (qb + 1)
                        act.activation(ssb[qb % 2][:, 0:n], ssb[qb % 2][:, 0:n], ACT.Exp,
                                       bias=small[:, NMX + qb:NMX + qb + 1],
                                       accum_out=small[:, LSUM + qb:LSUM + qb + 1]).then_inc(a_exp, 1)

                    def copy_turned(qb):
                        act.wait_ge(a_t, 4 * u + qb + 3)
                        for kb in range(qb + 1):
                            o = OFF[kb] + P * (qb - kb)
                            last = act.activation(pT[e][:, o:o + P], banks[:, 5, P * kb:P * (kb + 1)], ACT.Copy)
                        last.then_inc(a_tc, 1)

                    act.wait_ge(a_z, u + 1)
                    act.activation(two(ab[e])[0], Z01, ACT.Abs)
                    act.activation(two(ab[e])[1], Z23, ACT.Abs).then_inc(a_abs, 1)
                    act.wait_ge(a_abs, u + 1)
                    act.activation(ab[e], ab[e], ACT.Exp, scale=-1.0).then_inc(a_ex, 1)
                    act.wait_ge(a_ex, u + 1)
                    act.activation(ab[e], ab[e], ACT.Ln, bias=1.0).then_inc(a_ln, 1)
                    exps(0)
                    exps(1)
                    act.wait_ge(a_rc, u + 1)
                    act.activation(two(wk[e])[0], Z01, ACT.Exp)
                    act.activation(two(wk[e])[1], Z23, ACT.Exp).then_inc(a_w, 1)
                    copy_turned(0)
                    exps(2)
                    copy_turned(1)
                    exps(3)
                    copy_turned(2)
                    copy_turned(3)
                act.wait_ge(a_osb, 2 * i + 2)
                act.activation(at(xh, i), banks[:, 6, :], ACT.Copy).then_inc(a_oh, 1)
                act.wait_ge(a_odl, 2 * i + 2)
                act.activation(at(xh, i + 4), banks[:, 7, :], ACT.Copy).then_inc(a_oh, 1)

        def attention_vector(dve):
            dve.wait_ge(strip_in, 16)
            with dve.Fori(0, 4) as i:
                for e in range(2):
                    u = 2 * i + e

                    def add_bias(qb):
                        n = P * (qb + 1)
                        dve.wait_ge(a_s, 4 * u + qb + 1)
                        dve.wait_ge(a_t, 4 * u + qb + 1)
                        dve.tensor_tensor(ssb[qb % 2][:, 0:n], banks[:, 3 + qb % 2, 0:n],
                                          strip[:, bass.ds(u, 1), T - n:T].rearrange("p a n -> p (a n)"),
                                          ALU.add).then_inc(a_sadd, 1)
                        dve.wait_ge(a_sadd, 4 * u + qb + 3)
                        dve.tensor_reduce(small[:, NMX + qb:NMX + qb + 1], ssb[qb % 2][:, 0:n], AX.X, ALU.max,
                                          negate=True).then_inc(a_mx, 1)

                    def normalise(qb):
                        n = P * (qb + 1)
                        dve.wait_ge(a_exp, 4 * u + qb + 1)
                        dve.reciprocal(small[:, RL + qb:RL + qb + 1],
                                       small[:, LSUM + qb:LSUM + qb + 1]).then_inc(a_rl, 1)
                        dve.wait_ge(a_rl, 4 * u + qb + 1)
                        dve.tensor_scalar(ssb[qb % 2][:, 0:n], ssb[qb % 2][:, 0:n],
                                          small[:, RL + qb:RL + qb + 1], None, ALU.mult).then_inc(a_p, 1)

                    add_bias(0)
                    dve.wait_ge(a_ln, u + 1)
                    dve.scalar_tensor_tensor(two(sp_[e])[0], Z01, 0.0, two(ab[e])[0], ALU.max, ALU.add)
                    dve.scalar_tensor_tensor(two(sp_[e])[1], Z23, 0.0, two(ab[e])[1], ALU.max,
                                             ALU.add).then_inc(a_spr, 1)
                    add_bias(1)
                    normalise(0)
                    normalise(1)
                    add_bias(2)
                    normalise(2)
                    add_bias(3)
                    normalise(3)
                for o, ev in ((0, a_oev), (1, a_oev2)):
                    dve.wait_ge(a_oh, 2 * i + o + 1)
                    dve.tensor_tensor(at(xl, i + 4 * o), banks[:, 6 + o, :], at(xh_f, i + 4 * o),
                                      ALU.subtract).then_inc(ev, 1)

        c_row, m_row, e_row = (region(16384 + T * j, T)[0:HEADS, :] for j in range(3))
        i_row, f_row, cum, one_row = (region(17920 + T * j, T)[0:HEADS, :] for j in range(4))
        dm = [region(17920 + PACKED * e, PACKED) for e in range(2)]
        pm = dm
        ms_k = [region(20480 + T * e, T) for e in range(2)]
        ms_v = [region(21504 + T * e, T) for e in range(2)]
        num_sb = [region(22528 + T * e, T) for e in range(2)]
        num_sq = [region(23552 + T * e, T) for e in range(2)]
        cbuf = [hf[:, j, :] for j in range(2)]
        ms_sel = [hf_f[0:HEADS, P * e:P * (e + 1)] for e in range(2)]
        ccols_f = hf_f[:, 256:288]
        ccols = ccols_f.rearrange("p (s h) -> p s h", h=HEADS)
        ms_c = [hf_f[:, 288 + 4 * e:292 + 4 * e] for e in range(2)]
        ms_g = [hf_f[:, 296 + e:297 + e] for e in range(2)]
        dn = [hf[:, 2 + e, :] for e in range(2)]
        fac = [hf[:, 4 + e, :] for e in range(2)]

        def gates_tensor(pe):
            pe.wait_ge(strip_line, 64)
            for g in range(2):
                for k in range(KD):
                    last = pe.matmul(banks[0:HEADS, 4 + g, :], wg[:, 2 * HEADS * k + HEADS * g:
                                                                 2 * HEADS * k + HEADS * (g + 1)],
                                     hf[:, k, :], start=(k == 0), stop=(k == KD - 1))
            last.then_inc(g_pe, 1)

        def mlstm_tensor(pe):
            pe.wait_ge(g_rows, 1)
            for s in range(4):
                last = pe.transpose(banks[:, 6, HEADS * s:HEADS * (s + 1)], c_row[:, P * s:P * (s + 1)],
                                    ident[0:HEADS, 0:HEADS])
            last.then_inc(g_pe, 1)
            pe.wait_ge(g_cols, 1)
            pe.wait_ge(tiles_freed, FREE0 + TILE["mlstm.o"] + 8)
            with pe.Fori(0, 4) as i:
                def first(e):
                    u = 2 * i + e
                    pe.wait_ge(m_staged, u + 1)
                    pe.wait_ge(m_dm, u + 1)
                    pe.matmul(banks[:, 3, :], ms_sel[e], m_row, start=True, stop=True).then_inc(m_mb, 1)
                    pe.wait_ge(m_p, u + 1)
                    for kb in range(4):
                        last = pe.matmul(zcols(kb), ms_k[e][:, P * kb:P * (kb + 1)],
                                         mqk[:, bass.ds(u, 1), P * kb:T].rearrange("p a n -> p (a n)"),
                                         start=(kb != 3), stop=True, skip_group_check=True)
                    last.then_inc(m_s, 1)
                    pe.wait_ge(m_ebc, u + 1)
                    pe.matmul(banks[:, 4, :], ms_sel[e], e_row, start=True, stop=True).then_inc(m_eb, 1)

                def second(e):
                    u = 2 * i + e
                    pe.wait_ge(m_pm, u + 1)
                    pe.wait_ge(m_sqr, u + 1)
                    pe.wait_ge(m_dn, u + 1)
                    for kb in range(4):
                        pe.matmul(banks[:, 5, P * kb:T], ms_v[e][:, P * kb:P * (kb + 1)], packed(pm[e], kb),
                                  start=(kb == 0), stop=(kb == 3), skip_group_check=True)
                    for kb in range(4):
                        last = pe.matmul(banks[:, 6, P * kb:T], ones, packed(pm[e], kb),
                                         start=(kb == 0), stop=(kb == 3), skip_group_check=True)
                    last.then_inc(m_nd, 1)
                    pe.wait_ge(m_sqr, u + 2)
                    pe.matmul(ps_n, ones, num_sq[e], start=True, stop=True).then_inc(m_ss, 1)

                first(0)
                first(1)
                second(0)
                pe.wait_ge(m_var, 2 * i + 1)
                second(1)
                pe.wait_ge(m_var, 2 * i + 2)
            pe.wait_ge(m_hid, 10)

        def mlstm_scalar(act):
            act.wait_ge(g_vec, 1)
            act.activation(e_row, f_row, ACT.Abs).then_inc(g_act, 1)
            act.wait_ge(g_act, 1)
            act.activation(e_row, e_row, ACT.Exp, scale=-1.0).then_inc(g_act, 1)
            act.wait_ge(g_act, 2)
            act.activation(e_row, e_row, ACT.Ln, bias=1.0).then_inc(g_act, 1)
            act.wait_ge(g_vec, 2)
            act.activation(e_row, e_row, ACT.Exp, scale=-1.0).then_inc(g_act, 1)
            with act.Fori(0, 4) as i:
                for m in range(4):
                    high_part(act, "mlstm.qk", m, 4 * i)
                    act.wait_ge(tiles_freed, FREE0 + TILE["mlstm.qk"] + 4 * i + m + 1)
                    act.activation(at(mqk, 4 * i + m), cbuf[m % 2], ACT.Silu).then_inc(conv_act, 1)
            for half in range(2):
                for s in range(4):
                    high_part(act, "mlstm.v", s, 4 * half)
                for t in range(4):
                    act.activation(mv[:, t, T * half:T * (half + 1)], lin[t], ACT.Copy).then_inc(tiles_freed, 1)
            evac(act, "mlstm.o", 8, lambda i, m: act.activation(at(sigo, 4 * i + m), lin[m], ACT.Sigmoid))
            with act.Fori(0, 4) as i:
                for e in range(2):
                    u = 2 * i + e
                    act.wait_ge(m_dm, u + 2)
                    act.activation(dm[e], dm[e], ACT.Exp, scale=-1.0).then_inc(m_d, 1)
                    act.wait_ge(m_eb, u + 1)
                    act.activation(dn[e], banks[:, 4, :], ACT.Copy).then_inc(m_ebc, 1)
                for e in range(2):
                    u = 2 * i + e
                    act.wait_ge(m_nd, u + 1)
                    act.activation(fac[e], banks[:, 6, :], ACT.Abs)
                    act.activation(num_sb[e], banks[:, 5, :], ACT.Copy)
                    act.activation(num_sq[e], banks[:, 5, :], ACT.Square).then_inc(m_sqr, 1)
                for e in range(2):
                    act.wait_ge(m_var, 2 * i + e + 1)
                    act.activation(fac[e], fac[e], ACT.Sqrt).then_inc(m_std, 1)
                for e in range(2):
                    act.wait_ge(m_out, 2 * i + e + 1)
                    act.activation(at(xh, 2 * i + e), fac[e], ACT.Copy).then_inc(m_hh, 1)

        def mlstm_vector(dve):
            tt, ts, stt = dve.tensor_tensor, dve.tensor_scalar, dve.scalar_tensor_tensor
            chain = [0]

            def link(ins):
                chain[0] += 1
                ins.then_inc(g_chain, 1)
                dve.wait_ge(g_chain, chain[0])

            dve.wait_ge(g_pe, 1)
            dve.memset(one_row, 1.0)
            link(ts(i_row, banks[0:HEADS, 4, :], vec[0:HEADS, VEC["b_i"]:VEC["b_i"] + 1], None, ALU.add))
            ts(f_row, banks[0:HEADS, 5, :], vec[0:HEADS, VEC["b_f"]:VEC["b_f"] + 1], None,
               ALU.add).then_inc(g_vec, 1)
            dve.wait_ge(g_act, 3)
            link(stt(f_row, f_row, 0.0, e_row, ALU.min, ALU.subtract))
            link(dve.tensor_tensor_scan(cum, one_row, f_row, 0.0, ALU.mult, ALU.add))
            tt(c_row, i_row, cum, ALU.subtract).then_inc(g_rows, 1)
            dve.wait_ge(g_rows, 1)
            link(dve.tensor_tensor_scan(m_row, c_row, c_row, 0.0, ALU.max, ALU.max))
            tt(e_row, cum, m_row, ALU.add).then_inc(g_vec, 1)
            dve.wait_ge(g_act, 4)
            ts(e_row, e_row, 3e38, None, ALU.min).then_inc(g_cols, 1)
            mc = VEC["mconv_w"]
            with dve.Fori(0, 4) as i:
                for m in range(4):
                    dve.wait_ge(blocks_done, BLK["mlstm.qk"] + 4 * i + m + 1)
                    dve.wait_ge(conv_act, 4 * i + m + 1)
                    c = cbuf[m % 2]
                    w = lambda tap: vec[:, bass.ds(16 * i + (mc + 4 * m + tap), 1)]
                    ts(c, lin[m], w(3), None, ALU.mult).then_inc(conv_v, 1)
                    for tap in (2, 1, 0):
                        d = 3 - tap
                        dve.wait_ge(conv_v, 12 * i + 3 * m + d)
                        last = stt(c[:, d:T], lin[m][:, 0:T - d], w(tap), c[:, d:T], ALU.mult, ALU.add)
                        last.then_inc(conv_v if tap > 0 else tiles_freed, 1)
            dve.wait_ge(g_pe, 2)
            dve.tensor_copy(ccols_f, banks[:, 6, 0:32]).then_inc(g_cols, 1)
            dve.wait_ge(tiles_freed, FREE0 + TILE["mlstm.o"] + 8)
            with dve.Fori(0, 4) as i:
                for e in range(2):
                    u = 2 * i + e
                    dve.wait_ge(m_mb, u + 1)
                    dve.wait_ge(m_staged, u + 1)
                    for s in range(4):
                        last = ts(packed(dm[e], s), banks[:, 3, P * s:T], ms_c[e][:, s:s + 1], 0.0,
                                  ALU.subtract, ALU.max)
                    last.then_inc(m_dm, 1)
                    dve.wait_ge(m_d, u + 1)
                    dve.wait_ge(m_s, u + 1)
                    stt(two(pm[e])[0], Z01, P ** -0.5, two(dm[e])[0], ALU.mult, ALU.mult)
                    stt(two(pm[e])[1], Z23, P ** -0.5, two(dm[e])[1], ALU.mult, ALU.mult).then_inc(m_p, 1)
                for e in range(2):
                    u = 2 * i + e
                    dve.wait_ge(m_sqr, u + 2)
                    dve.wait_ge(m_ebc, u + 2)
                    tt(dn[e], fac[e], dn[e], ALU.max).then_inc(m_dn, 1)
                    dve.wait_ge(m_dn, u + 2)
                    stt(fac[e], dn[e], EPS_RMS, dn[e], ALU.mult, ALU.mult).then_inc(m_d2, 1)
                    dve.wait_ge(m_d2, u + 1)
                    dve.wait_ge(m_ss, u + 1)
                    stt(fac[e], ps_n, 1.0 / P, fac[e], ALU.mult, ALU.add).then_inc(m_var, 1)
                for e in range(2):
                    u = 2 * i + e
                    dve.wait_ge(m_std, u + 1)
                    dve.reciprocal(fac[e], fac[e]).then_inc(m_rec, 1)
                    dve.wait_ge(m_rec, u + 1)
                    stt(fac[e], num_sb[e], ms_g[e], fac[e], ALU.mult, ALU.mult).then_inc(m_fin, 1)
                    dve.wait_ge(m_fin, u + 1)
                    tt(fac[e], fac[e], at(sigo, u), ALU.mult).then_inc(m_out, 1)

        def mlstm_pool(pool):
            for name in ("mlstm.qk", "mlstm.v", "mlstm.o"):
                low_parts(pool, name)
            pool.wait_ge(tiles_freed, FREE0 + TILE["mlstm.o"] + 8)
            pool.wait_ge(g_cols, 2)
            with pool.Fori(0, 4) as i:
                for e in range(2):
                    u = 2 * i + e
                    pool.wait_ge(m_hid, u + 1)
                    pool.tensor_copy(ms_k[e], at(mqk, u + 8))
                    pool.tensor_copy(ms_v[e].rearrange("p (a n) -> p a n", a=4), mv[:, :, bass.ds(P * u, P)])
                    pool.tensor_copy(ms_sel[e], ident[0:HEADS, bass.ds(u, 1)].to_broadcast([HEADS, P]))
                    pool.tensor_copy(ms_c[e].unsqueeze(2), ccols[:, :, bass.ds(u, 1)])
                    pool.tensor_copy(ms_g[e], vec[:, bass.ds(u + VEC["head_g"], 1)]).then_inc(m_staged, 1)
                for e in range(2):
                    pool.wait_ge(m_p, 2 * i + e + 2)
                    pool.sem_inc(pool_turn, 1)
                    for kb in range(4):
                        d = pm[e][:, OFF[kb]:OFF[kb] + P]
                        last = pool.affine_select(out=d, in_=d, pattern=[[1, P]], compare_op=ALU.is_ge,
                                                  fill=0.0, base=0, channel_multiplier=-1)
                    last.then_inc(m_pm, 1)
                for e in range(2):
                    pool.wait_ge(m_hh, 2 * i + e + 1)
                    pool.sem_inc(pool_turn, 1)
                    pool.tensor_tensor(at(xl, 2 * i + e), fac[e], at(xh_f, 2 * i + e),
                                       ALU.subtract).then_inc(m_hid, 1)

        iota_t = std[:, :]
        tmp_t = rstd[:, :]

        def tables_pool(pool):
            pool.wait_ge(e_bb, 8)
            pool.iota(iota_t, [[1, T]], base=0, channel_multiplier=0,
                      allow_small_or_imprecise_dtypes=True).then_inc(iota_ready, 1)

        def tables_vector(dve):
            ts, tt = dve.tensor_scalar, dve.tensor_tensor
            dve.wait_ge(iota_ready, 1)
            with dve.Fori(0, NSTATE_T) as i:
                si = at(sinT, i)
                ts(si, iota_t, small[:, bass.ds(i + PHI, 1)], None, ALU.mult).then_inc(tab_v, 1)
                dve.wait_ge(tab_v, 4 * i + 1)
                ts(tmp_t, si, ROUND, ROUND, ALU.add, ALU.subtract).then_inc(tab_v, 1)
                dve.wait_ge(tab_v, 4 * i + 2)
                tt(si, si, tmp_t, ALU.subtract).then_inc(tab_v, 1)
                dve.wait_ge(tab_v, 4 * i + 3)
                ts(tmp_t, si, 0.25, None, ALU.is_gt).then_inc(tab_v, 1)
                dve.wait_ge(tab_v, 4 * i + 4)
                dve.scalar_tensor_tensor(at(cosT, i), si, 0.25, tmp_t, ALU.add, ALU.subtract).then_inc(tab, 1)

        def tables_scalar(act, n):
            act.wait_ge(tab, n + 1)
            act.activation(at(sinT, n), at(sinT, n), ACT.Sin, scale=TWO_PI)
            act.activation(at(cosT, n), at(cosT, n), ACT.Sin, scale=TWO_PI).then_inc(tab_act, 1)

        b_raw = [hf_f[:, 0:512], hf_f[:, 512:1024]]
        c_raw = [hf_f[:, 1024:1536], hf_f[:, 1536:2048]]
        bb = [hf_f[:, 2048:2560], hf_f[:, 2560:3072]]
        c_neg = [hf_f[:, 3072:3584], hf_f[:, 3584:4096]]
        bb_t = [rstd[:, :], std[:, :]]
        xbuf = chunks(xs[:, :])
        br, bi = [xbuf[:, e, :] for e in range(2)], [xbuf[:, 2 + e, :] for e in range(2)]
        r1, r2, r3 = (xbuf[:, 4 + j, :] for j in range(3))
        pr = [xbuf[:, 7 + j, :] for j in range(4)]
        bt = [xbuf[:, 11 + q, :] for q in range(2)]
        ucs = xbuf[:, 13, :]
        bts = [xbuf[:, 14, P * q:P * (q + 1)] for q in range(2)]
        cs = [xbuf[:, 15, P * j:P * (j + 1)] for j in range(3)]
        yr, yi = rstd[:, :], std[:, :]
        r_pool = [cosT[:, g, :] for g in range(4)]
        win = cosT[:, 4:6, :]
        sig_e = [cosT[:, 6 + g, :] for g in range(2)]
        Y_ORDER = (4, 5, 6, 7, 0, 1, 2, 3)

        def even_tensor(pe):
            pe.wait_ge(e_bb, 8)
            for q in range(2):
                for c in range(4):
                    last = pe.transpose(banks[:, 4 + q, P * c:P * (c + 1)], bb[q][:, P * c:P * (c + 1)], ident)
            last.then_inc(e_t, 1)

            def drive(c, j):
                n = 4 * c + j
                rows = slice(32 * j, 32 * j + 32)
                if j == 0:
                    pe.wait_ge(s_staged, c + 1)
                pe.wait_ge(s_buc, n + 1)
                for q in range(2):
                    last = pe.matmul(banks[:, 4 + q, :], bts[q][rows, :], ucs[rows, :], start=True, stop=True)
                last.then_inc(s_bu, 1)

            def read_out(c, j):
                n = 4 * c + j
                rows = slice(32 * j, 32 * j + 32)
                if j == 0:
                    pe.wait_ge(s_ych, c + 1)
                pe.wait_ge(s_pr, n + 2)
                for q, k in enumerate((0, 1, 2, 2)):
                    last = pe.matmul(banks[rows, 6, :], cs[k][:, rows], pr[q], start=(q == 0), stop=(q == 3),
                                     skip_group_check=True)
                last.then_inc(s_ym, 1)

            with pe.Fori(0, 4) as c:
                drive(c, 0)
                for j in range(4):
                    if j < 3:
                        drive(c, j + 1)
                    read_out(c, j)
            pe.wait_ge(xn_ready, SPLIT["glu"] + 4)
            pe.wait_ge(tiles_freed, FREE0 + TILE["even.glu"])
            for b in range(4):
                pe.wait_ge(w_split, BLK["even.glu"] + b + 1)
                if b >= 2:
                    pe.wait_ge(tiles_freed, FREE0 + TILE["even.glu"] + 2 * b - 2)
                for vg in range(2):
                    for k in range(4):
                        last = product3(pe, lin[2 * (b % 2) + vg], b % 2, 4 * vg + k, xh[:, k, :], xl[:, k, :],
                                        k == 0, k == 3)
                last.then_inc(blocks_done, 1)
            for g in range(4):
                pe.wait_ge(e_pool, g + 1)
                if g >= 2:
                    pe.wait_ge(t_ready, SPLIT["even.y"] + 4 + g - 1)
                pe.matmul(banks[:, 4 + g % 2, :], pw[:, P * g:P * (g + 1)], r_pool[g], start=True,
                          stop=True).then_inc(e_pm, 1)
            pe.wait_ge(xn_ready, SPLIT["even.y"] + 8)
            pe.wait_ge(tiles_freed, FREE0 + TILE["even.out"])

        def even_scalar(act):
            for lo, dst, func in ((0, uin, ACT.Copy), (8, zin, ACT.Silu)):
                with act.Fori(0, 2) as i:
                    for m in range(4):
                        high_part(act, "even.in", m, 4 * i + lo)
                        act.activation(at(dst, 4 * i + m), lin[m], func).then_inc(tiles_freed, 1)
                        tables_scalar(act, 4 * i + (lo + m))
            act.wait_ge(e_t, 1)
            for q in range(2):
                act.activation(bt[q], banks[:, 4 + q, :], ACT.Copy).then_inc(e_btc, 1)

            def take(c, j):
                n = 4 * c + j
                act.wait_ge(s_bu, n + 1)
                act.wait_ge(s_rot, n + 1)
                act.activation(br[j % 2], banks[:, 4, :], ACT.Copy)
                act.activation(bi[j % 2], banks[:, 5, :], ACT.Copy).then_inc(s_buc, 1)

            with act.Fori(0, 4) as c:
                take(c, 0)
                for j in range(3):
                    take(c, j + 1)
            act.wait_ge(s_ym, 17)
            split_high(act, "glu", 4, uin)
            for b in range(4):
                high_part(act, "even.glu", b)
                if b >= 2:
                    act.wait_ge(tiles_freed, FREE0 + TILE["even.glu"] + 2 * b - 2)
                act.activation(sig_e[b % 2], lin[2 * (b % 2) + 1], ACT.Sigmoid).then_inc(e_sig, 1)
            split_high(act, "even.y", order=Y_ORDER)
            with act.Fori(0, 2) as i:
                for s in range(4):
                    high_part(act, "even.out", s, 4 * i)

        def residual(dve, name):
            with dve.Fori(0, 2) as i:
                for m in range(4):
                    dve.wait_ge(blocks_done, BLK[name] + 4 * i + m + 1)
                    dve.tensor_tensor(at(x, 4 * i + m), at(x, 4 * i + m), lin[m], ALU.add).then_inc(tiles_freed, 1)

        def even_vector(dve):
            ts, tt, stt = dve.tensor_scalar, dve.tensor_tensor, dve.scalar_tensor_tensor
            dve.wait_ge(e_loaded, 64)

            def v3(ap):
                return ap.rearrange("p (a n) -> p a n", a=NSTATE_T)

            def gain(c):
                return col(c).unsqueeze(2).to_broadcast([P, NSTATE_T, 32])

            tt(v3(bb[0]), v3(b_raw[0]), gain(KRE), ALU.mult).then_inc(e_bb, 1)
            tt(v3(bb_t[0]), v3(b_raw[1]), gain(KIM), ALU.mult).then_inc(e_bb, 1)
            tt(v3(bb[1]), v3(b_raw[1]), gain(KRE), ALU.mult).then_inc(e_bb, 1)
            tt(v3(bb_t[1]), v3(b_raw[0]), gain(KIM), ALU.mult).then_inc(e_bb, 1)
            dve.wait_ge(e_bb, 4)
            tt(bb[0], bb[0], bb_t[0], ALU.subtract).then_inc(e_bb, 1)
            tt(bb[1], bb[1], bb_t[1], ALU.add).then_inc(e_bb, 1)
            for q in range(2):
                ts(c_neg[q], c_raw[q], -1.0, None, ALU.mult).then_inc(e_bb, 1)
            tables_vector(dve)
            dve.wait_ge(tab_act, NSTATE_T)
            with dve.Fori(0, 4) as c:
                for j in range(4):
                    n = 4 * c + j
                    co, si = at(cosT, n), at(sinT, n)
                    dve.wait_ge(s_buc, n + 2)
                    tt(r1, co, br[j % 2], ALU.mult)
                    tt(r2, si, bi[j % 2], ALU.mult).then_inc(s_v, 1)
                    tt(r3, co, bi[j % 2], ALU.mult)
                    dve.wait_ge(s_v, 3 * n + 1)
                    tt(r1, r1, r2, ALU.add).then_inc(s_v, 1)
                    dve.wait_ge(s_v, 3 * n + 2)
                    tt(r2, si, br[j % 2], ALU.mult).then_inc(s_rot, 1)
                    dve.wait_ge(s_pr, n + 1)
                    decay = small[:, bass.ds(n + R_, 1)].to_broadcast([P, T])
                    dve.tensor_tensor_scan(yr, decay, r1, 0.0, ALU.mult, ALU.add)
                    dve.wait_ge(s_rot, n + 3)
                    tt(r3, r3, r2, ALU.subtract).then_inc(s_v, 1)
                    dve.wait_ge(s_v, 3 * n + 3)
                    dve.tensor_tensor_scan(yi, decay, r3, 0.0, ALU.mult, ALU.add).then_inc(s_y, 1)
                    dve.wait_ge(s_y, n + 1)
                dve.wait_ge(s_ym, 4 * c + 5)
                stt(at(uin, c), at(uin, c), vec[:, bass.ds(c + VEC["ssm_d"], 1)], banks[:, 6, :],
                    ALU.mult, ALU.add).then_inc(s_ych, 1)
            dve.wait_ge(s_ych, 5)
            dve.memset(small[:, 0:1], 0.0).then_inc(t_ready, 4)
            dve.wait_ge(s_ych, 5)
            steps = 0
            for g, w in enumerate((2, 4, 8, 16)):
                u_g = uin[:, 4 + g, :]
                src, k = u_g, 1
                while k < w:
                    dst = win[:, steps % 2, :]
                    dve.tensor_copy(dst[:, 0:k], src[:, 0:k])
                    tt(dst[:, k:T], src[:, k:T], src[:, 0:T - k], ALU.add).then_inc(e_win, 1)
                    steps += 1
                    dve.wait_ge(e_win, steps)
                    src, k = dst, 2 * k
                o = C_INV + 16 * g
                stt(r_pool[g][:, 16:T], src[:, 16:T], 1.0 / w, u_g[:, 16:T], ALU.mult, ALU.subtract)
                tt(r_pool[g][:, 0:16], src[:, 0:16], cst_sb[:, o:o + 16], ALU.mult).then_inc(e_w2, 1)
                dve.wait_ge(e_w2, g + 1)
                tt(r_pool[g][:, 0:16], r_pool[g][:, 0:16], u_g[:, 0:16], ALU.subtract).then_inc(e_pool, 1)
            for b in range(4):
                dve.wait_ge(e_sig, b + 1)
                tt(hf[:, 4 + b, :], lin[2 * (b % 2)], sig_e[b % 2], ALU.mult).then_inc(tiles_freed, 2)
                dve.wait_ge(tiles_freed, FREE0 + TILE["even.glu"] + 2 * b + 2)
                tt(hf[:, 4 + b, :], hf[:, 4 + b, :], zin[:, 4 + b, :], ALU.mult).then_inc(t_ready, 1)
            for g in range(4):
                dve.wait_ge(e_pm, g + 1)
                c0 = VEC["pool_scale"] + g
                stt(hf[:, g, :], banks[:, 4 + g % 2, :], vec[:, c0:c0 + 1], zin[:, g, :],
                    ALU.mult, ALU.mult).then_inc(t_ready, 1)
            residual(dve, "even.out")

        def even_pool(pool):
            pool.wait_ge(xn_ready, SPLIT["even"] + 8)
            for dst, src in ((b_raw[0], bst[0]), (b_raw[1], bst[1]), (c_raw[0], cst[0]), (c_raw[1], cst[1])):
                pool.dma_start(dst, src).then_inc(e_loaded, 16)
            tables_pool(pool)
            low_parts(pool, "even.in")
            pool.wait_ge(e_btc, 2)
            tt = pool.tensor_tensor
            with pool.Fori(0, 4) as c:
                pool.tensor_copy(ucs, at(uin, c))
                for dst, src in ((bts[0], bt[0]), (bts[1], bt[1]), (cs[0], c_raw[0]), (cs[1], c_neg[0]),
                                 (cs[2], c_neg[1])):
                    last = pool.tensor_copy(dst, src[:, bass.ds(P * c, P)])
                last.then_inc(s_staged, 1)
                for j in range(4):
                    n = 4 * c + j
                    co, si = at(cosT, n), at(sinT, n)
                    pool.wait_ge(s_y, n + 1)
                    pool.wait_ge(s_ym, n + 1)
                    tt(pr[0], co, yr, ALU.mult)
                    tt(pr[1], si, yi, ALU.mult)
                    tt(pr[2], si, yr, ALU.mult)
                    tt(pr[3], co, yi, ALU.mult).then_inc(s_pr, 1)
                pool.wait_ge(s_ym, 4 * c + 5)
            split_low(pool, "glu", 4, uin)
            low_parts(pool, "even.glu")
            split_low(pool, "even.y", order=Y_ORDER)
            low_parts(pool, "even.out")

        sig_o = [region(12800 + T * s, T) for s in range(2)]
        mean = region(13824, T)

        def odd_tensor(pe):
            for c in range(KD):
                pe.wait_ge(o_conv, c + 1)
                last = pe.matmul(banks[:, 6, :], ones, cc[:, c, :], start=(c == 0), stop=(c == KD - 1))
            last.then_inc(o_sum, 1)
            sumsq_of(pe, squares, 64)
            pe.wait_ge(xn_ready, SPLIT["odd.y"] + 8)
            pe.wait_ge(tiles_freed, FREE0 + TILE["odd.out"])

        def odd_scalar(act):
            with act.Fori(0, 4) as i:
                for s in range(2):
                    high_part(act, "odd.in", 2 * s, 4 * i)
                    high_part(act, "odd.in", 2 * s + 1, 4 * i)
                    act.wait_ge(tiles_freed, FREE0 + TILE["odd.in"] + 4 * i + 2 * s - 2)
                    act.activation(sig_o[s], lin[2 * s + 1], ACT.Sigmoid).then_inc(o_sig, 1)
            with act.Fori(0, 2) as i:
                for m in range(4):
                    high_part(act, "odd.in", m, 4 * i + 16)
                    act.activation(at(zz, 4 * i + m), lin[m], ACT.Silu).then_inc(tiles_freed, 1)
            act.wait_ge(sumsq_ready, norm_no["odd.ln"])
            for c in range(KD):
                act.wait_ge(o_cen, c + 2)
                act.activation(sq[:, c, :], cc[:, c, :], ACT.Square).then_inc(squares, 1)
            n = norm_no["odd.ln"]
            act.wait_ge(var_ready, n + 1)
            act.activation(std[:, :], std[:, :], ACT.Sqrt).then_inc(std_ready, 1)
            for c in range(KD):
                act.wait_ge(o_n, c + 1)
                b = VEC["ln_b"] + c
                act.activation(cc[:, c, :], cc[:, c, :], ACT.Silu, bias=vec[:, b:b + 1]).then_inc(o_s, 1)
            split_high(act, "odd.y")
            for s in range(NBLK["odd.out"]):
                high_part(act, "odd.out", s % 4, s - s % 4)

        def odd_vector(dve):
            ts, tt, stt = dve.tensor_scalar, dve.tensor_tensor, dve.scalar_tensor_tensor
            dve.memset(gpad[:, :, 0:PAD], 0.0).then_inc(o_v, 1)
            dve.wait_ge(o_v, 1)
            cw = VEC["conv_w"]
            with dve.Fori(0, 4) as i:
                for s in range(2):
                    dve.wait_ge(o_sig, 2 * i + s + 1)
                    g = gpad[:, bass.ds(2 * i + s, 1), :].rearrange("p a n -> p (a n)")
                    c = at(cc, 2 * i + s)
                    tt(g[:, PAD:PAD + T], lin[2 * s], sig_o[s], ALU.mult).then_inc(tiles_freed, 2)
                    dve.wait_ge(tiles_freed, FREE0 + TILE["odd.in"] + 4 * i + 2 * s + 2)

                    def w(tap):
                        return vec[:, bass.ds(2 * CONV_K * i + (cw + CONV_K * s + tap), 1)]

                    ts(c, g[:, 0:T], w(0), vec[:, bass.ds(2 * i + (VEC["conv_b"] + s), 1)], ALU.mult,
                       ALU.add).then_inc(o_v, 1)
                    for tap in range(1, CONV_K):
                        dve.wait_ge(o_v, (CONV_K - 1) * (2 * i + s) + tap + 1)
                        last = stt(c, g[:, tap:tap + T], w(tap), c, ALU.mult, ALU.add)
                        last.then_inc(o_v if tap < CONV_K - 1 else o_conv, 1)
            dve.wait_ge(o_sum, 1)
            ts(mean, banks[:, 6, :], 1.0 / D, None, ALU.mult).then_inc(o_cen, 1)
            dve.wait_ge(o_cen, 1)
            for c in range(KD):
                tt(cc[:, c, :], cc[:, c, :], mean, ALU.subtract).then_inc(o_cen, 1)
            norm_stats(dve, "odd.ln", eps=EPS_LN)
            for c in range(KD):
                b = VEC["ln_g"] + c
                stt(cc[:, c, :], cc[:, c, :], vec[:, b:b + 1], rstd[:, :], ALU.mult, ALU.mult).then_inc(o_n, 1)
            for c in range(KD):
                dve.wait_ge(o_s, c + 1)
                tt(hf[:, c, :], cc[:, c, :], zz[:, c, :], ALU.mult).then_inc(t_ready, 1)
            residual(dve, "odd.out")

        def norm_stats(dve, name, scale=1.0 / D, eps=EPS_RMS):
            n = norm_no[name]
            dve.wait_ge(sumsq_ready, n + 1)
            dve.tensor_scalar(std[:, :], ps_n, scale, eps, ALU.mult, ALU.add).then_inc(var_ready, 1)
            dve.wait_ge(std_ready, n + 1)
            dve.reciprocal(rstd[:, :], std[:, :]).then_inc(rstd_ready, 1)
            dve.wait_ge(rstd_ready, n + 1)

        def sumsq_of(pe, signal, base, buf=sq):
            for c in range(KD):
                pe.wait_ge(signal, base + c + 1)
                last = pe.matmul(ps_n, ones, buf[:, c, :], start=(c == 0), stop=(c == KD - 1))
            last.then_inc(sumsq_ready, 1)

        def product3(pe, dst, q, t, in_hi, in_lo, first, last):
            cols = slice(t * P, (t + 1) * P)
            pe.matmul(dst, wh[:, q, cols], in_hi, start=first, stop=False)
            pe.matmul(dst, wl[:, q, cols], in_hi, start=False, stop=False)
            return pe.matmul(dst, wh[:, q, cols], in_lo, start=False, stop=last)

        def block_mm(pe, dst, q, hi, lo, n=KD, k0=0, total=KD):
            for k in range(n):
                last = product3(pe, dst, q, k, hi[:, k0 + k, :], lo[:, k0 + k, :], k0 + k == 0,
                                k0 + k == total - 1)
            last.then_inc(blocks_done, 1)

        block = ctx.enter_context(nc.Block())

        @block.sync
        def _(sp):
            for dst, src in ((cst_sb[:, :], consts), (vec[:, :], vecs), (x, x_in)):
                sp.dma_start(dst, src).then_inc(in_loaded, 16)
            def load(i, s):
                sp.dma_start(raw[:, s, :], weights[bass.ds(4 * i + s, 1)].rearrange("b p n -> (b p) n")
                             ).then_inc(w_loaded[s], 16)

            for s in range(RING):
                load(0, s)
            with sp.Fori(1, BLOCKS // RING) as i:
                for s in range(RING):
                    sp.wait_ge(w_split, 4 * i + s - 3)
                    load(i, s)
            sp.wait_ge(t_ready, SPLIT["final"] + 8)
            sp.dma_start(out, hf).then_inc(out_done, 16)
            sp.wait_ge(out_done, 16)

        @block.tensor
        def _(pe):
            def sumsq(name, signal, base, buf=sq):
                sumsq_of(pe, signal, base, buf)

            def linear(name, lo=0, hi=None):
                hi = NBLK[name] if hi is None else hi
                with pe.Fori(lo // 4, hi // 4) as i:
                    for s in range(4):
                        pe.wait_ge(w_split, BLK[name] + s + 1 + 4 * i)
                        pe.wait_ge(tiles_freed, FREE0 + TILE[name] + 4 * i + s - 3)
                        block_mm(pe, lin[s], s % 2, xh, xl)

            def token_major(name):
                for half in range(2):
                    pe.wait_ge(tiles_freed, FREE0 + TILE[name] + 4 * half)
                    for b in range(4):
                        pe.wait_ge(w_split, BLK[name] + 4 * half + b + 1)
                        for kk in range(2):
                            k = 2 * b + kk
                            cols = slice(kk * T, (kk + 1) * T)
                            for t in range(4):
                                tok = slice(t * P, (t + 1) * P)
                                pe.matmul(lin[t], xh[:, k, tok], wh[:, b % 2, cols], start=(k == 0), stop=False)
                                pe.matmul(lin[t], xh[:, k, tok], wl[:, b % 2, cols], start=False, stop=False)
                                last = pe.matmul(lin[t], xl[:, k, tok], wh[:, b % 2, cols], start=False,
                                                 stop=(k == 7))
                        last.then_inc(blocks_done, 1)

            def ffn(name, idx):
                pe.wait_ge(xn_ready, SPLIT[name] + 8)
                gu, dn_ = name + ".gu", name + ".dn"
                pe.wait_ge(tiles_freed, FREE0 + TILE[gu])
                with pe.Fori(0, KF // 2) as i:
                    for s in range(4):
                        pe.wait_ge(w_split, BLK[gu] + s + 1 + 4 * i)
                        if s % 2 == 0:
                            pe.wait_ge(tiles_freed, FREE0 + TILE[gu] + 4 * i + s - 2)
                        block_mm(pe, lin[s], s % 2, xh, xl)
                pe.wait_ge(tiles_freed, FREE0 + TILE[dn_])
                pe.wait_ge(h_lo, 2 + KF * (idx + 1))
                with pe.Fori(0, 2) as i:
                    for m in range(4):
                        pe.wait_ge(tiles_freed, FREE0 + TILE[dn_] + 4 * i + m - 3)
                        k0 = 0
                        for j, n in enumerate(DN):
                            pe.wait_ge(w_split, BLK[dn_] + 3 * m + j + 1 + 12 * i)
                            block_mm(pe, lin[m], (3 * m + j) % 2, hh, hl, n=n, k0=k0, total=KF)
                            k0 += n
                sumsq(name + ".post", tiles_freed, FREE0 + TILE[dn_])

            pe.wait_ge(in_loaded, 48)
            prep_tensor(pe)
            sumsq("ffn0.pre", squares, 0)
            ffn("ffn0", 0)
            sumsq("attn.pre", squares, 8)
            pe.wait_ge(xn_ready, SPLIT["attn"] + 8)
            pe.wait_ge(tiles_freed, FREE0 + TILE["attn.qk"])
            linear("attn.qk")
            token_major("attn.v")
            attention_tensor(pe)
            pe.wait_ge(tiles_freed, FREE0 + TILE["attn.out"])
            linear("attn.out")
            sumsq("attn.post", tiles_freed, FREE0 + TILE["attn.out"], mix_sq)
            sumsq("ffn1.pre", squares, 16)
            ffn("ffn1", 1)
            sumsq("ffn2.pre", squares, 24)
            ffn("ffn2", 2)
            sumsq("mlstm.pre", squares, 32)
            pe.wait_ge(xn_ready, SPLIT["mlstm"] + 8)
            pe.wait_ge(tiles_freed, FREE0 + TILE["mlstm.qk"])
            gates_tensor(pe)
            linear("mlstm.qk")
            token_major("mlstm.v")
            pe.wait_ge(tiles_freed, FREE0 + TILE["mlstm.o"])
            linear("mlstm.o")
            mlstm_tensor(pe)
            linear("mlstm.out")
            sumsq("mlstm.post", tiles_freed, FREE0 + TILE["mlstm.out"], mix_sq)
            sumsq("ffn3.pre", squares, 40)
            ffn("ffn3", 3)
            sumsq("even.pre", squares, 48)
            pe.wait_ge(xn_ready, SPLIT["even"] + 8)
            pe.wait_ge(tiles_freed, FREE0 + TILE["even.in"])
            linear("even.in")
            even_tensor(pe)
            linear("even.out")
            sumsq("odd.pre", squares, 56, hf)
            pe.wait_ge(xn_ready, SPLIT["odd"] + 8)
            pe.wait_ge(tiles_freed, FREE0 + TILE["odd.in"])
            linear("odd.in", 0, 16)
            pe.wait_ge(tiles_freed, FREE0 + TILE["odd.in"] + 16)
            linear("odd.in", 16, 24)
            odd_tensor(pe)
            linear("odd.out")
            sumsq("final", squares, 72, hf)

        @block.scalar
        def _(act):
            def square_x(u):
                if u > 0:
                    act.wait_ge(sumsq_ready, norm_no[PRE[u]])
                for c in range(KD):
                    if u == 0:
                        act.wait_ge(in_loaded, 48)
                    elif u <= 6:
                        act.wait_ge(x_ready, 8 * (u - 1) + c + 1)
                    else:
                        act.wait_ge(tiles_freed, FREE0 + TILE[("even.out", "odd.out")[u - 7]] + c + 1)
                    act.activation((sq if u <= 6 else hf)[:, c, :], x[:, c, :], ACT.Square).then_inc(squares, 1)

            def take_std(name):
                n = norm_no[name]
                act.wait_ge(var_ready, n + 1)
                act.activation(std[:, :], std[:, :], ACT.Sqrt).then_inc(std_ready, 1)

            def branch_out(name):
                n = norm_no[name.split(".")[0] + ".post"]
                act.wait_ge(sumsq_ready, n)
                per = NBLK[name] // KD
                dst = sq if per > 1 else mix_sq
                with act.Fori(0, 2) as i:
                    for m in range(4):
                        for j in range(per):
                            high_part(act, name, per * m + j, 4 * per * i)
                        act.activation(at(hf, 4 * i + m), lin[m], ACT.Copy)
                        act.activation(at(dst, 4 * i + m), lin[m], ACT.Square).then_inc(tiles_freed, 1)

            def ffn(name, idx):
                take_std(name + ".pre")
                split_high(act, name)
                gu = name + ".gu"
                with act.Fori(0, KF // 2) as i:
                    for s in range(2):
                        high_part(act, gu, 2 * s, 4 * i)
                        act.wait_ge(tiles_freed, FREE0 + TILE[gu] + 4 * i + 2 * s - 2)
                        act.activation(sg[:, s, :], lin[2 * s], ACT.Silu).then_inc(gate_act, 1)
                        high_part(act, gu, 2 * s + 1, 4 * i)
                        act.wait_ge(tiles_freed, FREE0 + TILE[gu] + 4 * i + 2 * s + 2)
                        act.activation(at(hh, 2 * i + s), ht[:, s, :], ACT.Copy).then_inc(h_hi, 1)
                branch_out(name + ".dn")
                take_std(name + ".post")

            prep_scalar(act)
            square_x(0)
            ffn("ffn0", 0)
            square_x(1)
            take_std("attn.pre")
            split_high(act, "attn")
            attention_in_scalar(act)
            attention_scalar(act)
            branch_out("attn.out")
            take_std("attn.post")
            square_x(2)
            ffn("ffn1", 1)
            square_x(3)
            ffn("ffn2", 2)
            square_x(4)
            take_std("mlstm.pre")
            split_high(act, "mlstm")
            mlstm_scalar(act)
            branch_out("mlstm.out")
            take_std("mlstm.post")
            square_x(5)
            ffn("ffn3", 3)
            square_x(6)
            take_std("even.pre")
            split_high(act, "even")
            even_scalar(act)
            square_x(7)
            take_std("odd.pre")
            split_high(act, "odd")
            odd_scalar(act)
            square_x(8)
            take_std("final")

        @block.vector
        def _(dve):
            def pre(name):
                norm_stats(dve, name)
                for c in range(KD):
                    dve.scalar_tensor_tensor(hf[:, c, :], x[:, c, :], g_of(name, c), rstd[:, :],
                                             ALU.mult, ALU.mult).then_inc(t_ready, 1)

            def post(name):
                norm_stats(dve, name + ".post")
                for c in range(KD):
                    dve.scalar_tensor_tensor(hf[:, c, :], hf[:, c, :], g_of(name + ".post", c), rstd[:, :],
                                             ALU.mult, ALU.mult).then_inc(scaled, 1)

            def ffn(name, idx):
                pre(name + ".pre")
                gu, dn = name + ".gu", name + ".dn"
                with dve.Fori(0, KF // 2) as i:
                    for s in range(2):
                        dve.wait_ge(blocks_done, BLK[gu] + 4 * i + 2 * s + 2)
                        dve.wait_ge(gate_act, KF * idx + 2 * i + s + 1)
                        dve.wait_ge(h_lo, KF * idx + 2 * i + s + 1)
                        dve.tensor_tensor(ht[:, s, :], sg[:, s, :], lin[2 * s + 1],
                                          ALU.mult).then_inc(tiles_freed, 2)
                post(name)

            prep_vector(dve)
            ffn("ffn0", 0)
            pre("attn.pre")
            attention_in_vector(dve)
            attention_vector(dve)
            post("attn")
            ffn("ffn1", 1)
            ffn("ffn2", 2)
            pre("mlstm.pre")
            mlstm_vector(dve)
            post("mlstm")
            ffn("ffn3", 3)
            pre("even.pre")
            even_vector(dve)
            pre("odd.pre")
            odd_vector(dve)
            pre("final")

        @block.gpsimd
        def _(pool):
            def update(u, n_before):
                for c in range(KD):
                    pool.wait_ge(scaled, 8 * n_before + c + 1)
                    pool.tensor_tensor(x[:, c, :], x[:, c, :], hf[:, c, :], ALU.add).then_inc(x_ready, 1)

            def ffn(name, idx):
                split_low(pool, name)
                gu = name + ".gu"
                with pool.Fori(0, KF // 2) as i:
                    for s in range(2):
                        low_part(pool, gu, 2 * s, 4 * i)
                        low_part(pool, gu, 2 * s + 1, 4 * i)
                        pool.wait_ge(h_hi, KF * idx + 2 * i + s + 1)
                        pool.sem_inc(pool_turn, 1)
                        pool.tensor_tensor(at(hl, 2 * i + s), ht[:, s, :], at(hh_f, 2 * i + s),
                                           ALU.subtract).then_inc(h_lo, 1)
                low_parts(pool, name + ".dn")

            first_parts(pool, True)
            ffn("ffn0", 0)
            pool.wait_ge(blocks_done, BLK["attn.qk"])
            pool.dma_start(strip, skewed(scratch)).then_inc(strip_in, 16)
            update(0, 0)
            split_low(pool, "attn")
            attention_pool(pool)
            low_parts(pool, "attn.out")
            update(1, 1)
            ffn("ffn1", 1)
            update(2, 2)
            ffn("ffn2", 2)
            update(3, 3)
            split_low(pool, "mlstm")
            mlstm_pool(pool)
            low_parts(pool, "mlstm.out")
            update(4, 4)
            ffn("ffn3", 3)
            update(5, 5)
            split_low(pool, "even")
            even_pool(pool)
            split_low(pool, "odd")
            low_parts(pool, "odd.in")
            split_low(pool, "odd.y")
            for s in range(NBLK["odd.out"]):
                low_part(pool, "odd.out", s % 4, s - s % 4)


def bucket(d):
    if d < 16:
        return d
    return min(16 + int(np.log(d / 16) / np.log(2048 / 16) * 16), NB_BUCKETS - 1)


def bias_columns():
    table = np.zeros((NB_BUCKETS + 1, STRIP_W), np.float32)
    for c in range(STRIP_W):
        d = T - 1 - c
        count = 0 if d < 0 else (d <= 128) + (d % 4 == 0) + (d % 16 == 0)
        if d >= 0:
            table[bucket(d), c] = 1.0
        table[NB_BUCKETS, c] = np.log(count) if count else NEG
    return table


def constants():
    c = np.zeros((P, NCONST), np.float32)
    c[:, C_ID:C_ID + P] = np.eye(P)
    c[:, C_TRI:C_TRI + P] = -np.tril(np.ones((P, P)))
    c[:, C_ONE:C_ONE + P] = 1.0
    for g, w in enumerate((2, 4, 8, 16)):
        c[:, C_INV + 16 * g:C_INV + 16 * (g + 1)] = 1.0 / np.minimum(np.arange(1, 17), w)
    return c


def kernel(**inputs):
    import concourse.bacc as _bacc
    from concourse.bass_utils import run_bass_kernel_spmd as _run

    a = {k: np.asarray(v) for k, v in inputs.items()}

    def blocks(w):
        k, n = w.shape
        return w.reshape(k // P, P, n // P, P).transpose(2, 1, 0, 3).reshape(n // P, P, k)

    def row_blocks(w):
        return w.reshape(4, 2, P, T).transpose(0, 2, 1, 3).reshape(4, P, 2 * T)

    def pairs(u, v):
        return np.stack([u, v], 1).reshape(-1, *u.shape[1:])

    def ffn(layer, j):
        w8.append(pairs(blocks(a["ffn_w_gate"][layer, j]), blocks(a["ffn_w_up"][layer, j])))
        down = np.zeros((KD, P, len(DN) * SLOT), np.float32)
        down[:, :, 0:FF] = blocks(a["ffn_w_down"][layer, j])
        w8.append(down.reshape(KD, P, len(DN), SLOT).transpose(0, 2, 1, 3).reshape(-1, P, SLOT))

    w8 = []
    ffn(0, 0)
    w = a["attn_w_in"][0]
    for lo in (0, 512, 1536, 2048):
        w8.append(blocks(w[:, lo:lo + 512]))
    w8.append(row_blocks(w[:, 1024:1536]))
    w8.append(row_blocks(w[:, 2560:3072]))
    w8.append(blocks(a["attn_w_out"][0]))
    ffn(0, 1)
    ffn(1, 0)
    w = a["mlstm_w_in"][0]
    w8.append(blocks(w[:, 0:2048]))
    w8.append(row_blocks(w[:, 2048:2560]))
    w8.append(row_blocks(w[:, 2560:3072]))
    w8.append(blocks(w[:, 3072:4096]))
    w_gates = w[:, 4096:].reshape(KD, P, 16).transpose(1, 0, 2).reshape(P, 128)
    w8.append(blocks(a["mlstm_w_out"][0]))
    ffn(1, 1)
    w = a["even_w_in_2"][0]
    w8.append(blocks(w[:, 512:1024]))
    w8.append(blocks(w[:, 0:512]))
    w8.append(blocks(w[:, 1024:2048]))
    w = blocks(a["ssm_w_glu_2"][0])
    w8.append(np.concatenate([w[0:4], w[4:8]], 2))
    w8.append(blocks(a["even_w_out_2"][0]))
    w = blocks(a["odd_w_in_2"][0])
    w8.append(pairs(w[0:8], w[8:16]))
    w8.append(w[16:24])
    w8.append(blocks(a["odd_w_out_2"][0]))
    w8 = np.concatenate(w8)

    def per_channel(v):
        return v.reshape(-1, P).T

    def per_state(v):
        return np.broadcast_to(v.reshape(32, -1), (32, 64)).reshape(NSTATE_T, P).T

    vecs = np.zeros((P, NVEC), np.float32)
    for name, v in (("norm_g", per_channel(a["norm_g"])), ("even_norm", per_channel(a["even_norm_2"])),
                    ("odd_norm", per_channel(a["odd_norm_2"])), ("final_norm", per_channel(a["final_norm_2"])),
                    ("pool_scale", per_channel(a["pool_scale_2"])), ("ssm_d", per_channel(a["ssm_d_2"])),
                    ("conv_b", per_channel(a["conv_b_2"])), ("ln_g", per_channel(a["conv_ln_g_2"])),
                    ("ln_b", per_channel(a["conv_ln_b_2"])), ("head_g", per_channel(a["mlstm_head_g"])),
                    ("conv_w", a["conv_w_2"][0].reshape(CONV_K, KD, P).transpose(2, 1, 0).reshape(P, -1)),
                    ("mconv_w", a["mlstm_conv_w"][0].reshape(MCONV_K, 16, P).transpose(2, 1, 0).reshape(P, -1)),
                    ("log_dt", per_state(a["ssm_log_dt_2"][0][:, None])), ("a_re", per_state(a["ssm_a_re_2"][0])),
                    ("a_im", per_state(a["ssm_a_im_2"][0]))):
        vecs[:, VEC[name]:VEC[name] + v.shape[1]] = v
    vecs[0:HEADS, VEC["b_i"]] = a["mlstm_b_gates"][0, 0:HEADS]
    vecs[0:HEADS, VEC["b_f"]] = a["mlstm_b_gates"][0, HEADS:]

    def diagonal(v):
        out = np.zeros((NSTATE_T, 2, 64, 2, 16), np.float32)
        v = v.reshape(NSTATE_T, 2, 64, 16)
        out[:, 0, :, 0] = v[:, 0]
        out[:, 1, :, 1] = v[:, 1]
        return out.reshape(NSTATE_T, P, 32).transpose(1, 0, 2).reshape(P, 512)

    bst = np.stack([diagonal(a["ssm_b_re_2"][0]), diagonal(a["ssm_b_im_2"][0])])
    cst = np.stack([diagonal(a["ssm_c_re_2"][0].transpose(0, 2, 1)),
                    diagonal(a["ssm_c_im_2"][0].transpose(0, 2, 1))])
    arrays = {
        "x_in": a["x"].reshape(T, KD, P).transpose(2, 1, 0), "weights": w8, "vecs": vecs,
        "consts": constants(), "rel_bias": a["rel_bias"], "buckets": bias_columns(), "w_gates": w_gates,
        "pool_w": a["pool_w_2"][0].transpose(1, 0, 2).reshape(P, 512), "bst": bst, "cst": cst,
    }
    arrays = {k: np.ascontiguousarray(v) for k, v in arrays.items()}
    nc = _bacc.Bacc("TRN2", target_bir_lowering=False, num_devices=1)
    args = [nc.dram_tensor(k, v.shape, F32, kind="ExternalInput").ap() for k, v in arrays.items()]
    scratch = nc.dram_tensor("scratch", (P, HEADS * STRIP_W), F32, kind="Internal").ap()
    out = nc.dram_tensor("out", (P, KD, T), F32, kind="ExternalOutput").ap()
    build(nc, *args, scratch, out)
    r = _run(nc, [arrays], core_ids=[0])
    return r.results[0]["out"].transpose(2, 1, 0).reshape(1, T, D)
```

```python
from contextlib import ExitStack

import numpy as np
import concourse.bass as bass
from concourse import mybir

F32 = mybir.dt.float32
F32R = mybir.dt.float32r
ALU = mybir.AluOpType
ACT = mybir.ActivationFunctionType
AX = mybir.AxisListType

P = 128
T = 512
D = 1024
KD = D // P
FF = 2816
KF = FF // P
DN = (8, 8, 6)
NB_BUCKETS = 32
RING = 4
SLOT = KD * P
HEADS = 8
EPS_RMS = 1e-6
EPS_LN = 1e-5
CONV_K = 31
PAD = CONV_K - 1
POOL_TAPS = 7
MCONV_K = 4
NSTATE_T = 16
TWO_PI = 6.2831845
ROUND = 12582912.0
NEG = -1e30
STRIP_W = 5 * P
OFF = (0, 512, 896, 1152)
PACKED = 1280

SECTIONS = []
for _name, _kinds in (("ffn0", "f"), ("attn", "a"), ("ffn1", "f"), ("ffn2", "f"), ("mlstm", "m"),
                      ("ffn3", "f"), ("even", "e"), ("odd", "o")):
    SECTIONS += {
        "f": [(_name + ".gu", 2 * KF), (_name + ".dn", len(DN) * KD)],
        "a": [("attn.qk", 16), ("attn.v", 8), ("attn.out", 8)],
        "m": [("mlstm.qk", 16), ("mlstm.v", 8), ("mlstm.o", 8), ("mlstm.out", 8)],
        "e": [("even.in", 16), ("even.glu", 4), ("even.out", 8)],
        "o": [("odd.in", 24), ("odd.out", 8)],
    }[_kinds]

BLK, TILE = {}, {}
_b = _t = 0
for _name, _n in SECTIONS:
    BLK[_name], TILE[_name] = _b, _t
    _b += _n
    _t += KD if _name.endswith(("dn", "glu")) else _n
NBLK = dict(SECTIONS)
BLOCKS = _b

SPLIT = {}
_c = 0
for _name, _n in (("ffn0", 8), ("attn", 8), ("ffn1", 8), ("ffn2", 8), ("mlstm", 8), ("ffn3", 8), ("even", 8),
                  ("glu", 4), ("even.y", 8), ("odd", 8), ("odd.y", 8), ("final", 8)):
    SPLIT[_name] = _c
    _c += _n

TNO = {}
_c = 0
for _name, _n in SPLIT.items():
    TNO[_name] = _c
    _c += 0 if _name.startswith("ffn") else 4 if _name == "glu" else 8

NORMS = ["ffn0.pre", "ffn0.post", "attn.pre", "attn.post", "ffn1.pre", "ffn1.post", "ffn2.pre", "ffn2.post",
         "mlstm.pre", "mlstm.post", "ffn3.pre", "ffn3.post", "even.pre", "odd.pre", "odd.ln", "final"]
ACC = {n: i for i, n in enumerate(n for n in NORMS if n != "odd.ln")}
ACC_STEPS = KD + 1
PRE = [n for n in NORMS if not n.endswith(("post", "ln"))]

VEC = {}
_c = 0
for _name, _n in (("norm_g", 96), ("even_norm", 8), ("odd_norm", 8), ("final_norm", 8), ("pool_scale", 4),
                  ("ssm_d", 4), ("conv_b", 8), ("ln_g", 8), ("ln_b", 8), ("head_g", 8), ("conv_w", 31 * 8),
                  ("mconv_w", 4 * 16), ("log_dt", 16), ("a_re", 16), ("a_im", 16), ("b_i", 1), ("b_f", 1)):
    VEC[_name] = _c
    _c += _n
NVEC = _c
GCOL = {"ffn0.pre": 0, "ffn0.post": 8, "attn.pre": 16, "attn.post": 24, "ffn1.pre": 32, "ffn1.post": 40,
        "ffn2.pre": 48, "ffn2.post": 56, "mlstm.pre": 64, "mlstm.post": 72, "ffn3.pre": 80, "ffn3.post": 88,
        "even.pre": VEC["even_norm"], "odd.pre": VEC["odd_norm"], "final": VEC["final_norm"]}

C_ID, C_TRI, C_ONE, C_INV = 0, P, 2 * P, 3 * P
NCONST = C_INV + 64


def skewed(scratch):
    w = HEADS * STRIP_W
    return bass.AP(tensor=scratch.tensor, offset=scratch.offset + P - 1,
                   ap=[[w - 1, P], [STRIP_W, HEADS], [1, T]])


def build(nc, x_in, weights, vecs, consts, rel_bias, buckets, w_gates, pool_w, bst, cst, scratch, out):
    ctx = ExitStack()
    with ctx:
        def sem(name):
            return ctx.enter_context(nc.semaphore(name))

        def chunks(ap, n=None):
            return ap.rearrange("p (a n) -> p a n", n=n or T)

        def at(buf, i):
            return buf[:, bass.ds(i, 1), :].rearrange("p a n -> p (a n)")

        base = (nc.sbuf_base + 31) // 32 * 32
        X, XH, XL, HF, MIX = 0, 4096, 8192, 12288, 16384
        RAW = MIX + 24576
        WH, WL = RAW + RING * SLOT, RAW + RING * SLOT + 2 * SLOT
        REST = WL + 2 * SLOT

        def place(name, col, cols, dtype=F32):
            return nc.alloc_sbuf_tensor_at(name + "_sb", [P, cols], dtype, offset=base + 4 * col)

        x = chunks(place("x", X, 4096)[:, :])
        xh = chunks(place("xh", XH, 4096, F32R)[:, :])
        xl = chunks(place("xl", XL, 4096, F32R)[:, :])
        xs = place("xs", XH, 8192)
        xh_f = xh.bitcast(F32)
        sq = chunks(xs[:, 0:4096])
        hf_f = place("hf", HF, 4096)
        hf = chunks(hf_f[:, :])
        mix = place("mix", MIX, 24576)
        hh = chunks(place("hh", MIX, KF * T, F32R)[:, :])
        hl = chunks(place("hl", MIX + KF * T, KF * T, F32R)[:, :])
        raw = chunks(place("raw", RAW, RING * SLOT)[:, :], SLOT)
        wh = chunks(place("wh", WH, 2 * SLOT, F32R)[:, :], SLOT)
        wl = chunks(place("wl", WL, 2 * SLOT, F32R)[:, :], SLOT)
        wh_f, hh_f = wh.bitcast(F32), hh.bitcast(F32)
        rest = [REST]

        def sb(name, cols):
            rest[0] += cols
            return place(name, rest[0] - cols, cols)

        cst_sb = sb("consts", NCONST)
        vec = sb("vecs", (NVEC + 7) // 8 * 8)[:, 0:NVEC]
        rstd = sb("rstd", T)
        std = sb("std", T)
        acc = sb("acc", T)
        small = sb("small", 320)
        wg = sb("wg", KD * 2 * HEADS)
        pw = sb("pw", T)
        sg = hf[:, 0:2, :]
        ht = hf[:, 2:4, :]
        ident = cst_sb[:, C_ID:C_ID + P]
        negtri = cst_sb[:, C_TRI:C_TRI + P]
        ones = cst_sb[:, C_ONE:C_ONE + P]
        negones = sb("negones", P)
        eps = sb("eps", 8)

        def region(start, n):
            return mix[:, start:start + n]

        mix_sq = chunks(region(0, KD * T))
        qkT = chunks(region(0, 16 * T))
        va = chunks(region(8192, 4 * T))
        vd = chunks(region(10240, 4 * T))
        strip = chunks(region(12288, HEADS * T))
        mqk = chunks(region(0, 16 * T))
        mv = region(8192, 4 * D).rearrange("p (a n) -> p a n", n=D)
        sigo = chunks(region(12288, KD * T))
        uin = chunks(region(0, 8 * T))
        zin = chunks(region(4096, 8 * T))
        cosT = chunks(region(8192, 16 * T))
        sinT = chunks(region(16384, 16 * T))
        gpad = region(0, KD * (T + PAD)).rearrange("p (a n) -> p a n", n=T + PAD)
        cc = chunks(region(4608, KD * T))
        zz = chunks(region(8704, KD * T))

        banks = ctx.enter_context(nc.psum_tensor("banks", [P, 8, T], F32))
        lin = [banks[:, i, :] for i in range(4)]
        ps_n = banks[:, 7, :]

        w_loaded = [sem(f"w_loaded{i}") for i in range(RING)]
        blocks_done = sem("blocks_done")
        tiles_freed = sem("tiles_freed")
        gate_act = sem("gate_act")
        in_loaded = sem("in_loaded")
        squares = sem("squares")
        sumsq_ready = sem("sumsq_ready")
        acc_ready = sem("acc_ready")
        branch_sq = sem("branch_sq")
        gate_scaled = sem("gate_scaled")
        up_scaled = sem("up_scaled")
        g_mul = sem("g_mul")
        tap_prod = sem("tap_prod")
        tap_sum = sem("tap_sum")
        std_ready = sem("std_ready")
        rstd_ready = sem("rstd_ready")
        xn_ready = sem("xn_ready")
        scaled = sem("scaled")
        x_ready = sem("x_ready")
        prep = sem("prep")
        prep_act = sem("prep_act")
        prep_pe = sem("prep_pe")
        strip_line = sem("strip_line")
        strip_out = sem("strip_out")
        strip_in = sem("strip_in")
        out_done = sem("out_done")
        pool_turn = sem("pool_turn")
        tab = sem("tab")
        w_hi = sem("w_hi")
        w_split = sem("w_split")
        t_ready = sem("t_ready")
        hi_ready = sem("hi_ready")
        h_hi = sem("h_hi")
        h_lo = sem("h_lo")
        a_oh = sem("a_oh")
        m_hh = sem("m_hh")
        m_out = sem("m_out")
        tab_act = sem("tab_act")
        a_abs = sem("a_abs")
        a_ex = sem("a_ex")
        a_exp = sem("a_exp")
        a_ln = sem("a_ln")
        a_mx = sem("a_mx")
        a_odl = sem("a_odl")
        a_oev = sem("a_oev")
        a_oev2 = sem("a_oev2")
        a_osb = sem("a_osb")
        a_p = sem("a_p")
        a_rc = sem("a_rc")
        a_rl = sem("a_rl")
        a_s = sem("a_s")
        a_sadd = sem("a_sadd")
        a_sp = sem("a_sp")
        a_spr = sem("a_spr")
        a_staged = sem("a_staged")
        a_t = sem("a_t")
        a_tc = sem("a_tc")
        a_w = sem("a_w")
        a_vst = sem("a_vst")
        a_wm = sem("a_wm")
        a_z = sem("a_z")
        conv_act = sem("conv_act")
        conv_v = sem("conv_v")
        e_bb = sem("e_bb")
        e_btc = sem("e_btc")
        e_loaded = sem("e_loaded")
        e_pm = sem("e_pm")
        e_pool = sem("e_pool")
        e_sig = sem("e_sig")
        e_t = sem("e_t")
        e_w2 = sem("e_w2")
        e_win = sem("e_win")
        g_act = sem("g_act")
        g_chain = sem("g_chain")
        g_cols = sem("g_cols")
        g_pe = sem("g_pe")
        g_rows = sem("g_rows")
        g_vec = sem("g_vec")
        halved = sem("halved")
        iota_ready = sem("iota_ready")
        m_d = sem("m_d")
        m_d2 = sem("m_d2")
        m_dm = sem("m_dm")
        m_dn = sem("m_dn")
        m_eb = sem("m_eb")
        m_ebc = sem("m_ebc")
        m_fin = sem("m_fin")
        m_hid = sem("m_hid")
        m_mb = sem("m_mb")
        m_nd = sem("m_nd")
        m_p = sem("m_p")
        m_pm = sem("m_pm")
        m_rec = sem("m_rec")
        m_s = sem("m_s")
        m_sqr = sem("m_sqr")
        m_ss = sem("m_ss")
        m_staged = sem("m_staged")
        m_std = sem("m_std")
        m_var = sem("m_var")
        o_cen = sem("o_cen")
        o_conv = sem("o_conv")
        o_n = sem("o_n")
        o_s = sem("o_s")
        o_sum = sem("o_sum")
        o_v = sem("o_v")
        prep_exp = sem("prep_exp")
        prep_x = sem("prep_x")
        s_bu = sem("s_bu")
        s_buc = sem("s_buc")
        s_pr = sem("s_pr")
        s_rot = sem("s_rot")
        s_staged = sem("s_staged")
        s_v = sem("s_v")
        s_y = sem("s_y")
        s_ych = sem("s_ych")
        s_ym = sem("s_ym")
        s_cs = sem("s_cs")
        m_kv = sem("m_kv")
        tab_v = sem("tab_v")

        norm_no = {n: i for i, n in enumerate(NORMS)}
        pre_no = {n: i for i, n in enumerate(PRE)}
        POSTS = ["ffn0", "attn", "ffn1", "ffn2", "mlstm", "ffn3"]
        FREE0 = 4

        def g_of(name, c):
            col = GCOL[name] + c
            return vec[:, col:col + 1]

        def high_part(act, name, s, k=0):
            if isinstance(k, int) and BLK[name] + k + s + 2 >= BLOCKS:
                return
            act.wait_ge(w_loaded[(s + 2) % RING], 16 * (BLK[name] // RING + (s + 2) // RING + 1) + 4 * k)
            act.wait_ge(blocks_done, BLK[name] + s + 1 + k)
            act.activation(wh[:, s % 2, :], raw[:, (s + 2) % RING, :], ACT.Copy).then_inc(w_hi, 1)

        def low_part(pool, name, s, k=0):
            if isinstance(k, int) and BLK[name] + k + s + 2 >= BLOCKS:
                return
            pool.wait_ge(w_hi, BLK[name] + s + 3 + k)
            pool.tensor_tensor(wl[:, s % 2, :], raw[:, (s + 2) % RING, :], wh_f[:, s % 2, :],
                               ALU.subtract).then_inc(w_split, 1)

        def first_parts(eng, low):
            for s in range(2):
                if low:
                    eng.wait_ge(w_hi, s + 1)
                    eng.tensor_tensor(wl[:, s, :], raw[:, s, :], wh_f[:, s, :], ALU.subtract).then_inc(w_split, 1)
                else:
                    eng.wait_ge(w_loaded[s], 16)
                    eng.activation(wh[:, s, :], raw[:, s, :], ACT.Copy).then_inc(w_hi, 1)

        def low_parts(pool, name):
            with pool.Fori(0, NBLK[name] // 4) as i:
                for s in range(4):
                    low_part(pool, name, s, 4 * i)

        def split_high(act, key, n=KD, src=None, order=None):
            for j in range(n):
                c = order[j] if order else j
                act.wait_ge(t_ready, TNO[key] + j + 1)
                act.activation(xh[:, c, :], (hf if src is None else src)[:, c, :], ACT.Copy).then_inc(hi_ready, 1)

        def split_low(pool, key, n=KD, src=None, order=None):
            for j in range(n):
                c = order[j] if order else j
                pool.wait_ge(hi_ready, SPLIT[key] + j + 1)
                pool.tensor_tensor(xl[:, c, :], (hf if src is None else src)[:, c, :], xh_f[:, c, :],
                                   ALU.subtract).then_inc(xn_ready, 1)

        DT, XR, PHI, R_, EM, SER, MASK, E1, SI, S2, CO, NR, NI, KRE, KIM, DEN, TA, TB = range(0, 288, 16)
        NMX, LSUM, RL = 288, 296, 304

        def col(c, n=16):
            return small[:, c:c + n]

        lines = region(0, HEADS * STRIP_W).rearrange("p (h n) -> p h n", n=STRIP_W)
        bk = region(5120, 640)
        rb = region(5760, 8)
        rb8 = region(5768, 1024).rearrange("p (h n) -> p h n", n=P)
        LB = NB_BUCKETS + 1

        def prep_tensor(pe):
            pe.wait_ge(prep, 2)
            for hh in range(HEADS):
                if hh >= 2:
                    pe.wait_ge(prep_act, hh - 1)
                for half in range(2):
                    last = pe.matmul(banks[:, 4 + 2 * (hh % 2) + half, 0:320], rb8[0:LB, hh, :],
                                     bk[0:LB, 320 * half:320 * half + 320], start=True, stop=True)
                last.then_inc(prep_pe, 1)

        def prep_scalar(act, split_x):
            act.dma_start(bk[0:LB, :], buckets).then_inc(strip_line, 16)
            act.dma_start(rb[0:NB_BUCKETS, :], rel_bias).then_inc(strip_line, 16)
            act.dma_start(wg[:, :], w_gates).then_inc(strip_line, 16)
            act.dma_start(pw[:, :], pool_w).then_inc(strip_line, 16)
            first_parts(act, False)
            act.wait_ge(in_loaded, 48)
            act.activation(std[:, 0:1], vec[:, 0:1], ACT.Copy).then_inc(a_w, 1)
            act.activation(std[:, 1:2], vec[:, 0:1], ACT.Copy).then_inc(a_oev, 1)
            act.activation(std[:, 2:3], vec[:, 0:1], ACT.Copy).then_inc(a_oev2, 1)
            act.activation(std[:, 3:4], vec[:, 0:1], ACT.Copy).then_inc(a_tc, 1)
            act.activation(std[:, 4:5], vec[:, 0:1], ACT.Copy).then_inc(m_ebc, 1)
            act.activation(std[:, 5:6], vec[:, 0:1], ACT.Copy).then_inc(m_sqr, 1)
            act.activation(std[:, 6:7], vec[:, 0:1], ACT.Copy).then_inc(s_buc, 1)
            split_x()
            for hh in range(HEADS):
                act.wait_ge(prep_pe, hh + 1)
                act.activation(lines[:, hh, :].rearrange("p (a n) -> p a n", a=2),
                               banks[:, 4 + 2 * (hh % 2):6 + 2 * (hh % 2), 0:320], ACT.Copy).then_inc(prep_act, 1)
            act.wait_ge(prep_act, HEADS)
            act.dma_start(scratch, region(0, HEADS * STRIP_W)).then_inc(strip_out, 16)
            act.activation(col(DT), vec[:, VEC["log_dt"]:VEC["log_dt"] + 16], ACT.Exp).then_inc(prep_exp, 1)
            act.wait_ge(strip_out, 16)
            act.wait_ge(prep_x, 1)
            act.activation(col(E1), col(XR), ACT.Exp).then_inc(prep_exp, 1)
            act.activation(col(SI), col(PHI), ACT.Sin, scale=TWO_PI).then_inc(prep_exp, 1)
            act.activation(col(S2), col(PHI), ACT.Sin, scale=TWO_PI / 2).then_inc(prep_exp, 1)

        def prep_vector(dve, split_x):
            chain = [0]

            def link(ins):
                chain[0] += 1
                ins.then_inc(prep, 1)
                dve.wait_ge(prep, chain[0])

            link(dve.memset(rb[NB_BUCKETS:LB, :], 1.0))
            dve.wait_ge(strip_line, 64)
            link(dve.tensor_copy(rb8[0:LB, :, :], rb[0:LB, :].unsqueeze(2).to_broadcast([LB, HEADS, P])))
            dve.memset(eps[:, 0:1], EPS_RMS)
            dve.memset(eps[:, 1:2], EPS_LN)
            dve.memset(negones[:, :], -1.0).then_inc(tiles_freed, FREE0)
            dve.memset(rstd[:, 0:1], 0.0).then_inc(a_sadd, 2)
            dve.memset(rstd[:, 1:2], 0.0).then_inc(m_dm, 1)
            dve.memset(rstd[:, 2:3], 0.0).then_inc(m_p, 1)
            dve.memset(rstd[:, 3:4], 0.0).then_inc(m_dn, 1)
            dve.memset(rstd[:, 4:5], 0.0).then_inc(m_hid, 2)
            dve.memset(rstd[:, 5:6], 0.0).then_inc(s_rot, 2)
            dve.memset(rstd[:, 7:8], 0.0).then_inc(a_t, 2)
            dve.memset(rstd[:, 8:9], 0.0).then_inc(conv_act, 2)
            dve.memset(rstd[:, 11:12], 0.0).then_inc(h_lo, 2)
            dve.memset(rstd[:, 12:13], 0.0).then_inc(tap_sum, 1)
            dve.memset(rstd[:, 9:10], 0.0).then_inc(s_pr, 4)
            dve.memset(rstd[:, 10:11], 0.0).then_inc(s_ym, 2)
            dve.memset(rstd[:, 6:7], 0.0).then_inc(s_ych, 1)
            dve.wait_ge(in_loaded, 48)
            split_x()
            for c in (8, 40, 56, 88):
                dve.tensor_scalar(vec[:, c:c + 8], vec[:, c:c + 8], 0.5, None, ALU.mult).then_inc(halved, 1)
            dve.wait_ge(halved, 4)
            are, aim = (vec[:, VEC[n]:VEC[n] + 16] for n in ("a_re", "a_im"))
            tt = dve.tensor_tensor
            ts = dve.tensor_scalar
            dve.wait_ge(prep_exp, 1)
            link(tt(col(XR), are, col(DT), ALU.mult))
            link(tt(col(TA), aim, col(DT), ALU.mult))
            link(ts(col(TA), col(TA), float(1 / (2 * np.pi)), None, ALU.mult))
            link(ts(col(TB), col(TA), ROUND, ROUND, ALU.add, ALU.subtract))
            tt(col(PHI), col(TA), col(TB), ALU.subtract).then_inc(prep_x, 1)
            dve.wait_ge(prep_x, 1)
            link(ts(col(TA), col(XR), 0.5, -0.5, ALU.min, ALU.max))
            link(dve.memset(col(SER), 1.0))
            for k in range(9, 1, -1):
                link(dve.scalar_tensor_tensor(col(SER), col(SER), 1.0 / k, col(TA), ALU.mult, ALU.mult))
                link(ts(col(SER), col(SER), 1.0, None, ALU.add))
            link(tt(col(SER), col(SER), col(TA), ALU.mult))
            link(tt(col(MASK), col(TA), col(XR), ALU.is_equal))
            link(tt(col(SER), col(SER), col(MASK), ALU.mult))
            link(ts(col(MASK), col(MASK), -1.0, 1.0, ALU.mult, ALU.add))
            dve.wait_ge(prep_exp, 4)
            link(ts(col(E1), col(E1), -1.0, None, ALU.add))
            link(tt(col(E1), col(E1), col(MASK), ALU.mult))
            link(tt(col(EM), col(E1), col(SER), ALU.add))
            link(ts(col(R_), col(EM), 1.0, None, ALU.add))
            link(tt(col(S2), col(S2), col(S2), ALU.mult))
            link(ts(col(CO), col(S2), -2.0, 1.0, ALU.mult, ALU.add))
            link(tt(col(NR), col(EM), col(CO), ALU.mult))
            link(dve.scalar_tensor_tensor(col(NR), col(S2), -2.0, col(NR), ALU.mult, ALU.add))
            link(tt(col(NI), col(R_), col(SI), ALU.mult))
            link(tt(col(DEN), are, are, ALU.mult))
            link(tt(col(TA), aim, aim, ALU.mult))
            link(tt(col(DEN), col(DEN), col(TA), ALU.add))
            link(dve.reciprocal(col(DEN), col(DEN)))
            link(tt(col(TA), col(NR), are, ALU.mult))
            link(tt(col(TB), col(NI), aim, ALU.mult))
            link(tt(col(TA), col(TA), col(TB), ALU.add))
            link(tt(col(KRE), col(TA), col(DEN), ALU.mult))
            link(tt(col(TA), col(NI), are, ALU.mult))
            link(tt(col(TB), col(NR), aim, ALU.mult))
            link(tt(col(TA), col(TA), col(TB), ALU.subtract))
            link(tt(col(KIM), col(TA), col(DEN), ALU.mult))

        def evac(eng, name, n, fn):
            with eng.Fori(0, n // 4) as i:
                for m in range(4):
                    high_part(eng, name, m, 4 * i)
                    fn(i, m).then_inc(tiles_freed, 1)

        qp, kp, vp, qdp, kdp, vdp = (region(16384 + T * j, T) for j in range(6))
        wk = [region(19456 + PACKED * e, PACKED) for e in range(2)]
        ab = [region(22016 + PACKED * e, PACKED) for e in range(2)]
        sp_ = ab
        pT = [hf_f[:, PACKED * e:PACKED * (e + 1)] for e in range(2)]
        ssb = [hf_f[:, 2560 + T * j:3072 + T * j] for j in range(2)]
        Z01 = banks[:, 0, :]
        Z23 = banks[:, 1:3, 0:384]

        def zcols(kb):
            return (banks[:, 0, :], banks[:, 1, 0:384], banks[:, 2, 0:256], banks[:, 2, 256:384])[kb]

        def packed(buf, kb):
            return buf[:, OFF[kb]:OFF[kb] + T - P * kb]

        def two(buf):
            return buf[:, 0:T], buf[:, T:PACKED].rearrange("p (a n) -> p a n", a=2)

        def attention_in_scalar(act):
            for c in range(16):
                high_part(act, "attn.qk", c % 4, c - c % 4)
                act.activation(qkT[:, c, :], lin[c % 4], ACT.Copy,
                               scale=0.125 if c // 4 % 2 == 0 else 1.0).then_inc(tiles_freed, 1)
            for half, dst in enumerate((va, vd)):
                for s in range(4):
                    high_part(act, "attn.v", s, 4 * half)
                for t in range(4):
                    act.activation(dst[:, t, :], lin[t], ACT.Copy).then_inc(tiles_freed, 1)

        def attention_pool(pool):
            low_parts(pool, "attn.qk")
            low_parts(pool, "attn.v")
            with pool.Fori(0, 4) as i:
                for e in range(2):
                    for buf, signal, done, base in ((sp_[e], a_spr, a_sp, 1), (wk[e], a_w, a_wm, 2)):
                        pool.wait_ge(signal, 2 * i + e + base)
                        pool.sem_inc(pool_turn, 1)
                        for kb in range(4):
                            d = buf[:, OFF[kb]:OFF[kb] + P]
                            last = pool.affine_select(out=d, in_=d, pattern=[[1, P]], compare_op=ALU.is_gt,
                                                      fill=0.0, base=0, channel_multiplier=-1)
                        last.then_inc(done, 1)

        def attention_tensor(pe):
            with pe.Fori(0, 4) as i:
                for e in range(2):
                    rows = slice(64 * e, 64 * e + 64)
                    u = 2 * i + e

                    def scores(qb):
                        pe.wait_ge(a_sadd, 4 * u + qb + 1)
                        pe.matmul(banks[:, 3 + qb % 2, 0:P * (qb + 1)], qdp[rows, P * qb:P * (qb + 1)],
                                  kdp[rows, 0:P * (qb + 1)], start=True, stop=True).then_inc(a_s, 1)

                    def turn(qb):
                        pe.wait_ge(a_p, 4 * u + qb + 1)
                        pe.wait_ge(a_tc, 4 * u + qb + 1)
                        for kb in range(qb + 1):
                            last = pe.transpose(banks[:, 5, P * kb:P * (kb + 1)],
                                                ssb[qb % 2][:, P * kb:P * (kb + 1)], ident)
                        last.then_inc(a_t, 1)

                    if e == 0:
                        pe.wait_ge(a_staged, i + 1)
                    pe.wait_ge(a_w, u + 1)
                    for kb in range(4):
                        last = pe.matmul(zcols(kb), kp[rows, P * kb:P * (kb + 1)], qp[rows, P * kb:T],
                                         start=(kb != 3), stop=False, skip_group_check=True)
                    last.then_inc(a_z, 1)
                    scores(0)
                    scores(1)
                    pe.wait_ge(a_sp, u + 1)
                    for kb in range(4):
                        dst = zcols(kb)
                        last = pe.matmul(dst, negtri, packed(sp_[e], kb), start=False, stop=(kb == 3),
                                         skip_group_check=True)
                        for later in range(kb + 1, 4):
                            last = pe.matmul(dst[:, P * (later - kb):T - P * kb], negones[:, :],
                                             packed(sp_[e], later), start=False, stop=True,
                                             skip_group_check=True)
                    last.then_inc(a_rc, 1)
                    turn(0)
                    scores(2)
                    turn(1)
                    scores(3)
                    turn(2)
                    pe.wait_ge(a_wm, u + 1)
                    pe.wait_ge(a_vst, i + 1)
                    if e == 0:
                        pe.wait_ge(a_oev, i + 1)
                    for kb in range(4):
                        last = pe.matmul(banks[rows, 6, P * kb:T], vp[:, P * kb + 64 * e:P * kb + 64 * e + 64],
                                         packed(wk[e], kb), start=(kb == 0), stop=(kb == 3),
                                         skip_group_check=True)
                    last.then_inc(a_osb, 1)
                    turn(3)
                    pe.wait_ge(a_tc, 4 * u + 5)
                    if e == 0:
                        pe.wait_ge(a_oev2, i + 1)
                    for kb in range(4):
                        last = pe.matmul(banks[rows, 7, P * kb:T], vdp[:, P * kb + 64 * e:P * kb + 64 * e + 64],
                                         packed(pT[e], kb), start=(kb == 0), stop=(kb == 3),
                                         skip_group_check=True)
                    last.then_inc(a_odl, 1)
            pe.wait_ge(a_oev, 5)
            pe.wait_ge(a_oev2, 5)

        def attention_scalar(act):
            with act.Fori(0, 4) as i:
                for e in range(2):
                    u = 2 * i + e

                    def exps(qb):
                        act.wait_ge(a_mx, 4 * u + qb + 1)
                        n = P * (qb + 1)
                        act.activation(ssb[qb % 2][:, 0:n], ssb[qb % 2][:, 0:n], ACT.Exp,
                                       bias=small[:, NMX + qb:NMX + qb + 1],
                                       accum_out=small[:, LSUM + qb:LSUM + qb + 1]).then_inc(a_exp, 1)

                    def copy_turned(qb):
                        act.wait_ge(a_t, 4 * u + qb + 3)
                        for kb in range(qb + 1):
                            o = OFF[kb] + P * (qb - kb)
                            last = act.activation(pT[e][:, o:o + P], banks[:, 5, P * kb:P * (kb + 1)], ACT.Copy)
                        last.then_inc(a_tc, 1)

                    act.wait_ge(a_z, u + 1)
                    act.activation(two(ab[e])[0], Z01, ACT.Abs)
                    act.activation(two(ab[e])[1], Z23, ACT.Abs).then_inc(a_abs, 1)
                    act.wait_ge(a_abs, u + 1)
                    act.activation(ab[e], ab[e], ACT.Exp, scale=-1.0).then_inc(a_ex, 1)
                    act.wait_ge(a_ex, u + 1)
                    act.activation(ab[e], ab[e], ACT.Ln, bias=1.0).then_inc(a_ln, 1)
                    exps(0)
                    exps(1)
                    act.wait_ge(a_rc, u + 1)
                    act.activation(two(wk[e])[0], Z01, ACT.Exp)
                    act.activation(two(wk[e])[1], Z23, ACT.Exp).then_inc(a_w, 1)
                    copy_turned(0)
                    exps(2)
                    copy_turned(1)
                    exps(3)
                    copy_turned(2)
                    copy_turned(3)
                act.wait_ge(a_osb, 2 * i + 2)
                act.activation(at(xh, i), banks[:, 6, :], ACT.Copy).then_inc(a_oh, 1)
                act.wait_ge(a_odl, 2 * i + 2)
                act.activation(at(xh, i + 4), banks[:, 7, :], ACT.Copy).then_inc(a_oh, 1)

        def attention_vector(dve):
            dve.wait_ge(strip_in, 16)
            dve.wait_ge(tiles_freed, FREE0 + TILE["attn.v"] + 8)
            with dve.Fori(0, 4) as i:
                dve.tensor_copy(qp, at(qkT, i))
                dve.tensor_copy(kp, at(qkT, i + 4))
                dve.tensor_copy(qdp, at(qkT, i + 8))
                dve.tensor_copy(kdp, at(qkT, i + 12)).then_inc(a_staged, 1)
                dve.tensor_copy(vp.rearrange("p (a n) -> p a n", a=4), va[:, :, bass.ds(P * i, P)])
                dve.tensor_copy(vdp.rearrange("p (a n) -> p a n", a=4),
                                vd[:, :, bass.ds(P * i, P)]).then_inc(a_vst, 1)
                for e in range(2):
                    u = 2 * i + e

                    def add_bias(qb):
                        n = P * (qb + 1)
                        dve.wait_ge(a_s, 4 * u + qb + 1)
                        dve.wait_ge(a_t, 4 * u + qb + 1)
                        dve.tensor_tensor(ssb[qb % 2][:, 0:n], banks[:, 3 + qb % 2, 0:n],
                                          strip[:, bass.ds(u, 1), T - n:T].rearrange("p a n -> p (a n)"),
                                          ALU.add).then_inc(a_sadd, 1)
                        dve.wait_ge(a_sadd, 4 * u + qb + 3)
                        dve.tensor_reduce(small[:, NMX + qb:NMX + qb + 1], ssb[qb % 2][:, 0:n], AX.X, ALU.max,
                                          negate=True).then_inc(a_mx, 1)

                    def normalise(qb):
                        n = P * (qb + 1)
                        dve.wait_ge(a_exp, 4 * u + qb + 1)
                        dve.reciprocal(small[:, RL + qb:RL + qb + 1],
                                       small[:, LSUM + qb:LSUM + qb + 1]).then_inc(a_rl, 1)
                        dve.wait_ge(a_rl, 4 * u + qb + 1)
                        dve.tensor_scalar(ssb[qb % 2][:, 0:n], ssb[qb % 2][:, 0:n],
                                          small[:, RL + qb:RL + qb + 1], None, ALU.mult).then_inc(a_p, 1)

                    add_bias(0)
                    dve.wait_ge(a_ln, u + 1)
                    dve.scalar_tensor_tensor(two(sp_[e])[0], Z01, 0.0, two(ab[e])[0], ALU.max, ALU.add)
                    dve.scalar_tensor_tensor(two(sp_[e])[1], Z23, 0.0, two(ab[e])[1], ALU.max,
                                             ALU.add).then_inc(a_spr, 1)
                    add_bias(1)
                    normalise(0)
                    normalise(1)
                    add_bias(2)
                    normalise(2)
                    add_bias(3)
                    normalise(3)
                for o, ev in ((0, a_oev), (1, a_oev2)):
                    dve.wait_ge(a_oh, 2 * i + o + 1)
                    dve.tensor_tensor(at(xl, i + 4 * o), banks[:, 6 + o, :], at(xh_f, i + 4 * o),
                                      ALU.subtract).then_inc(ev, 1)

        c_row, m_row, e_row = (region(16384 + T * j, T)[0:HEADS, :] for j in range(3))
        i_row, f_row, cum, one_row = (region(17920 + T * j, T)[0:HEADS, :] for j in range(4))
        dm = [region(17920 + PACKED * e, PACKED) for e in range(2)]
        pm = dm
        ms_k = [region(20480 + T * e, T) for e in range(2)]
        ms_v = [region(21504 + T * e, T) for e in range(2)]
        num_sb = [region(22528 + T * e, T) for e in range(2)]
        num_sq = [region(23552 + T * e, T) for e in range(2)]
        cbuf = [hf[:, j, :] for j in range(2)]
        ms_sel = [hf_f[0:HEADS, P * e:P * (e + 1)] for e in range(2)]
        ccols_f = hf_f[:, 256:288]
        ccols = ccols_f.rearrange("p (s h) -> p s h", h=HEADS)
        ms_c = [hf_f[:, 288 + 4 * e:292 + 4 * e] for e in range(2)]
        ms_g = [hf_f[:, 296 + e:297 + e] for e in range(2)]
        dn = [hf[:, 2 + e, :] for e in range(2)]
        fac = [hf[:, 4 + e, :] for e in range(2)]

        def gates_tensor(pe):
            pe.wait_ge(strip_line, 64)
            for g in range(2):
                for k in range(KD):
                    if g == 0:
                        pe.wait_ge(t_ready, TNO["mlstm"] + k + 1)
                    last = pe.matmul(banks[0:HEADS, 4 + g, :], wg[:, 2 * HEADS * k + HEADS * g:
                                                                 2 * HEADS * k + HEADS * (g + 1)],
                                     hf[:, k, :], start=(k == 0), stop=(k == KD - 1))
            last.then_inc(g_pe, 1)

        def mlstm_tensor(pe):
            pe.wait_ge(g_rows, 1)
            for s in range(4):
                last = pe.transpose(banks[:, 6, HEADS * s:HEADS * (s + 1)], c_row[:, P * s:P * (s + 1)],
                                    ident[0:HEADS, 0:HEADS])
            last.then_inc(g_pe, 1)
            pe.wait_ge(g_cols, 1)
            pe.wait_ge(tiles_freed, FREE0 + TILE["mlstm.o"] + 8)
            with pe.Fori(0, 4) as i:
                def first(e):
                    u = 2 * i + e
                    pe.wait_ge(m_staged, u + 1)
                    pe.wait_ge(m_dm, u + 1)
                    pe.matmul(banks[:, 3, :], ms_sel[e], m_row, start=True, stop=True).then_inc(m_mb, 1)
                    pe.wait_ge(m_p, u + 1)
                    pe.wait_ge(m_kv, u + 1)
                    for kb in range(4):
                        last = pe.matmul(zcols(kb), ms_k[e][:, P * kb:P * (kb + 1)],
                                         mqk[:, bass.ds(u, 1), P * kb:T].rearrange("p a n -> p (a n)"),
                                         start=(kb != 3), stop=True, skip_group_check=True)
                    last.then_inc(m_s, 1)
                    pe.wait_ge(m_ebc, u + 1)
                    pe.matmul(banks[:, 4, :], ms_sel[e], e_row, start=True, stop=True).then_inc(m_eb, 1)

                def second(e):
                    u = 2 * i + e
                    pe.wait_ge(m_pm, u + 1)
                    pe.wait_ge(m_sqr, u + 1)
                    pe.wait_ge(m_dn, u + 1)
                    for kb in range(4):
                        pe.matmul(banks[:, 5, P * kb:T], ms_v[e][:, P * kb:P * (kb + 1)], packed(pm[e], kb),
                                  start=(kb == 0), stop=(kb == 3), skip_group_check=True)
                    for kb in range(4):
                        last = pe.matmul(banks[:, 6, P * kb:T], ones, packed(pm[e], kb),
                                         start=(kb == 0), stop=(kb == 3), skip_group_check=True)
                    last.then_inc(m_nd, 1)
                    pe.wait_ge(m_sqr, u + 2)
                    pe.matmul(ps_n, ones, num_sq[e], start=True, stop=True).then_inc(m_ss, 1)

                first(0)
                first(1)
                second(0)
                pe.wait_ge(m_var, 2 * i + 1)
                second(1)
                pe.wait_ge(m_var, 2 * i + 2)
            pe.wait_ge(m_hid, 10)

        def mlstm_scalar(act):
            act.wait_ge(g_vec, 1)
            act.activation(e_row, f_row, ACT.Abs).then_inc(g_act, 1)
            act.wait_ge(g_act, 1)
            act.activation(e_row, e_row, ACT.Exp, scale=-1.0).then_inc(g_act, 1)
            act.wait_ge(g_act, 2)
            act.activation(e_row, e_row, ACT.Ln, bias=1.0).then_inc(g_act, 1)
            act.wait_ge(g_vec, 2)
            act.activation(e_row, e_row, ACT.Exp, scale=-1.0).then_inc(g_act, 1)
            with act.Fori(0, 4) as i:
                for m in range(4):
                    high_part(act, "mlstm.qk", m, 4 * i)
                    act.wait_ge(tiles_freed, FREE0 + TILE["mlstm.qk"] + 4 * i + m + 1)
                    act.activation(at(mqk, 4 * i + m), cbuf[m % 2], ACT.Silu).then_inc(conv_act, 1)
            for half in range(2):
                for s in range(4):
                    high_part(act, "mlstm.v", s, 4 * half)
                for t in range(4):
                    act.activation(mv[:, t, T * half:T * (half + 1)], lin[t], ACT.Copy).then_inc(tiles_freed, 1)
            evac(act, "mlstm.o", 8, lambda i, m: act.activation(at(sigo, 4 * i + m), lin[m], ACT.Sigmoid))
            with act.Fori(0, 4) as i:
                for e in range(2):
                    u = 2 * i + e
                    act.wait_ge(m_hid, u + 1)
                    act.activation(ms_k[e], at(mqk, u + 8), ACT.Copy)
                    act.activation(ms_v[e].rearrange("p (a n) -> p a n", a=4), mv[:, :, bass.ds(P * u, P)],
                                   ACT.Copy).then_inc(m_kv, 1)
                for e in range(2):
                    u = 2 * i + e
                    act.wait_ge(m_dm, u + 2)
                    act.activation(dm[e], dm[e], ACT.Exp, scale=-1.0).then_inc(m_d, 1)
                    act.wait_ge(m_eb, u + 1)
                    act.activation(dn[e], banks[:, 4, :], ACT.Copy).then_inc(m_ebc, 1)
                for e in range(2):
                    u = 2 * i + e
                    act.wait_ge(m_nd, u + 1)
                    act.activation(fac[e], banks[:, 6, :], ACT.Abs)
                    act.activation(num_sb[e], banks[:, 5, :], ACT.Copy)
                    act.activation(num_sq[e], banks[:, 5, :], ACT.Square).then_inc(m_sqr, 1)
                for e in range(2):
                    act.wait_ge(m_var, 2 * i + e + 1)
                    act.activation(fac[e], fac[e], ACT.Sqrt).then_inc(m_std, 1)
                for e in range(2):
                    act.wait_ge(m_out, 2 * i + e + 1)
                    act.activation(at(xh, 2 * i + e), fac[e], ACT.Copy).then_inc(m_hh, 1)

        def mlstm_vector(dve):
            tt, ts, stt = dve.tensor_tensor, dve.tensor_scalar, dve.scalar_tensor_tensor
            chain = [0]

            def link(ins):
                chain[0] += 1
                ins.then_inc(g_chain, 1)
                dve.wait_ge(g_chain, chain[0])

            dve.wait_ge(g_pe, 1)
            dve.memset(one_row, 1.0)
            link(ts(i_row, banks[0:HEADS, 4, :], vec[0:HEADS, VEC["b_i"]:VEC["b_i"] + 1], None, ALU.add))
            ts(f_row, banks[0:HEADS, 5, :], vec[0:HEADS, VEC["b_f"]:VEC["b_f"] + 1], None,
               ALU.add).then_inc(g_vec, 1)
            dve.wait_ge(g_act, 3)
            link(stt(f_row, f_row, 0.0, e_row, ALU.min, ALU.subtract))
            link(dve.tensor_tensor_scan(cum, one_row, f_row, 0.0, ALU.mult, ALU.add))
            tt(c_row, i_row, cum, ALU.subtract).then_inc(g_rows, 1)
            dve.wait_ge(g_rows, 1)
            link(dve.tensor_tensor_scan(m_row, c_row, c_row, 0.0, ALU.max, ALU.max))
            tt(e_row, cum, m_row, ALU.add).then_inc(g_vec, 1)
            dve.wait_ge(g_act, 4)
            ts(e_row, e_row, 3e38, None, ALU.min).then_inc(g_cols, 1)
            mc = VEC["mconv_w"]
            with dve.Fori(0, 4) as i:
                for m in range(4):
                    dve.wait_ge(blocks_done, BLK["mlstm.qk"] + 4 * i + m + 1)
                    dve.wait_ge(conv_act, 4 * i + m + 1)
                    c = cbuf[m % 2]
                    w = lambda tap: vec[:, bass.ds(16 * i + (mc + 4 * m + tap), 1)]
                    ts(c, lin[m], w(3), None, ALU.mult).then_inc(conv_v, 1)
                    for tap in (2, 1, 0):
                        d = 3 - tap
                        dve.wait_ge(conv_v, 12 * i + 3 * m + d)
                        last = stt(c[:, d:T], lin[m][:, 0:T - d], w(tap), c[:, d:T], ALU.mult, ALU.add)
                        last.then_inc(conv_v if tap > 0 else tiles_freed, 1)
            dve.wait_ge(g_pe, 2)
            dve.tensor_copy(ccols_f, banks[:, 6, 0:32]).then_inc(g_cols, 1)
            dve.wait_ge(tiles_freed, FREE0 + TILE["mlstm.o"] + 8)
            with dve.Fori(0, 4) as i:
                for e in range(2):
                    u = 2 * i + e
                    dve.wait_ge(m_mb, u + 1)
                    dve.wait_ge(m_staged, u + 1)
                    for s in range(4):
                        last = ts(packed(dm[e], s), banks[:, 3, P * s:T], ms_c[e][:, s:s + 1], 0.0,
                                  ALU.subtract, ALU.max)
                    last.then_inc(m_dm, 1)
                    dve.wait_ge(m_d, u + 1)
                    dve.wait_ge(m_s, u + 1)
                    stt(two(pm[e])[0], Z01, P ** -0.5, two(dm[e])[0], ALU.mult, ALU.mult)
                    stt(two(pm[e])[1], Z23, P ** -0.5, two(dm[e])[1], ALU.mult, ALU.mult).then_inc(m_p, 1)
                for e in range(2):
                    u = 2 * i + e
                    dve.wait_ge(m_sqr, u + 2)
                    dve.wait_ge(m_ebc, u + 2)
                    tt(dn[e], fac[e], dn[e], ALU.max).then_inc(m_dn, 1)
                    dve.wait_ge(m_dn, u + 2)
                    stt(fac[e], dn[e], EPS_RMS, dn[e], ALU.mult, ALU.mult).then_inc(m_d2, 1)
                    dve.wait_ge(m_d2, u + 1)
                    dve.wait_ge(m_ss, u + 1)
                    stt(fac[e], ps_n, 1.0 / P, fac[e], ALU.mult, ALU.add).then_inc(m_var, 1)
                for e in range(2):
                    u = 2 * i + e
                    dve.wait_ge(m_std, u + 1)
                    dve.reciprocal(fac[e], fac[e]).then_inc(m_rec, 1)
                    dve.wait_ge(m_rec, u + 1)
                    stt(fac[e], num_sb[e], ms_g[e], fac[e], ALU.mult, ALU.mult).then_inc(m_fin, 1)
                    dve.wait_ge(m_fin, u + 1)
                    tt(fac[e], fac[e], at(sigo, u), ALU.mult).then_inc(m_out, 1)

        def mlstm_pool(pool):
            for name in ("mlstm.qk", "mlstm.v", "mlstm.o"):
                low_parts(pool, name)
            pool.wait_ge(tiles_freed, FREE0 + TILE["mlstm.o"] + 8)
            pool.wait_ge(g_cols, 2)
            with pool.Fori(0, 4) as i:
                for e in range(2):
                    u = 2 * i + e
                    pool.wait_ge(m_hid, u + 1)
                    pool.tensor_copy(ms_sel[e], ident[0:HEADS, bass.ds(u, 1)].to_broadcast([HEADS, P]))
                    pool.tensor_copy(ms_c[e].unsqueeze(2), ccols[:, :, bass.ds(u, 1)])
                    pool.tensor_copy(ms_g[e], vec[:, bass.ds(u + VEC["head_g"], 1)]).then_inc(m_staged, 1)
                for e in range(2):
                    pool.wait_ge(m_p, 2 * i + e + 2)
                    pool.sem_inc(pool_turn, 1)
                    for kb in range(4):
                        d = pm[e][:, OFF[kb]:OFF[kb] + P]
                        last = pool.affine_select(out=d, in_=d, pattern=[[1, P]], compare_op=ALU.is_ge,
                                                  fill=0.0, base=0, channel_multiplier=-1)
                    last.then_inc(m_pm, 1)
                for e in range(2):
                    pool.wait_ge(m_hh, 2 * i + e + 1)
                    pool.sem_inc(pool_turn, 1)
                    pool.tensor_tensor(at(xl, 2 * i + e), fac[e], at(xh_f, 2 * i + e),
                                       ALU.subtract).then_inc(m_hid, 1)

        iota_t = std[:, :]
        tmp_t = rstd[:, :]

        def tables_pool(pool):
            pool.wait_ge(e_bb, 8)
            pool.iota(iota_t, [[1, T]], base=0, channel_multiplier=0,
                      allow_small_or_imprecise_dtypes=True).then_inc(iota_ready, 1)

        def tables_vector(dve):
            ts, tt = dve.tensor_scalar, dve.tensor_tensor
            dve.wait_ge(iota_ready, 1)
            with dve.Fori(0, NSTATE_T) as i:
                si = at(sinT, i)
                ts(si, iota_t, small[:, bass.ds(i + PHI, 1)], None, ALU.mult).then_inc(tab_v, 1)
                dve.wait_ge(tab_v, 4 * i + 1)
                ts(tmp_t, si, ROUND, ROUND, ALU.add, ALU.subtract).then_inc(tab_v, 1)
                dve.wait_ge(tab_v, 4 * i + 2)
                tt(si, si, tmp_t, ALU.subtract).then_inc(tab_v, 1)
                dve.wait_ge(tab_v, 4 * i + 3)
                ts(tmp_t, si, 0.25, None, ALU.is_gt).then_inc(tab_v, 1)
                dve.wait_ge(tab_v, 4 * i + 4)
                dve.scalar_tensor_tensor(at(cosT, i), si, 0.25, tmp_t, ALU.add, ALU.subtract).then_inc(tab, 1)

        def tables_scalar(act, n):
            act.wait_ge(tab, n + 1)
            act.activation(at(sinT, n), at(sinT, n), ACT.Sin, scale=TWO_PI)
            act.activation(at(cosT, n), at(cosT, n), ACT.Sin, scale=TWO_PI).then_inc(tab_act, 1)

        b_raw = [hf_f[:, 0:512], hf_f[:, 512:1024]]
        c_raw = [hf_f[:, 1024:1536], hf_f[:, 1536:2048]]
        bb = [hf_f[:, 2048:2560], hf_f[:, 2560:3072]]
        c_neg = [hf_f[:, 3072:3584], hf_f[:, 3584:4096]]
        bb_t = [rstd[:, :], std[:, :]]
        xbuf = chunks(xs[:, :])
        br, bi = [xbuf[:, e, :] for e in range(2)], [xbuf[:, 2 + e, :] for e in range(2)]
        r1, r2, r3 = (xbuf[:, 4 + j, :] for j in range(3))
        pr = [xbuf[:, 7 + j, :] for j in range(4)]
        bt = [xbuf[:, 11 + q, :] for q in range(2)]
        ucs = xbuf[:, 13, :]
        bts = [xbuf[:, 14, P * q:P * (q + 1)] for q in range(2)]
        cs = [xbuf[:, 15, P * j:P * (j + 1)] for j in range(3)]
        ys = [(rstd[:, :], std[:, :]), (acc[:, :], b_raw[0])]
        r_pool = [cosT[:, g, :] for g in range(4)]
        win = cosT[:, 4:6, :]
        sig_e = [cosT[:, 6 + g, :] for g in range(2)]
        Y_ORDER = (4, 5, 6, 7, 0, 1, 2, 3)

        def even_tensor(pe):
            pe.wait_ge(e_bb, 8)
            for q in range(2):
                for c in range(4):
                    last = pe.transpose(banks[:, 4 + q, P * c:P * (c + 1)], bb[q][:, P * c:P * (c + 1)], ident)
            last.then_inc(e_t, 1)

            def drive(c, j):
                n = 4 * c + j
                rows = slice(32 * j, 32 * j + 32)
                if j == 0:
                    pe.wait_ge(s_staged, c + 1)
                pe.wait_ge(s_buc, n + 1)
                for q in range(2):
                    last = pe.matmul(banks[:, 4 + q, :], bts[q][rows, :], ucs[rows, :], start=True, stop=True)
                last.then_inc(s_bu, 1)

            def read_out(c, j):
                n = 4 * c + j
                rows = slice(32 * j, 32 * j + 32)
                if j == 0:
                    pe.wait_ge(s_ych, c + 1)
                    pe.wait_ge(s_cs, c + 1)
                for q, k in enumerate((0, 1, 2, 2)):
                    if q % 2 == 0:
                        pe.wait_ge(s_pr, 2 * n + q // 2 + 5)
                    last = pe.matmul(banks[rows, 6, :], cs[k][:, rows], pr[q], start=(q == 0), stop=(q == 3),
                                     skip_group_check=True)
                    if q % 2 == 1:
                        last.then_inc(s_ym, 1)

            def input_chunk(c, last=False):
                for j in range(3):
                    drive(c, j + 1)
                    read_out(c, j)
                if not last:
                    drive(c + 1, 0)
                read_out(c, 3)

            drive(0, 0)
            with pe.Fori(0, 3) as c:
                input_chunk(c)
            input_chunk(3, last=True)
            pe.wait_ge(xn_ready, SPLIT["glu"] + 4)
            pe.wait_ge(tiles_freed, FREE0 + TILE["even.glu"])
            for b in range(4):
                pe.wait_ge(w_split, BLK["even.glu"] + b + 1)
                if b >= 2:
                    pe.wait_ge(tiles_freed, FREE0 + TILE["even.glu"] + 2 * b - 2)
                for vg in range(2):
                    for k in range(4):
                        last = product3(pe, lin[2 * (b % 2) + vg], b % 2, 4 * vg + k, xh[:, k, :], xl[:, k, :],
                                        k == 0, k == 3)
                last.then_inc(blocks_done, 1)
            for g in range(4):
                pe.wait_ge(e_pool, g + 1)
                if g >= 2:
                    pe.wait_ge(t_ready, TNO["even.y"] + 4 + g - 1)
                pe.matmul(banks[:, 4 + g % 2, :], pw[:, P * g:P * (g + 1)], r_pool[g], start=True,
                          stop=True).then_inc(e_pm, 1)

        def even_scalar(act):
            for lo, dst, func in ((0, uin, ACT.Copy), (8, zin, ACT.Silu)):
                with act.Fori(0, 2) as i:
                    for m in range(4):
                        high_part(act, "even.in", m, 4 * i + lo)
                        act.activation(at(dst, 4 * i + m), lin[m], func).then_inc(tiles_freed, 1)
                        tables_scalar(act, 4 * i + (lo + m))
            act.wait_ge(e_t, 1)
            for q in range(2):
                act.activation(bt[q], banks[:, 4 + q, :], ACT.Copy).then_inc(e_btc, 1)

            def take(c, j):
                n = 4 * c + j
                act.wait_ge(s_bu, n + 1)
                act.wait_ge(s_rot, n + 1)
                act.activation(br[j % 2], banks[:, 4, :], ACT.Copy)
                act.activation(bi[j % 2], banks[:, 5, :], ACT.Copy).then_inc(s_buc, 1)

            act.wait_ge(e_btc, 2)
            act.wait_ge(e_bb, 8)
            with act.Fori(0, 4) as c:
                act.activation(ucs, at(uin, c), ACT.Copy)
                for q in range(2):
                    last = act.activation(bts[q], bt[q][:, bass.ds(P * c, P)], ACT.Copy)
                last.then_inc(s_staged, 1)
                take(c, 0)
                take(c, 1)
                act.wait_ge(s_ym, 8 * c + 2)
                for dst, src in zip(cs, (c_raw[0], c_neg[0], c_neg[1])):
                    last = act.activation(dst, src[:, bass.ds(P * c, P)], ACT.Copy)
                last.then_inc(s_cs, 1)
                take(c, 2)
                take(c, 3)
            split_high(act, "glu", 4, uin)
            for b in range(4):
                high_part(act, "even.glu", b)
                if b >= 2:
                    act.wait_ge(tiles_freed, FREE0 + TILE["even.glu"] + 2 * b - 2)
                act.activation(sig_e[b % 2], lin[2 * (b % 2) + 1], ACT.Sigmoid).then_inc(e_sig, 1)
            split_high(act, "even.y", order=Y_ORDER)
            with act.Fori(0, 2) as i:
                for s in range(4):
                    high_part(act, "even.out", s, 4 * i)

        def residual(dve, name):
            with dve.Fori(0, 2) as i:
                for m in range(4):
                    dve.wait_ge(blocks_done, BLK[name] + 4 * i + m + 1)
                    dve.tensor_tensor(at(x, 4 * i + m), at(x, 4 * i + m), lin[m], ALU.add).then_inc(tiles_freed, 1)

        def even_vector(dve):
            ts, tt, stt = dve.tensor_scalar, dve.tensor_tensor, dve.scalar_tensor_tensor
            dve.wait_ge(e_loaded, 64)

            def v3(ap):
                return ap.rearrange("p (a n) -> p a n", a=NSTATE_T)

            def gain(c):
                return col(c).unsqueeze(2).to_broadcast([P, NSTATE_T, 32])

            tt(v3(bb[0]), v3(b_raw[0]), gain(KRE), ALU.mult).then_inc(e_bb, 1)
            tt(v3(bb_t[0]), v3(b_raw[1]), gain(KIM), ALU.mult).then_inc(e_bb, 1)
            tt(v3(bb[1]), v3(b_raw[1]), gain(KRE), ALU.mult).then_inc(e_bb, 1)
            tt(v3(bb_t[1]), v3(b_raw[0]), gain(KIM), ALU.mult).then_inc(e_bb, 1)
            dve.wait_ge(e_bb, 4)
            tt(bb[0], bb[0], bb_t[0], ALU.subtract).then_inc(e_bb, 1)
            tt(bb[1], bb[1], bb_t[1], ALU.add).then_inc(e_bb, 1)
            for q in range(2):
                ts(c_neg[q], c_raw[q], -1.0, None, ALU.mult).then_inc(e_bb, 1)
            tables_vector(dve)
            dve.wait_ge(tab_act, NSTATE_T)

            def add_skip(c):
                dve.wait_ge(s_ym, 8 * c + 10)
                stt(at(uin, c), at(uin, c), vec[:, bass.ds(c + VEC["ssm_d"], 1)], banks[:, 6, :],
                    ALU.mult, ALU.add).then_inc(s_ych, 1)

            def scan_chunk(c, first=False):
                for j in range(4):
                    if j == 1 and not first:
                        add_skip(c - 1)
                    n = 4 * c + j
                    co, si = at(cosT, n), at(sinT, n)
                    dve.wait_ge(s_buc, n + 2)
                    tt(r1, co, br[j % 2], ALU.mult)
                    tt(r2, si, bi[j % 2], ALU.mult).then_inc(s_v, 1)
                    tt(r3, co, bi[j % 2], ALU.mult)
                    dve.wait_ge(s_v, 3 * n + 1)
                    tt(r1, r1, r2, ALU.add).then_inc(s_v, 1)
                    dve.wait_ge(s_v, 3 * n + 2)
                    tt(r2, si, br[j % 2], ALU.mult).then_inc(s_rot, 1)
                    yr, yi = ys[j % 2]
                    dve.wait_ge(s_pr, 2 * n + 2)
                    decay = small[:, bass.ds(n + R_, 1)].to_broadcast([P, T])
                    dve.tensor_tensor_scan(yr, decay, r1, 0.0, ALU.mult, ALU.add)
                    dve.wait_ge(s_rot, n + 3)
                    tt(r3, r3, r2, ALU.subtract).then_inc(s_v, 1)
                    dve.wait_ge(s_v, 3 * n + 3)
                    dve.tensor_tensor_scan(yi, decay, r3, 0.0, ALU.mult, ALU.add).then_inc(s_y, 1)
                    dve.wait_ge(s_y, n + 1)

            scan_chunk(0, first=True)
            with dve.Fori(1, 4) as c:
                scan_chunk(c)
            add_skip(3)
            dve.wait_ge(s_ych, 5)
            dve.memset(small[:, 0:1], 0.0).then_inc(t_ready, 4)
            dve.wait_ge(s_ych, 5)
            steps = 0
            for g, w in enumerate((2, 4, 8, 16)):
                u_g = uin[:, 4 + g, :]
                src, k = u_g, 1
                while k < w:
                    dst = win[:, steps % 2, :]
                    dve.tensor_copy(dst[:, 0:k], src[:, 0:k])
                    tt(dst[:, k:T], src[:, k:T], src[:, 0:T - k], ALU.add).then_inc(e_win, 1)
                    steps += 1
                    dve.wait_ge(e_win, steps)
                    src, k = dst, 2 * k
                o = C_INV + 16 * g
                stt(r_pool[g][:, 16:T], src[:, 16:T], 1.0 / w, u_g[:, 16:T], ALU.mult, ALU.subtract)
                tt(r_pool[g][:, 0:16], src[:, 0:16], cst_sb[:, o:o + 16], ALU.mult).then_inc(e_w2, 1)
                dve.wait_ge(e_w2, g + 1)
                tt(r_pool[g][:, 0:16], r_pool[g][:, 0:16], u_g[:, 0:16], ALU.subtract).then_inc(e_pool, 1)
            for b in range(4):
                dve.wait_ge(e_sig, b + 1)
                tt(hf[:, 4 + b, :], lin[2 * (b % 2)], sig_e[b % 2], ALU.mult).then_inc(tiles_freed, 2)
                dve.wait_ge(tiles_freed, FREE0 + TILE["even.glu"] + 2 * b + 2)
                tt(hf[:, 4 + b, :], hf[:, 4 + b, :], zin[:, 4 + b, :], ALU.mult).then_inc(t_ready, 1)
            for g in range(4):
                dve.wait_ge(e_pm, g + 1)
                c0 = VEC["pool_scale"] + g
                stt(hf[:, g, :], banks[:, 4 + g % 2, :], vec[:, c0:c0 + 1], zin[:, g, :],
                    ALU.mult, ALU.mult).then_inc(t_ready, 1)
            residual(dve, "even.out")

        def even_pool(pool):
            pool.wait_ge(xn_ready, SPLIT["even"] + 8)
            for dst, src in ((b_raw[0], bst[0]), (b_raw[1], bst[1]), (c_raw[0], cst[0]), (c_raw[1], cst[1])):
                pool.dma_start(dst, src).then_inc(e_loaded, 16)
            tables_pool(pool)
            low_parts(pool, "even.in")
            pool.wait_ge(e_btc, 2)
            tt = pool.tensor_tensor
            with pool.Fori(0, 4) as c:
                for j in range(4):
                    n = 4 * c + j
                    co, si = at(cosT, n), at(sinT, n)
                    yr, yi = ys[j % 2]
                    pool.wait_ge(s_y, n + 1)
                    pool.sem_inc(pool_turn, 1)
                    pool.wait_ge(s_ym, 2 * n + 1)
                    pool.sem_inc(pool_turn, 1)
                    tt(pr[0], co, yr, ALU.mult)
                    tt(pr[1], si, yi, ALU.mult).then_inc(s_pr, 1)
                    pool.wait_ge(s_ym, 2 * n + 2)
                    pool.sem_inc(pool_turn, 1)
                    tt(pr[2], si, yr, ALU.mult)
                    tt(pr[3], co, yi, ALU.mult).then_inc(s_pr, 1)
            split_low(pool, "glu", 4, uin)
            low_parts(pool, "even.glu")
            split_low(pool, "even.y", order=Y_ORDER)
            low_parts(pool, "even.out")

        sig_o = chunks(region(12800, KD * T))
        mean = region(16896, T)
        tap_acc = sig_o
        taps = [region(17408 + T * j, T) for j in range(POOL_TAPS)]

        def odd_tensor(pe):
            for c in range(KD):
                pe.wait_ge(o_conv, c + 1)
                last = pe.matmul(banks[:, 6, :], ones, cc[:, c, :], start=(c == 0), stop=(c == KD - 1))
            last.then_inc(o_sum, 1)
            sumsq_of(pe, squares, 64)

        def odd_scalar(act):
            act.wait_ge(o_v, 1)
            with act.Fori(0, 4) as i:
                for s in range(2):
                    high_part(act, "odd.in", 2 * s, 4 * i)
                    high_part(act, "odd.in", 2 * s + 1, 4 * i)
                    g = gpad[:, bass.ds(2 * i + s, 1), PAD:PAD + T].rearrange("p a n -> p (a n)")
                    act.activation(g, lin[2 * s], ACT.Copy)
                    act.activation(at(sig_o, 2 * i + s), lin[2 * s + 1], ACT.Sigmoid).then_inc(tiles_freed, 2)
                    act.wait_ge(g_mul, 2 * i + s + 1)
                    act.wait_ge(tap_sum, POOL_TAPS * (2 * i + s) + 1)
                    for j in range(POOL_TAPS):
                        tap = CONV_K - POOL_TAPS + j
                        g = gpad[:, bass.ds(2 * i + s, 1), tap:tap + T].rearrange("p a n -> p (a n)")
                        w = vec[:, bass.ds(2 * CONV_K * i + (VEC["conv_w"] + CONV_K * s + tap), 1)]
                        act.activation(taps[j], g, ACT.Copy, scale=w).then_inc(tap_prod, 1)
            with act.Fori(0, 2) as i:
                for m in range(4):
                    high_part(act, "odd.in", m, 4 * i + 16)
                    act.activation(at(zz, 4 * i + m), lin[m], ACT.Silu).then_inc(tiles_freed, 1)
            act.wait_ge(sumsq_ready, norm_no["odd.ln"])
            for c in range(KD):
                act.wait_ge(o_cen, c + 2)
                act.activation(sq[:, c, :], cc[:, c, :], ACT.Square).then_inc(squares, 1)
            take_std(act, "odd.ln")
            for c in range(KD):
                act.wait_ge(o_n, c + 1)
                b = VEC["ln_b"] + c
                act.activation(cc[:, c, :], cc[:, c, :], ACT.Silu, bias=vec[:, b:b + 1]).then_inc(o_s, 1)
            split_high(act, "odd.y")
            for s in range(NBLK["odd.out"]):
                high_part(act, "odd.out", s % 4, s - s % 4)

        def odd_vector(dve):
            ts, tt, stt = dve.tensor_scalar, dve.tensor_tensor, dve.scalar_tensor_tensor
            dve.memset(gpad[:, :, 0:PAD], 0.0).then_inc(o_v, 1)
            dve.wait_ge(o_v, 1)
            cw = VEC["conv_w"]
            with dve.Fori(0, 4) as i:
                own = CONV_K - POOL_TAPS
                gs = [gpad[:, bass.ds(2 * i + s, 1), :].rearrange("p a n -> p (a n)") for s in range(2)]
                cs_ = [at(cc, 2 * i + s) for s in range(2)]
                for tap in range(own):
                    for s in range(2):
                        w = vec[:, bass.ds(2 * CONV_K * i + (cw + CONV_K * s + tap), 1)]
                        if tap == 0:
                            dve.wait_ge(g_mul, 2 * i + s + 1)
                            ts(cs_[s], gs[s][:, 0:T], w, vec[:, bass.ds(2 * i + (VEC["conv_b"] + s), 1)],
                               ALU.mult, ALU.add).then_inc(o_v, 1)
                        else:
                            dve.wait_ge(o_v, 2 * own * i + 2 * (tap - 1) + s + 2)
                            stt(cs_[s], gs[s][:, tap:tap + T], w, cs_[s], ALU.mult, ALU.add).then_inc(o_v, 1)
                for s in range(2):
                    dve.wait_ge(o_v, 2 * own * i + 2 * (own - 1) + s + 2)
                    dve.wait_ge(tap_sum, POOL_TAPS * (2 * i + s + 1) + 1)
                    tt(cs_[s], cs_[s], at(tap_acc, 2 * i + s), ALU.add).then_inc(o_conv, 1)
            dve.wait_ge(o_sum, 1)
            ts(mean, banks[:, 6, :], 1.0 / D, None, ALU.mult).then_inc(o_cen, 1)
            dve.wait_ge(o_cen, 1)
            for c in range(KD):
                tt(cc[:, c, :], cc[:, c, :], mean, ALU.subtract).then_inc(o_cen, 1)
            norm_stats(dve, "odd.ln")
            for c in range(KD):
                b = VEC["ln_g"] + c
                stt(cc[:, c, :], cc[:, c, :], vec[:, b:b + 1], rstd[:, :], ALU.mult, ALU.mult).then_inc(o_n, 1)
            for c in range(KD):
                dve.wait_ge(o_s, c + 1)
                tt(hf[:, c, :], cc[:, c, :], zz[:, c, :], ALU.mult).then_inc(t_ready, 1)
            residual(dve, "odd.out")

        def take_std(act, name):
            n = norm_no[name]
            which = 1 if name == "odd.ln" else 0
            act.wait_ge(sumsq_ready, n + 1)
            act.activation(std[:, :], ps_n, ACT.Sqrt, bias=eps[:, which:which + 1],
                           scale=1.0 / D).then_inc(std_ready, 1)

        def norm_stats(dve, name):
            n = norm_no[name]
            dve.wait_ge(std_ready, n + 1)
            dve.reciprocal(rstd[:, :], std[:, :]).then_inc(rstd_ready, 1)
            dve.wait_ge(rstd_ready, n + 1)

        def acc_start(dve, name):
            dve.memset(acc[:, :], 0.0).then_inc(acc_ready, 1)

        def acc_add(dve, name, chunk, k):
            dve.wait_ge(acc_ready, ACC_STEPS * ACC[name] + 1 + k)
            dve.tensor_tensor(acc[:, :], acc[:, :], chunk, ALU.add).then_inc(acc_ready, 1)

        def sum_acc(pe, name):
            pe.wait_ge(acc_ready, ACC_STEPS * (ACC[name] + 1))
            if norm_no[name] > 0:
                pe.wait_ge(std_ready, norm_no[name])
            else:
                pe.wait_ge(prep_act, HEADS)
            pe.matmul(ps_n, ones, acc[:, :], start=True, stop=True).then_inc(sumsq_ready, 1)

        def sumsq_of(pe, signal, base, buf=sq):
            for c in range(KD):
                pe.wait_ge(signal, base + c + 1)
                last = pe.matmul(ps_n, ones, buf[:, c, :], start=(c == 0), stop=(c == KD - 1))
            last.then_inc(sumsq_ready, 1)

        def product3(pe, dst, q, t, in_hi, in_lo, first, last):
            cols = slice(t * P, (t + 1) * P)
            pe.matmul(dst, wh[:, q, cols], in_hi, start=first, stop=False)
            pe.matmul(dst, wl[:, q, cols], in_hi, start=False, stop=False)
            return pe.matmul(dst, wh[:, q, cols], in_lo, start=False, stop=last)

        def block_mm(pe, dst, q, hi, lo, n=KD, k0=0, total=KD):
            for k in range(n):
                last = product3(pe, dst, q, k, hi[:, k0 + k, :], lo[:, k0 + k, :], k0 + k == 0,
                                k0 + k == total - 1)
            last.then_inc(blocks_done, 1)

        block = ctx.enter_context(nc.Block())

        @block.sync
        def _(sp):
            for dst, src in ((cst_sb[:, :], consts), (vec[:, :], vecs), (x, x_in)):
                sp.dma_start(dst, src).then_inc(in_loaded, 16)
            def load(i, s):
                sp.dma_start(raw[:, s, :], weights[bass.ds(4 * i + s, 1)].rearrange("b p n -> (b p) n")
                             ).then_inc(w_loaded[s], 16)

            for s in range(RING):
                load(0, s)
            with sp.Fori(1, BLOCKS // RING) as i:
                for s in range(RING):
                    sp.wait_ge(w_split, 4 * i + s - 3)
                    load(i, s)
            sp.wait_ge(t_ready, TNO["final"] + 8)
            sp.dma_start(out, hf).then_inc(out_done, 16)
            sp.wait_ge(out_done, 16)

        @block.tensor
        def _(pe):
            def first_pair(name, key, order=range(KD)):
                pe.wait_ge(tiles_freed, FREE0 + TILE[name])
                pe.wait_ge(w_split, BLK[name] + 2)
                for j, k in enumerate(order):
                    pe.wait_ge(xn_ready, SPLIT[key] + j + 1)
                    for s in range(2):
                        last = product3(pe, lin[s], s, k, xh[:, k, :], xl[:, k, :], j == 0, j == KD - 1)
                        if j == KD - 1:
                            last.then_inc(blocks_done, 1)

            def linear(name, key=None, order=range(KD)):
                if key:
                    first_pair(name, key, order)
                    for s in (2, 3):
                        pe.wait_ge(w_split, BLK[name] + s + 1)
                        block_mm(pe, lin[s], s % 2, xh, xl)
                with pe.Fori(1 if key else 0, NBLK[name] // 4) as i:
                    for s in range(4):
                        pe.wait_ge(w_split, BLK[name] + s + 1 + 4 * i)
                        pe.wait_ge(tiles_freed, FREE0 + TILE[name] + 4 * i + s - 3)
                        block_mm(pe, lin[s], s % 2, xh, xl)

            def token_major(name):
                for half in range(2):
                    pe.wait_ge(tiles_freed, FREE0 + TILE[name] + 4 * half)
                    for b in range(4):
                        pe.wait_ge(w_split, BLK[name] + 4 * half + b + 1)
                        for kk in range(2):
                            k = 2 * b + kk
                            cols = slice(kk * T, (kk + 1) * T)
                            for t in range(4):
                                tok = slice(t * P, (t + 1) * P)
                                pe.matmul(lin[t], xh[:, k, tok], wh[:, b % 2, cols], start=(k == 0), stop=False)
                                pe.matmul(lin[t], xh[:, k, tok], wl[:, b % 2, cols], start=False, stop=False)
                                last = pe.matmul(lin[t], xl[:, k, tok], wh[:, b % 2, cols], start=False,
                                                 stop=(k == 7))
                        last.then_inc(blocks_done, 1)

            def ffn(name, idx):
                gu, dn_ = name + ".gu", name + ".dn"
                first_pair(gu, name)
                for s in (2, 3):
                    pe.wait_ge(w_split, BLK[gu] + s + 1)
                    block_mm(pe, lin[s], s % 2, xh, xl)
                    if s == 2:
                        sum_acc(pe, name + ".pre")
                with pe.Fori(1, KF // 2) as i:
                    for s in range(4):
                        pe.wait_ge(w_split, BLK[gu] + s + 1 + 4 * i)
                        if s % 2 == 0:
                            pe.wait_ge(tiles_freed, FREE0 + TILE[gu] + 4 * i + s - 2)
                        block_mm(pe, lin[s], s % 2, xh, xl)
                pe.wait_ge(h_lo, 2 + KF * idx + 16)
                with pe.Fori(0, 2) as i:
                    for m in range(4):
                        pe.wait_ge(tiles_freed, FREE0 + TILE[dn_] + 4 * i + m - 3)
                        k0 = 0
                        for j, n in enumerate(DN):
                            pe.wait_ge(w_split, BLK[dn_] + 3 * m + j + 1 + 12 * i)
                            if j == 2 and m == 0:
                                pe.wait_ge(h_lo, 2 + KF * (idx + 1))
                            block_mm(pe, lin[m], (3 * m + j) % 2, hh, hl, n=n, k0=k0, total=KF)
                            k0 += n
                sum_acc(pe, name + ".post")

            pe.wait_ge(in_loaded, 48)
            prep_tensor(pe)
            ffn("ffn0", 0)
            sum_acc(pe, "attn.pre")
            linear("attn.qk", "attn")
            token_major("attn.v")
            attention_tensor(pe)
            pe.wait_ge(tiles_freed, FREE0 + TILE["attn.out"])
            linear("attn.out")
            sum_acc(pe, "attn.post")
            ffn("ffn1", 1)
            ffn("ffn2", 2)
            sum_acc(pe, "mlstm.pre")
            gates_tensor(pe)
            linear("mlstm.qk", "mlstm")
            token_major("mlstm.v")
            pe.wait_ge(tiles_freed, FREE0 + TILE["mlstm.o"])
            linear("mlstm.o")
            mlstm_tensor(pe)
            linear("mlstm.out")
            sum_acc(pe, "mlstm.post")
            ffn("ffn3", 3)
            sum_acc(pe, "even.pre")
            linear("even.in", "even")
            even_tensor(pe)
            linear("even.out", "even.y", Y_ORDER)
            sum_acc(pe, "odd.pre")
            linear("odd.in", "odd")
            odd_tensor(pe)
            linear("odd.out", "odd.y")
            sum_acc(pe, "final")

        @block.scalar
        def _(act):
            def square_x(u, ffn_name=None):
                for c in range(KD):
                    if u == 0:
                        act.wait_ge(in_loaded, 48)
                    elif u <= 6:
                        act.wait_ge(x_ready, 8 * (u - 1) + c + 1)
                    else:
                        act.wait_ge(tiles_freed, FREE0 + TILE[("even.out", "odd.out")[u - 7]] + c + 1)
                    if ffn_name:
                        act.activation(xh[:, c, :], x[:, c, :], ACT.Copy,
                                       scale=g_of(ffn_name + ".pre", c)).then_inc(hi_ready, 1)
                    act.activation(hf[:, c, :], x[:, c, :], ACT.Square).then_inc(squares, 1)

            def branch_out(name):
                per = NBLK[name] // KD
                dst = sq if per > 1 else mix_sq
                with act.Fori(0, 2) as i:
                    for m in range(4):
                        for j in range(per):
                            high_part(act, name, per * m + j, 4 * per * i)
                        act.activation(at(dst, 4 * i + m), lin[m], ACT.Square).then_inc(branch_sq, 1)
                        act.activation(at(hf, 4 * i + m), lin[m], ACT.Copy).then_inc(tiles_freed, 1)

            def ffn(name, idx):
                gu = name + ".gu"

                def silu(i, s):
                    act.wait_ge(gate_scaled, KF * idx + 2 * i + s + 1)
                    act.activation(sg[:, s, :], sg[:, s, :], ACT.Silu).then_inc(gate_act, 1)

                def hidden_high(i, s):
                    act.wait_ge(tiles_freed, FREE0 + TILE[gu] + 4 * i + 2 * s + 2)
                    act.activation(at(hh, 2 * i + s), ht[:, s, :], ACT.Copy).then_inc(h_hi, 1)

                for s in range(2):
                    high_part(act, gu, s)
                take_std(act, name + ".pre")
                high_part(act, gu, 2)
                silu(0, 0)
                hidden_high(0, 0)
                silu(0, 1)
                high_part(act, gu, 3)
                hidden_high(0, 1)
                with act.Fori(1, KF // 2) as i:
                    for s in range(2):
                        high_part(act, gu, 2 * s, 4 * i)
                        silu(i, s)
                        high_part(act, gu, 2 * s + 1, 4 * i)
                        hidden_high(i, s)
                branch_out(name + ".dn")
                take_std(act, name + ".post")

            prep_scalar(act, lambda: square_x(0, "ffn0"))
            ffn("ffn0", 0)
            square_x(1)
            take_std(act, "attn.pre")
            split_high(act, "attn")
            attention_in_scalar(act)
            attention_scalar(act)
            branch_out("attn.out")
            take_std(act, "attn.post")
            square_x(2, "ffn1")
            ffn("ffn1", 1)
            square_x(3, "ffn2")
            ffn("ffn2", 2)
            square_x(4)
            take_std(act, "mlstm.pre")
            split_high(act, "mlstm")
            mlstm_scalar(act)
            branch_out("mlstm.out")
            take_std(act, "mlstm.post")
            square_x(5, "ffn3")
            ffn("ffn3", 3)
            square_x(6)
            take_std(act, "even.pre")
            split_high(act, "even")
            even_scalar(act)
            square_x(7)
            take_std(act, "odd.pre")
            split_high(act, "odd")
            odd_scalar(act)
            square_x(8)
            take_std(act, "final")

        @block.vector
        def _(dve):
            def add_square(name, c):
                if c == 0:
                    acc_start(dve, name)
                dve.wait_ge(squares, 8 * pre_no[name] + (8 if name == "final" else 0) + c + 1)
                acc_add(dve, name, hf[:, c, :], c)

            def sum_squares(name):
                for c in range(KD):
                    add_square(name, c)
                norm_stats(dve, name)

            def branch_squares(name):
                buf = sq if name.startswith("ffn") else mix_sq
                acc_start(dve, name + ".post")
                base = 8 * POSTS.index(name)
                with dve.Fori(0, 2) as i:
                    for m in range(4):
                        dve.wait_ge(branch_sq, base + 4 * i + m + 1)
                        acc_add(dve, name + ".post", at(buf, 4 * i + m), 4 * i + m)

            def pre(name, summed=False):
                if summed:
                    norm_stats(dve, name)
                else:
                    sum_squares(name)
                for c in range(KD):
                    dve.scalar_tensor_tensor(hf[:, c, :], x[:, c, :], g_of(name, c), rstd[:, :],
                                             ALU.mult, ALU.mult).then_inc(t_ready, 1)

            LAG = 3

            def low_x(dve, name, c):
                dve.wait_ge(hi_ready, SPLIT[name] + c + 1)
                dve.scalar_tensor_tensor(xl[:, c, :], x[:, c, :], g_of(name + ".pre", c), xh_f[:, c, :],
                                         ALU.mult, ALU.subtract).then_inc(xn_ready, 1)

            def post(name, next_ffn=None, next_mixer=None):
                branch_squares(name)
                norm_stats(dve, name + ".post")
                n = 8 * POSTS.index(name)
                for c in range(KD + LAG):
                    if c < KD:
                        dve.scalar_tensor_tensor(hf[:, c, :], hf[:, c, :], g_of(name + ".post", c), rstd[:, :],
                                                 ALU.mult, ALU.mult).then_inc(scaled, 1)
                    if next_ffn and c >= LAG:
                        low_x(dve, next_ffn, c - LAG)
                    if next_mixer and c >= LAG:
                        add_square(next_mixer + ".pre", c - LAG)

            def ffn(name, idx, next_ffn=None, next_mixer=None):
                sum_squares(name + ".pre")
                gu, dn = name + ".gu", name + ".dn"
                with dve.Fori(0, KF // 2) as i:
                    for s in range(2):
                        n = 2 * i + (KF * idx + s)
                        dve.wait_ge(blocks_done, BLK[gu] + 4 * i + 2 * s + 1)
                        dve.wait_ge(tiles_freed, FREE0 + TILE[gu] + 4 * i + 2 * s - 2)
                        dve.tensor_tensor(sg[:, s, :], lin[2 * s], rstd[:, :], ALU.mult).then_inc(gate_scaled, 1)
                        dve.wait_ge(blocks_done, BLK[gu] + 4 * i + 2 * s + 2)
                        dve.wait_ge(h_lo, n + 1)
                        dve.tensor_tensor(ht[:, s, :], lin[2 * s + 1], rstd[:, :], ALU.mult).then_inc(up_scaled, 1)
                        dve.wait_ge(gate_act, n + 1)
                        dve.wait_ge(up_scaled, n + 1)
                        dve.tensor_tensor(ht[:, s, :], ht[:, s, :], sg[:, s, :], ALU.mult).then_inc(tiles_freed, 2)
                post(name, next_ffn, next_mixer)

            def split_x():
                for c in range(KD):
                    low_x(dve, "ffn0", c)

            prep_vector(dve, split_x)
            ffn("ffn0", 0, next_mixer="attn")
            pre("attn.pre", True)
            attention_vector(dve)
            post("attn", "ffn1")
            ffn("ffn1", 1, "ffn2")
            ffn("ffn2", 2, next_mixer="mlstm")
            pre("mlstm.pre", True)
            mlstm_vector(dve)
            post("mlstm", "ffn3")
            ffn("ffn3", 3, next_mixer="even")
            pre("even.pre", True)
            even_vector(dve)
            pre("odd.pre")
            odd_vector(dve)
            pre("final")

        @block.gpsimd
        def _(pool):
            def update(name):
                n = 8 * POSTS.index(name)
                for c in range(KD):
                    pool.wait_ge(scaled, n + c + 1)
                    pool.tensor_tensor(x[:, c, :], x[:, c, :], hf[:, c, :], ALU.add).then_inc(x_ready, 1)

            def ffn(name, idx):
                gu = name + ".gu"

                def hidden_low(i, s):
                    pool.wait_ge(h_hi, KF * idx + 2 * i + s + 1)
                    pool.sem_inc(pool_turn, 1)
                    pool.tensor_tensor(at(hl, 2 * i + s), ht[:, s, :], at(hh_f, 2 * i + s),
                                       ALU.subtract).then_inc(h_lo, 1)

                for s in range(3):
                    low_part(pool, gu, s)
                hidden_low(0, 0)
                low_part(pool, gu, 3)
                hidden_low(0, 1)
                with pool.Fori(1, KF // 2) as i:
                    for s in range(2):
                        low_part(pool, gu, 2 * s, 4 * i)
                        low_part(pool, gu, 2 * s + 1, 4 * i)
                        hidden_low(i, s)
                low_parts(pool, name + ".dn")
                update(name)

            first_parts(pool, True)
            ffn("ffn0", 0)
            pool.wait_ge(blocks_done, BLK["attn.qk"])
            pool.dma_start(strip, skewed(scratch)).then_inc(strip_in, 16)
            split_low(pool, "attn")
            attention_pool(pool)
            low_parts(pool, "attn.out")
            update("attn")
            ffn("ffn1", 1)
            ffn("ffn2", 2)
            split_low(pool, "mlstm")
            mlstm_pool(pool)
            low_parts(pool, "mlstm.out")
            update("mlstm")
            ffn("ffn3", 3)
            split_low(pool, "even")
            even_pool(pool)
            split_low(pool, "odd")
            def gated(i, s):
                pool.wait_ge(tiles_freed, FREE0 + TILE["odd.in"] + 4 * i + 2 * s + 2)
                pool.sem_inc(pool_turn, 1)
                g = gpad[:, bass.ds(2 * i + s, 1), PAD:PAD + T].rearrange("p a n -> p (a n)")
                pool.tensor_tensor(g, g, at(sig_o, 2 * i + s), ALU.mult).then_inc(g_mul, 1)

            with pool.Fori(0, 4) as i:
                for s in range(2):
                    low_part(pool, "odd.in", 2 * s, 4 * i)
                    low_part(pool, "odd.in", 2 * s + 1, 4 * i)
                    gated(i, s)
                    a = at(tap_acc, 2 * i + s)
                    for j in range(1, POOL_TAPS):
                        pool.wait_ge(tap_prod, POOL_TAPS * (2 * i + s) + j + 1)
                        if j > 1:
                            pool.wait_ge(tap_sum, POOL_TAPS * (2 * i + s) + j)
                        pool.sem_inc(pool_turn, 1)
                        pool.tensor_tensor(a, taps[0] if j == 1 else a, taps[j],
                                           ALU.add).then_inc(tap_sum, 2 if j == POOL_TAPS - 1 else 1)
            with pool.Fori(4, 6) as i:
                for s in range(4):
                    low_part(pool, "odd.in", s, 4 * i)
            split_low(pool, "odd.y")
            for s in range(NBLK["odd.out"]):
                low_part(pool, "odd.out", s % 4, s - s % 4)


def bucket(d):
    if d < 16:
        return d
    return min(16 + int(np.log(d / 16) / np.log(2048 / 16) * 16), NB_BUCKETS - 1)


def bias_columns():
    table = np.zeros((NB_BUCKETS + 1, STRIP_W), np.float32)
    for c in range(STRIP_W):
        d = T - 1 - c
        count = 0 if d < 0 else (d <= 128) + (d % 4 == 0) + (d % 16 == 0)
        if d >= 0:
            table[bucket(d), c] = 1.0
        table[NB_BUCKETS, c] = np.log(count) if count else NEG
    return table


def constants():
    c = np.zeros((P, NCONST), np.float32)
    c[:, C_ID:C_ID + P] = np.eye(P)
    c[:, C_TRI:C_TRI + P] = -np.tril(np.ones((P, P)))
    c[:, C_ONE:C_ONE + P] = 1.0
    for g, w in enumerate((2, 4, 8, 16)):
        c[:, C_INV + 16 * g:C_INV + 16 * (g + 1)] = 1.0 / np.minimum(np.arange(1, 17), w)
    return c


def kernel(**inputs):
    import concourse.bacc as _bacc
    from concourse.bass_utils import run_bass_kernel_spmd as _run

    a = {k: np.asarray(v) for k, v in inputs.items()}

    def blocks(w):
        k, n = w.shape
        return w.reshape(k // P, P, n // P, P).transpose(2, 1, 0, 3).reshape(n // P, P, k)

    def row_blocks(w):
        return w.reshape(4, 2, P, T).transpose(0, 2, 1, 3).reshape(4, P, 2 * T)

    def pairs(u, v):
        return np.stack([u, v], 1).reshape(-1, *u.shape[1:])

    def ffn(layer, j):
        w8.append(pairs(blocks(a["ffn_w_gate"][layer, j]), blocks(a["ffn_w_up"][layer, j])))
        down = np.zeros((KD, P, len(DN) * SLOT), np.float32)
        down[:, :, 0:FF] = blocks(a["ffn_w_down"][layer, j])
        w8.append(down.reshape(KD, P, len(DN), SLOT).transpose(0, 2, 1, 3).reshape(-1, P, SLOT))

    w8 = []
    ffn(0, 0)
    w = a["attn_w_in"][0]
    for lo in (0, 512, 1536, 2048):
        w8.append(blocks(w[:, lo:lo + 512]))
    w8.append(row_blocks(w[:, 1024:1536]))
    w8.append(row_blocks(w[:, 2560:3072]))
    w8.append(blocks(a["attn_w_out"][0]))
    ffn(0, 1)
    ffn(1, 0)
    w = a["mlstm_w_in"][0]
    w8.append(blocks(w[:, 0:2048]))
    w8.append(row_blocks(w[:, 2048:2560]))
    w8.append(row_blocks(w[:, 2560:3072]))
    w8.append(blocks(w[:, 3072:4096]))
    w_gates = w[:, 4096:].reshape(KD, P, 16).transpose(1, 0, 2).reshape(P, 128)
    w8.append(blocks(a["mlstm_w_out"][0]))
    ffn(1, 1)
    w = a["even_w_in_2"][0]
    w8.append(blocks(w[:, 512:1024]))
    w8.append(blocks(w[:, 0:512]))
    w8.append(blocks(w[:, 1024:2048]))
    w = blocks(a["ssm_w_glu_2"][0])
    w8.append(np.concatenate([w[0:4], w[4:8]], 2))
    w8.append(blocks(a["even_w_out_2"][0]))
    w = blocks(a["odd_w_in_2"][0])
    w8.append(pairs(w[0:8], w[8:16]))
    w8.append(w[16:24])
    w8.append(blocks(a["odd_w_out_2"][0]))
    w8 = np.concatenate(w8)

    def per_channel(v):
        return v.reshape(-1, P).T

    def per_state(v):
        return np.broadcast_to(v.reshape(32, -1), (32, 64)).reshape(NSTATE_T, P).T

    vecs = np.zeros((P, NVEC), np.float32)
    for name, v in (("norm_g", per_channel(a["norm_g"])), ("even_norm", per_channel(a["even_norm_2"])),
                    ("odd_norm", per_channel(a["odd_norm_2"])), ("final_norm", per_channel(a["final_norm_2"])),
                    ("pool_scale", per_channel(a["pool_scale_2"])), ("ssm_d", per_channel(a["ssm_d_2"])),
                    ("conv_b", per_channel(a["conv_b_2"])), ("ln_g", per_channel(a["conv_ln_g_2"])),
                    ("ln_b", per_channel(a["conv_ln_b_2"])), ("head_g", per_channel(a["mlstm_head_g"])),
                    ("conv_w", a["conv_w_2"][0].reshape(CONV_K, KD, P).transpose(2, 1, 0).reshape(P, -1)),
                    ("mconv_w", a["mlstm_conv_w"][0].reshape(MCONV_K, 16, P).transpose(2, 1, 0).reshape(P, -1)),
                    ("log_dt", per_state(a["ssm_log_dt_2"][0][:, None])), ("a_re", per_state(a["ssm_a_re_2"][0])),
                    ("a_im", per_state(a["ssm_a_im_2"][0]))):
        vecs[:, VEC[name]:VEC[name] + v.shape[1]] = v
    vecs[0:HEADS, VEC["b_i"]] = a["mlstm_b_gates"][0, 0:HEADS]
    vecs[0:HEADS, VEC["b_f"]] = a["mlstm_b_gates"][0, HEADS:]

    def diagonal(v):
        out = np.zeros((NSTATE_T, 2, 64, 2, 16), np.float32)
        v = v.reshape(NSTATE_T, 2, 64, 16)
        out[:, 0, :, 0] = v[:, 0]
        out[:, 1, :, 1] = v[:, 1]
        return out.reshape(NSTATE_T, P, 32).transpose(1, 0, 2).reshape(P, 512)

    bst = np.stack([diagonal(a["ssm_b_re_2"][0]), diagonal(a["ssm_b_im_2"][0])])
    cst = np.stack([diagonal(a["ssm_c_re_2"][0].transpose(0, 2, 1)),
                    diagonal(a["ssm_c_im_2"][0].transpose(0, 2, 1))])
    arrays = {
        "x_in": a["x"].reshape(T, KD, P).transpose(2, 1, 0), "weights": w8, "vecs": vecs,
        "consts": constants(), "rel_bias": a["rel_bias"], "buckets": bias_columns(), "w_gates": w_gates,
        "pool_w": a["pool_w_2"][0].transpose(1, 0, 2).reshape(P, 512), "bst": bst, "cst": cst,
    }
    arrays = {k: np.ascontiguousarray(v) for k, v in arrays.items()}
    nc = _bacc.Bacc("TRN2", target_bir_lowering=False, num_devices=1)
    args = [nc.dram_tensor(k, v.shape, F32, kind="ExternalInput").ap() for k, v in arrays.items()]
    scratch = nc.dram_tensor("scratch", (P, HEADS * STRIP_W), F32, kind="Internal").ap()
    out = nc.dram_tensor("out", (P, KD, T), F32, kind="ExternalOutput").ap()
    build(nc, *args, scratch, out)
    r = _run(nc, [arrays], core_ids=[0])
    return r.results[0]["out"].transpose(2, 1, 0).reshape(1, T, D)
```
